# Optimizing a Trainium2 kernel written in Bass

```python
import math
import jax, jax.numpy as jnp
from jax import lax
import numpy as np

D_MODEL = 1024
BATCH = 1
SEQ = 256
DEPTH = 1

CTX_LEN = 256
GRID_W = 64
D_MIX = D_MODEL
ATTN_WIDTH = D_MIX // 2
SSM_WIDTH = D_MIX - ATTN_WIDTH
HEAD_DIM = 64
N_Q_HEADS = ATTN_WIDTH // HEAD_DIM
N_KV_HEADS = N_Q_HEADS // 4
KV_WIDTH = N_KV_HEADS * HEAD_DIM
Q_BLOCK = 128
ATTN_SCALE = HEAD_DIM ** -0.5
ROPE_THETA = 10000.0
ROPE_HALF = HEAD_DIM // 2
ROPE_FREQS = ROPE_HALF // 2
SSM_GROUP = 16
N_SSM_GROUPS = SSM_WIDTH // SSM_GROUP
SSM_STATE = 64
N_DIRS = 2
NORM_EPS = 1e-6
Q_END = ATTN_WIDTH
K_END = Q_END + KV_WIDTH
V_END = K_END + KV_WIDTH
GA_END = V_END + ATTN_WIDTH
U_END = GA_END + SSM_WIDTH
IN_WIDTH = U_END + SSM_WIDTH

kernel_name = 'hymba_gqa_s5_diffusion_layer'

def rmsnorm(x, gain):
    x32 = x.astype(jnp.float32)
    y = x32 * lax.rsqrt(jnp.mean(x32 * x32, axis=-1, keepdims=True) + NORM_EPS)
    return (y * gain.astype(jnp.float32)).astype(x.dtype)

def adaln(cvec, w_ada, b_ada):
    m = jax.nn.silu(cvec) @ w_ada + b_ada
    return jnp.split(m, 3, axis=-1)

def modulate(h, shift, scale):
    return h * (1.0 + scale) + shift

def axial_rope_tables(row_pos, col_pos):
    inv_freq = ROPE_THETA ** (-jnp.arange(ROPE_FREQS, dtype=jnp.float32) / ROPE_FREQS)
    ang_r = row_pos[:, None] * inv_freq
    ang_c = col_pos[:, None] * inv_freq
    return (jnp.cos(ang_r)[:, None, :], jnp.sin(ang_r)[:, None, :],
            jnp.cos(ang_c)[:, None, :], jnp.sin(ang_c)[:, None, :])

def apply_axial_rope(x, rope):
    cos_r, sin_r, cos_c, sin_c = rope
    x32 = x.astype(jnp.float32)

    def rot(xh, cos, sin):
        x1, x2 = xh[..., :ROPE_FREQS], xh[..., ROPE_FREQS:]
        return jnp.concatenate([x1 * cos - x2 * sin, x1 * sin + x2 * cos], axis=-1)

    out = jnp.concatenate([rot(x32[..., :ROPE_HALF], cos_r, sin_r),
                           rot(x32[..., ROPE_HALF:], cos_c, sin_c)], axis=-1)
    return out.astype(x.dtype)

def mixer_inputs(h, w_in, q_gain, k_gain):
    b, l, _ = h.shape
    z = h @ w_in
    q = rmsnorm(z[..., :Q_END].reshape(b, l, N_Q_HEADS, HEAD_DIM), q_gain)
    k = rmsnorm(z[..., Q_END:K_END].reshape(b, l, N_KV_HEADS, HEAD_DIM), k_gain)
    v = z[..., K_END:V_END].reshape(b, l, N_KV_HEADS, HEAD_DIM)
    gate_a = z[..., V_END:GA_END]
    u = z[..., GA_END:U_END]
    gate_s = z[..., U_END:]
    return q, k, v, gate_a, u, gate_s

def _attend(qg, k, v):
    s = jnp.einsum('bqhgd,bkhd->bhgqk', qg, k).astype(jnp.float32) * ATTN_SCALE
    p = jax.nn.softmax(s, axis=-1).astype(v.dtype)
    return jnp.einsum('bhgqk,bkhd->bqhgd', p, v)

def latent_attention(q, k_lat, v_lat, k_ctx, v_ctx):
    b, l, hq, dh = q.shape
    n_blk = l // Q_BLOCK
    k_all = jnp.concatenate([k_ctx, k_lat], axis=1)
    v_all = jnp.concatenate([v_ctx, v_lat], axis=1)
    qb = q.reshape(b, n_blk, Q_BLOCK, N_KV_HEADS, hq // N_KV_HEADS, dh)
    qb = jnp.moveaxis(qb, 1, 0)
    out = lax.map(lambda q_blk: _attend(q_blk, k_all, v_all), qb)
    return jnp.moveaxis(out, 0, 1).reshape(b, l, hq * dh)

def context_attention(q, k, v):
    b, l, hq, dh = q.shape
    qg = q.reshape(b, l, N_KV_HEADS, hq // N_KV_HEADS, dh)
    return _attend(qg, k, v).reshape(b, l, hq * dh)

def s5_discretise(lam_re, lam_im, log_dt, b_re, b_im):
    lam_re = lam_re.astype(jnp.float32)
    lam_im = lam_im.astype(jnp.float32)
    dt = jnp.exp(log_dt.astype(jnp.float32))[:, None]
    mag = jnp.exp(dt * lam_re)
    ab_re, ab_im = mag * jnp.cos(dt * lam_im), mag * jnp.sin(dt * lam_im)
    nr, ni = ab_re - 1.0, ab_im
    den = lam_re * lam_re + lam_im * lam_im
    cr = (nr * lam_re + ni * lam_im) / den
    ci = (ni * lam_re - nr * lam_im) / den
    b_re = b_re.astype(jnp.float32)
    b_im = b_im.astype(jnp.float32)
    bb_re = cr[..., None] * b_re - ci[..., None] * b_im
    bb_im = cr[..., None] * b_im + ci[..., None] * b_re
    return ab_re, ab_im, bb_re, bb_im

def _complex_affine_combine(e1, e2):
    a1r, a1i, b1r, b1i = e1
    a2r, a2i, b2r, b2i = e2
    return (a2r * a1r - a2i * a1i,
            a2r * a1i + a2i * a1r,
            a2r * b1r - a2i * b1i + b2r,
            a2r * b1i + a2i * b1r + b2i)

def s5_states(u, h0_re, h0_im, ab_re, ab_im, bb_re, bb_im):
    bu_re = jnp.einsum('blgp,gnp->blgn', u, bb_re)
    bu_im = jnp.einsum('blgp,gnp->blgn', u, bb_im)
    bu_re = bu_re.at[:, 0].add(ab_re * h0_re - ab_im * h0_im)
    bu_im = bu_im.at[:, 0].add(ab_re * h0_im + ab_im * h0_re)
    a_re = jnp.broadcast_to(ab_re, bu_re.shape)
    a_im = jnp.broadcast_to(ab_im, bu_im.shape)
    _, _, h_re, h_im = lax.associative_scan(_complex_affine_combine,
                                            (a_re, a_im, bu_re, bu_im), axis=1)
    return h_re, h_im

def s5_readout(h_re, h_im, c_re, c_im):
    return (jnp.einsum('blgn,gpn->blgp', h_re, c_re.astype(jnp.float32))
            - jnp.einsum('blgn,gpn->blgp', h_im, c_im.astype(jnp.float32)))

def s5_glu(y, w_glu, b_glu):
    y = jax.nn.gelu(y)
    return y * jax.nn.sigmoid(y @ w_glu + b_glu)

def branch_merge(attn, gate_a, ssm, gate_s, w_out):
    merged = jnp.concatenate([attn * jax.nn.silu(gate_a),
                              ssm.astype(attn.dtype) * jax.nn.silu(gate_s)], axis=-1)
    return merged @ w_out

def hybrid_layer(x, ctx, c, c_ctx, w_ada, b_ada, pre_g, post_g, w_in, q_g, k_g,
                 lam_re, lam_im, log_dt, b_re, b_im, c_re, c_im, d_skip, w_glu, b_glu,
                 w_out, rope, update_ctx):
    bsz, n_lat, _ = x.shape
    n_ctx = ctx.shape[1]
    shift_l, scale_l, gate_l = adaln(c, w_ada, b_ada)
    shift_c, scale_c, gate_c = adaln(c_ctx, w_ada, b_ada)
    h_lat = modulate(rmsnorm(x, pre_g), shift_l[:, None], scale_l[:, None])
    h_ctx = modulate(rmsnorm(ctx, pre_g), shift_c, scale_c)
    q_l, k_l, v_l, ga_l, u_l, gs_l = mixer_inputs(h_lat, w_in, q_g, k_g)
    q_c, k_c, v_c, ga_c, u_c, gs_c = mixer_inputs(h_ctx, w_in, q_g, k_g)

    q_l = apply_axial_rope(q_l, rope)
    k_l = apply_axial_rope(k_l, rope)
    attn_l = latent_attention(q_l, k_l, v_l, k_c, v_c)

    d32 = d_skip.astype(jnp.float32)
    u_l_g = u_l.astype(jnp.float32).reshape(bsz, n_lat, N_SSM_GROUPS, SSM_GROUP)
    u_c_g = u_c.astype(jnp.float32).reshape(bsz, n_ctx, N_SSM_GROUPS, SSM_GROUP)
    zero = jnp.zeros((bsz, N_SSM_GROUPS, SSM_STATE), jnp.float32)
    y_l = d32 * u_l_g
    y_c = d32 * u_c_g
    for d in range(N_DIRS):
        def orient(a):
            return jnp.flip(a, axis=1) if d == 1 else a
        disc = s5_discretise(lam_re[d], lam_im[d], log_dt[d], b_re[d], b_im[d])
        hc_re, hc_im = s5_states(orient(u_c_g), zero, zero, *disc)
        hl_re, hl_im = s5_states(orient(u_l_g), hc_re[:, -1], hc_im[:, -1], *disc)
        y_l = y_l + orient(s5_readout(hl_re, hl_im, c_re[d], c_im[d]))
        if update_ctx:
            y_c = y_c + orient(s5_readout(hc_re, hc_im, c_re[d], c_im[d]))
    ssm_l = s5_glu(y_l.reshape(bsz, n_lat, SSM_WIDTH).astype(x.dtype), w_glu, b_glu)

    out_l = branch_merge(attn_l, ga_l, ssm_l, gs_l, w_out)
    x_new = x + gate_l[:, None] * rmsnorm(out_l, post_g)

    if update_ctx:
        attn_c = context_attention(q_c, k_c, v_c)
        ssm_c = s5_glu(y_c.reshape(bsz, n_ctx, SSM_WIDTH).astype(ctx.dtype), w_glu, b_glu)
        out_c = branch_merge(attn_c, ga_c, ssm_c, gs_c, w_out)
        ctx = ctx + gate_c * rmsnorm(out_c, post_g)
    return x_new, ctx

def setup_inputs(seed: int = 0) -> dict:
    key = jax.random.key(seed)
    ks = jax.random.split(key, 24)
    f32 = jnp.float32
    G, N, P = N_SSM_GROUPS, SSM_STATE, SSM_GROUP
    n_idx = jnp.arange(N, dtype=f32)
    return {
        'x': jax.random.normal(ks[0], (BATCH, SEQ, D_MODEL), f32),
        'c': jax.random.normal(ks[1], (BATCH, D_MODEL), f32),
        'ctx': jax.random.normal(ks[2], (BATCH, CTX_LEN, D_MODEL), f32),
        'c_ctx': jax.random.normal(ks[3], (D_MODEL,), f32),
        'w_ada': jax.random.normal(ks[4], (DEPTH, D_MODEL, 3 * D_MODEL), f32) * D_MODEL ** -0.5,
        'b_ada': jax.random.normal(ks[5], (DEPTH, 3 * D_MODEL), f32) * 0.01,
        'pre_norm': 1.0 + 0.02 * jax.random.normal(ks[6], (DEPTH, D_MODEL), f32),
        'post_norm': 1.0 + 0.02 * jax.random.normal(ks[7], (DEPTH, D_MODEL), f32),
        'w_in': jax.random.normal(ks[8], (DEPTH, D_MODEL, IN_WIDTH), f32) * D_MODEL ** -0.5,
        'q_norm': 1.0 + 0.02 * jax.random.normal(ks[9], (DEPTH, HEAD_DIM), f32),
        'k_norm': 1.0 + 0.02 * jax.random.normal(ks[10], (DEPTH, HEAD_DIM), f32),
        'ssm_lam_re': -0.5 + 0.01 * jax.random.normal(ks[11], (DEPTH, N_DIRS, G, N), f32),
        'ssm_lam_im': math.pi * n_idx + 0.01 * jax.random.normal(ks[12], (DEPTH, N_DIRS, G, N), f32),
        'ssm_log_dt': jax.random.uniform(ks[13], (DEPTH, N_DIRS, G), f32,
                                         minval=math.log(1e-3), maxval=math.log(1e-1)),
        'ssm_b_re': jax.random.normal(ks[14], (DEPTH, N_DIRS, G, N, P), f32) * (2 * P) ** -0.5,
        'ssm_b_im': jax.random.normal(ks[15], (DEPTH, N_DIRS, G, N, P), f32) * (2 * P) ** -0.5,
        'ssm_c_re': jax.random.normal(ks[16], (DEPTH, N_DIRS, G, P, N), f32) * N ** -0.5,
        'ssm_c_im': jax.random.normal(ks[17], (DEPTH, N_DIRS, G, P, N), f32) * N ** -0.5,
        'ssm_d': jax.random.normal(ks[18], (DEPTH, G, P), f32),
        'w_glu': jax.random.normal(ks[19], (DEPTH, SSM_WIDTH, SSM_WIDTH), f32) * SSM_WIDTH ** -0.5,
        'b_glu': jax.random.normal(ks[20], (DEPTH, SSM_WIDTH), f32) * 0.01,
        'w_out': jax.random.normal(ks[21], (DEPTH, D_MIX, D_MODEL), f32) * D_MIX ** -0.5,
    }

def reference(x, c, ctx, c_ctx, w_ada, b_ada, pre_norm, post_norm, w_in, q_norm, k_norm,
              ssm_lam_re, ssm_lam_im, ssm_log_dt, ssm_b_re, ssm_b_im, ssm_c_re, ssm_c_im,
              ssm_d, w_glu, b_glu, w_out):
    n_lat = x.shape[1]
    rows = n_lat // GRID_W
    row_pos = jnp.repeat(jnp.arange(rows, dtype=jnp.float32), GRID_W)
    col_pos = jnp.tile(jnp.arange(GRID_W, dtype=jnp.float32), rows)
    rope = axial_rope_tables(row_pos, col_pos)
    for i in range(DEPTH):
        x, ctx = hybrid_layer(x, ctx, c, c_ctx, w_ada[i], b_ada[i], pre_norm[i], post_norm[i],
                              w_in[i], q_norm[i], k_norm[i], ssm_lam_re[i], ssm_lam_im[i],
                              ssm_log_dt[i], ssm_b_re[i], ssm_b_im[i], ssm_c_re[i], ssm_c_im[i],
                              ssm_d[i], w_glu[i], b_glu[i], w_out[i], rope,
                              update_ctx=(i < DEPTH - 1))
    return x


_drawn_inputs = setup_inputs


def setup_inputs(seed=0):
    import zlib

    import numpy as np

    out = dict(_drawn_inputs(seed))
    spreads = {}
    factors = {'b_ada': 4.194,
     'pre_norm': 4.627,
     'post_norm': 18.052,
     'q_norm': 8.0,
     'k_norm': 8.0,
     'ssm_lam_re': 64.0,
     'b_glu': 64.0,
     'ssm_b_re': 3.069,
     'ssm_b_im': 3.075,
     'ssm_c_re': 3.135,
     'ssm_c_im': 3.096}
    for name, (base, spread) in spreads.items():
        noise = np.random.default_rng([zlib.crc32(name.encode()), seed]).standard_normal(out[name].shape)
        drawn = base * np.exp(spread * noise) if base else spread * noise
        out[name] = __import__('jax').numpy.asarray(drawn.astype(out[name].dtype))
    for name, factor in factors.items():
        out[name] = (out[name] * factor).astype(out[name].dtype)
    return out
```

```python
from contextlib import ExitStack

import concourse.bass as bass
from concourse import mybir

ALU = mybir.AluOpType
ACT = mybir.ActivationFunctionType
F32 = mybir.dt.float32
AX_X = mybir.AxisListType.X

P = 128
D = 1024
KT = D // P
S_LAT = 256
S_CTX = 256
TOK = S_CTX + S_LAT
HD = 64
NH = 8
NKV = 2
KEYT = TOK // P
EPS = 1e-6
G = 32
SP_ = 16
L = 8
NC = S_LAT // L
TAPS = L + 1
GW = G * SP_

Q0, KV0, GA0, U0, GS0 = 0, 512, 768, 1280, 1792

BW = 256
BLK = KT * BW
SLOTS = 5
STREAM = ([("ada", b) for b in (0, 4, 1, 5, 2, 6, 3, 7)]
          + [("u", 0), ("u", 1), ("kv", 0), ("q", 0), ("q", 1), ("ga", 0), ("ga", 1), ("gs", 0), ("gs", 1)]
          + [("ada", 8), ("ada", 9), ("ada", 10), ("ada", 11)]
          + [("T", 0), ("T", 1), ("glu", 0), ("x", 0)]
          + [("out", b) for b in range(4)])
PLACE = {key: n for n, key in enumerate(STREAM)}


def last_reader(n):
    kind, b = STREAM[n]
    if kind == "ada":
        return ("ada", n) if n < 8 else ("gate", b - 8)
    return {"u": ("u", 4 * b + 3), "kv": ("kv", 3), "q": ("q", b), "ga": ("ga", 2 * b + 1),
            "gs": ("gs", 2 * b + 1), "T": ("y", 1), "glu": ("glu", 3)}[kind]


USES = {}
RESULTS = {}


def _results():
    USES.clear()
    RESULTS.clear()

    def put(key, bank):
        USES[bank] = USES.get(bank, 0) + 1
        RESULTS[key] = (bank, USES[bank])

    for b in range(8):
        put(("ada", b), b % 2)
        put(("mT", b), 4)
    for k in range(KT):
        put(("xT", k), 2 + k % 2)
    for n in range(8):
        put(("u", n), n % 2)
        put(("phi", n, 0), 5)
        put(("phi", n, 1), 6)
    for n in range(8):
        put(("UT", n), 2 + n % 2)
    for n in range(8):
        put(("S", n), (4, 7)[n % 2])
    for n in range(4):
        put(("kv", n), n % 2)
    for n in range(2):
        put(("q", n), 5 + n)
    put(("M", 0), 4)
    put(("M", 1), 7)
    put(("M0", 0), 2)
    for n in range(4):
        put(("ga", n), n % 2)
    put(("kT", 0), 3)
    put(("qT", 0), 2)
    put(("qT", 1), 7)
    for n in range(2 * NH):
        put(("sc", n), 4 + n % 3)
        put(("pt", n), 2 + n % 2)
    for n in range(NH // 2):
        put(("o", n), 7)
    for n in range(4):
        put(("gs", n), n % 2)
    for n in range(4):
        put(("gate", n), n % 2)
    for n in range(2):
        put(("gb", n), n)
    for n in range(2):
        put(("y", n), 4 + n)
    for n in range(2):
        put(("yT", n), 2 + n)
    for n in range(4):
        put(("glu", n), (0, 1, 6, 7)[n])
    for n in range(4):
        put(("out", n), (4, 5, 2, 3)[n])


_results()

TWO_PI = 6.283185307179586
PI32 = 3.1415925
INV_2PI = 1.0 / TWO_PI
ROUND = 12582912.0
C1 = 6.28125
C2 = 0.0019350051879882812
C3 = TWO_PI - C1 - C2
MISC = 7


def bcast(ap, at, n):
    dims = [list(d) for d in ap.ap]
    dims.insert(at, [0, n])
    return bass.AP(ap.tensor, ap.offset, dims)


def hymba_layer(nc, x, cc, ctx_in, w_ada, b_ada_t, b_ada_g, pre_t, post, w_in, q_norm, k_norm,
                rope, lam_re, lam_im, log_dt, b_re, b_im, c_re, c_im, d_t, w_glu, b_glu_t, w_out,
                ident_in, quad_in, id16_in, out):
    kernel_scratch = nc.dram_tensor("toeplitz_rows", [G, SP_, (2 * L - 1) * SP_], F32, kind="Internal")
    rows = kernel_scratch.ap()

    with ExitStack() as stack:
        def sb(name, *shape):
            return stack.enter_context(nc.sbuf_tensor(name, [P, *shape], F32))

        def sem(name):
            return stack.enter_context(nc.semaphore(name))

        ps = stack.enter_context(nc.psum_tensor("ps", [P, 8, 512], F32))

        ring = sb("ring", SLOTS, BLK)
        hT_mem = sb("hT_mem", KT * TOK)
        psi = sb("psi", 2, G, TAPS, SP_)
        phi_mem = sb("phi_mem", G * 2 * P)
        scan_mem = sb("scan_mem", NC * 2 * 2 * G)
        U = sb("U", G, 2 * NC)
        early = sb("early", 4096)
        qT_mem = sb("qT_mem", NH * S_LAT)
        kT = sb("kT", TOK)
        V = sb("V", KEYT, NKV * HD)
        bc_mem = sb("bc_mem", 4, GW)
        bh = sb("bh", 2, GW + SP_)
        pw = sb("pw", TAPS, 2, G)
        e_psi = sb("e_psi", L, 2, G)
        pool_mem = sb("pool_mem", 8 * (L * SP_ + SP_))
        small = sb("small", 24, G)
        ident = sb("ident", P)
        quad = sb("quad", P)
        id16 = sb("id16", SP_)
        dcol = sb("dcol", 8)
        ropes = sb("ropes", 2, 2, HD)
        gains = sb("gains", 2, HD)
        kc_raw = sb("kc_raw", 2, NKV * HD)
        silu_c = sb("silu_c", KT, 32)
        ccb = sb("ccb", 2, KT)
        bias_ada = sb("bias_ada", 16)
        pre = sb("pre", KT)
        bglu = sb("bglu", 4)
        ssq = sb("ssq", 40)
        rstd = sb("rstd", 40)
        mhalf = sb("mhalf", 32)
        red = sb("red", 8, 2, 2)
        mshift = sb("mshift", KT, 2)
        mgain = sb("mgain", KT, 2)
        nmax = sb("nmax", 2 * NH)
        rsum = sb("rsum", 2 * NH)
        rinv = sb("rinv", 2 * NH)

        hT = hT_mem[:, :].rearrange("p (k t) -> p k t", k=KT)
        phi = phi_mem[:, :].rearrange("p (g r n) -> p g r n", g=G, r=2)
        S = scan_mem[:, :].rearrange("p (j b r g) -> p j b r g", j=NC, b=2, r=2)
        phiT = scan_mem[:, 0:2048].rearrange("p (b g r t q) -> p b g r t q", b=2, g=4, r=2, t=L)
        vt = scan_mem[:, 2048:4096].rearrange("p (i n) -> p i n", i=4)
        xc = early[:, :].rearrange("p (i d) -> p i d", i=4)
        u_sb = early[:, 0:2048].rearrange("p (g t q) -> p g t q", g=G, t=4)
        neg_c = early[:, 2048:3072].rearrange("p (r n) -> p r n", r=2)
        b_blk = early[:, 2048:4096].rearrange("p (r g n) -> p r g n", r=2, g=G)
        raw = early[:, 0:1280].rearrange("p (t n) -> p t n", t=2)
        rot_a = early[:, 1280:1920]
        prob = early[:, 0:2048].rearrange("p (i n) -> p i n", i=4)
        ga = early[:, 2048:3072].rearrange("p (i t) -> p i t", i=4)
        gs = early[:, 3072:4096].rearrange("p (i t) -> p i t", i=4)
        m_ada = V[:, :, :].rearrange("p a b -> p (a b)")[:, 0:512].rearrange("p (b n) -> p b n", b=2)
        w8 = qT_mem[:, :].rearrange("p (i r g) -> p i r g", i=NC, r=2)
        qT = qT_mem[:, :].rearrange("p (h t) -> p h t", h=NH)
        merged = phi_mem[:, 0:2048].rearrange("p (k t) -> p k t", k=KT)
        hprev = phi_mem[:, 2048:4096].rearrange("p (c r g) -> p c r g", c=NC, r=2)
        PT = phi_mem[:, 4096:8192].rearrange("p (b h k t) -> p b h k t", b=2, h=2, k=KEYT)
        pool_t = pool_mem[:, 0:1024].rearrange("p (i n) -> p i n", i=2)
        m_rows = pool_mem[:, :].rearrange("p (g n) -> p g n", g=8)
        gate_m = bc_mem[:, 0:2, :].rearrange("p a b -> p (a b)")
        post_b = bc_mem[:, 2:4, :].rearrange("p a b -> p (a b)")
        y_sb = hT_mem[:, 0:1024].rearrange("p (t g q) -> p t g q", g=8, t=L)
        yT = hT_mem[:, 1024:2048].rearrange("p (j t c) -> p j t c", j=4, t=L)
        gpost = hT_mem[:, 2048:3072]
        sig = hT_mem[:, 3072:4096].rearrange("p (i t c) -> p i t c", i=4, t=L)
        e_phi = kT[:, :].rearrange("p (t r g) -> p t r g", t=L, r=2)
        prod = bc_mem[:, 0, 0:256].rearrange("p (a g) -> p a g", a=8)
        qsum = bc_mem[:, 0, 256:384].rearrange("p (a g) -> p a g", a=4)
        brow = scan_mem[:, 2048:3072]
        rot_b = scan_mem[:, 3072:3712]
        o_sb = scan_mem[:, 0:2048].rearrange("p (i d) -> p i d", i=2)
        a4 = sb("a4", 4, G)
        h_ctx = sb("h_ctx", 2, G)
        skip = sb("skip", 8, SP_)
        sq_junk = sb("sq_junk", HD)
        sq_out = early[:, 0:512]

        slot_loaded = [sem(f"slot_loaded{s}") for s in range(SLOTS)]
        bank_filled = [sem(f"bank_filled{b}") for b in range(8)]
        bank_drained = [sem(f"bank_drained{b}") for b in range(8)]
        cc_loaded = sem("cc_loaded")
        lam_loaded = sem("lam_loaded")
        consts_loaded = sem("consts_loaded")
        xc_loaded = [sem(f"xc_loaded{i}") for i in range(4)]
        bc_loaded = sem("bc_loaded")
        misc_loaded = sem("misc_loaded")
        post_loaded = sem("post_loaded")
        brow_loaded = sem("brow_loaded")
        silu_zeroed = sem("silu_zeroed")
        silu_ready = sem("silu_ready")
        dt_ready = sem("dt_ready")
        damp_ready = sem("damp_ready")
        mag_ready = sem("mag_ready")
        angle_ready = sem("angle_ready")
        trig_ready = sem("trig_ready")
        ssx_ready = sem("ssx_ready")
        rstdx_ready = sem("rstdx_ready")
        xn_ready = sem("xn_ready")
        h_ready = sem("h_ready")
        phiT_ready = sem("phiT_ready")
        epsi_ready = sem("epsi_ready")
        pool_consts = sem("pool_consts")
        bblk_ready = sem("bblk_ready")
        skip_ready = sem("skip_ready")
        rows_written = sem("rows_written")
        ssqk_ready = sem("ssqk_ready")
        rstdqk_ready = sem("rstdqk_ready")
        w8_ready = sem("w8_ready")
        scan_step = sem("scan_step")
        hprev_ready = sem("hprev_ready")
        qT_zeroed = sem("qT_zeroed")
        rot_ready = sem("rot_ready")
        max_ready = sem("max_ready")
        prob_ready = sem("prob_ready")
        gs_ready = sem("gs_ready")
        merged_ssm = sem("merged_ssm")
        sig_ready = sem("sig_ready")
        sso_ready = sem("sso_ready")
        sso_sum = sem("sso_sum")
        rstdo_ready = sem("rstdo_ready")
        o_ready = sem("o_ready")
        out_written = sem("out_written")
        dve_step = sem("dve_step")
        act_step = sem("act_step")
        pool_step = sem("pool_step")

        def filled(eng, key):
            bank, use = RESULTS[key]
            eng.wait_ge(bank_filled[bank], use)
            return bank

        def drained(eng, key):
            bank, use = RESULTS[key]
            eng.wait_ge(bank_drained[bank], use)

        def block_of(key):
            return ring[:, PLACE[key] % SLOTS, :]

        def loaded(eng, key):
            n = PLACE[key]
            eng.wait_ge(slot_loaded[n % SLOTS], LOADS[key])

        LOADS = {}
        per_slot = [0] * SLOTS
        for n, key in enumerate(STREAM):
            per_slot[n % SLOTS] += 16 * (L if key[0] == "T" else 1)
            LOADS[key] = per_slot[n % SLOTS]

        block = stack.enter_context(nc.Block())

        @block.sync
        def _(sp):
            def cols(w, c0):
                return w.rearrange("(k p) n -> p k n", p=P)[:, :, c0:c0 + BW]

            sources = {"ada": (w_ada, 0), "u": (w_in, U0), "kv": (w_in, KV0), "q": (w_in, Q0),
                       "ga": (w_in, GA0), "gs": (w_in, GS0), "out": (w_out, 0)}
            for n, key in enumerate(STREAM):
                kind, b = key
                if n >= SLOTS:
                    filled(sp, last_reader(n - SLOTS))
                dst = ring[:, n % SLOTS, :]
                done = slot_loaded[n % SLOTS]
                if kind in sources:
                    w, c0 = sources[kind]
                    sp.dma_start(dst.rearrange("p (k n) -> p k n", k=KT), cols(w, c0 + b * BW)).then_inc(done, 16)
                elif kind == "glu":
                    sp.dma_start(dst.rearrange("p (k n) -> p k n", k=4),
                                 w_glu.rearrange("(k p) n -> p k n", p=P)).then_inc(done, 16)
                elif kind == "x":
                    sp.dma_start(dst.rearrange("p (k n) -> p k n", k=2),
                                 x.rearrange("(k p) n -> p k n", p=P)).then_inc(done, 16)
                else:
                    if b == 0:
                        sp.wait_ge(rows_written, 16 * 12)
                    for t in range(L):
                        src = rows.rearrange("g q n -> q g n")[:, b * 16:b * 16 + 16, (L - 1 - t) * SP_:(2 * L - 1 - t) * SP_]
                        sp.dma_start(dst.rearrange("p (g n) -> p g n", g=16)[t * SP_:(t + 1) * SP_],
                                     src).then_inc(done, 16)
            for t in range(2):
                sp.wait_ge(o_ready, 2 * (t + 1))
                sp.dma_start(out[t * P:(t + 1) * P, :], o_sb[:, t, :]).then_inc(out_written, 16)
            sp.wait_ge(out_written, 32)

        @block.gpsimd
        def _(pool):
            steps = [0]

            def step(ins):
                steps[0] += 1
                ins.then_inc(pool_step, 1)
                return steps[0]

            pool.memset(silu_c[:, :, :], 0.0).then_inc(silu_zeroed, 1)
            pool.memset(mhalf[:, :], -0.5).then_inc(pool_consts, 1)
            pool.memset(bh[:, :, GW:GW + SP_], 0.0).then_inc(pool_consts, 1)
            pool.memset(pw[:, 0, 0, :], 1.0).then_inc(pool_consts, 1)
            pool.memset(pw[:, 0, 1, :], 0.0).then_inc(pool_consts, 1)
            pool.memset(w8[:, 0, 0, :], 1.0).then_inc(pool_consts, 1)
            pool.memset(w8[:, 0, 1, :], 0.0).then_inc(pool_consts, 1)

            def rsqrt(n0, n1, ready, count):
                s = step(pool.tensor_scalar(rstd[:, n0:n1], ssq[:, n0:n1], 1.0 / count, EPS, ALU.mult, ALU.add))
                pool.wait_ge(pool_step, s)
                pool.tensor_tensor(rstd[:, n0:n1], rstd[:, n0:n1], mhalf[:, 0:n1 - n0], ALU.pow).then_inc(ready, 1)

            pool.wait_ge(pool_consts, 6)
            pool.wait_ge(ssx_ready, 4)
            rsqrt(0, 4, rstdx_ready, D)

            pool.wait_ge(bc_loaded, 64)
            filled(pool, ("xT", KT - 1))
            s = step(pool.tensor_scalar(neg_c[:, :, :], bc_mem[:, 2:4, :], -1.0, 0.0, ALU.mult, ALU.add))
            pool.wait_ge(pool_step, s)
            pool.wait_ge(epsi_ready, 2)

            def cmat(ap, g0):
                return bcast(ap[:, g0 * SP_:(g0 + 4) * SP_].rearrange("p (g q) -> p g q", g=4), 2, L)

            def power(r, g0):
                return bcast(e_psi[:, :, r, g0:g0 + 4].rearrange("p t g -> p g t"), 3, SP_)

            added = [0, 0]
            for g0 in range(0, G, 4):
                out_ = [psi[:, r, g0:g0 + 4, 1:TAPS, :] for r in range(2)]
                tmp = [pool_t[:, r, :].rearrange("p (g t q) -> p g t q", g=4, t=L) for r in range(2)]
                made = []
                for r, (c_a, c_b) in enumerate(((bc_mem[:, 2, :], neg_c[:, 1, :]), (neg_c[:, 1, :], neg_c[:, 0, :]))):
                    step(pool.tensor_tensor(out_[r], power(0, g0), cmat(c_a, g0), ALU.mult))
                    if added[r]:
                        pool.wait_ge(pool_step, added[r])
                    made.append(step(pool.tensor_tensor(tmp[r], power(1, g0), cmat(c_b, g0), ALU.mult)))
                for r in range(2):
                    pool.wait_ge(pool_step, made[r])
                    added[r] = step(pool.tensor_tensor(out_[r], out_[r], tmp[r], ALU.add))
            step(pool.tensor_copy(psi[:, 0, :, 0, :], bc_mem[:, 2, :].rearrange("p (g q) -> p g q", g=G)))
            s = step(pool.tensor_copy(psi[:, 1, :, 0, :], neg_c[:, 1, :].rearrange("p (g q) -> p g q", g=G)))
            pool.wait_ge(pool_step, s)
            pool.dma_start(post_b, bass.AP(post.tensor, post.offset, [[0, P], [1, D]])).then_inc(post_loaded, 16)
            s = step(pool.memset(b_blk[:, :, :, :], 0.0))
            pool.wait_ge(pool_step, s)
            for r in range(2):
                for d in range(2):
                    pool.tensor_copy(b_blk[d * 64:(d + 1) * 64, r, :, d * SP_:(d + 1) * SP_],
                                     bh[d * 64:(d + 1) * 64, r, 0:GW].rearrange("p (g q) -> p g q", g=G))\
                        .then_inc(bblk_ready, 1)
                    pool.wait_ge(bblk_ready, 2 * r + d + 1)
            pool.wait_ge(misc_loaded, 16 * MISC)
            pool.tensor_tensor(skip[:, :, :], bcast(dcol[:, :], 2, SP_), bcast(id16[:, :], 1, 8), ALU.mult)\
                .then_inc(skip_ready, 1)

            pool.wait_ge(ssqk_ready, 4)
            rsqrt(4, 28, rstdqk_ready, HD)
            pool.wait_ge(hprev_ready, 8)
            pool.wait_ge(rstdqk_ready, 1)
            pool.dma_start(brow[0:1, :], b_ada_g).then_inc(brow_loaded, 16)
            pool.memset(qT[64:128, 0:4, :], 0.0).then_inc(qT_zeroed, 1)
            pool.wait_ge(qT_zeroed, 1)
            pool.memset(qT[0:64, 4:8, :], 0.0).then_inc(qT_zeroed, 1)
            for key in (("M", 0), ("M", 1), ("M0", 0)):
                drained(pool, key)
            for j in range(4):
                for p0, c0, c1, r0 in ((0, 0, SP_, L - 1), (0, SP_, L * SP_, L), (SP_, 2 * SP_, TAPS * SP_, 0)):
                    dst = rows.rearrange("g q n -> q g n")[:, j * 8:j * 8 + 8, r0 * SP_:r0 * SP_ + c1 - c0]
                    pool.dma_start(dst, m_rows[32 * j + p0:32 * j + p0 + SP_, :, c0:c1]).then_inc(rows_written, 16)
            for t in range(2):
                pool.wait_ge(sso_sum, t + 1)
                rsqrt(36 + t, 37 + t, rstdo_ready, D)

        @block.scalar
        def _(act):
            def load(dst, src, s):
                act.dma_start(dst, src).then_inc(s, 16)

            load(ccb[:, :, :], cc, cc_loaded)
            load(small[:, 0, :], lam_re, lam_loaded)
            load(small[:, 1, :], lam_im, lam_loaded)
            for d in range(2):
                load(small[d * 64:(d + 1) * 64, 2, :], bass.AP(log_dt.tensor, log_dt.offset + d * G, [[0, 64], [1, G]]), lam_loaded)
            load(ident[:, :], ident_in, consts_loaded)
            for i in range(4):
                src = (ctx_in, x)[i // 2]
                load(xc[:, i, :], src[(i % 2) * P:(i % 2 + 1) * P, :], xc_loaded[i])
            for i, a in enumerate((b_re, b_im, c_re, c_im)):
                load(bc_mem[:, i, :], a, bc_loaded)
            load(bias_ada[:, :], b_ada_t, consts_loaded)
            load(pre[:, :], pre_t, consts_loaded)
            load(quad[:, :], quad_in, misc_loaded)
            load(id16[:, :], id16_in, misc_loaded)
            load(dcol[:, :], d_t, misc_loaded)
            load(bglu[:, :], b_glu_t, misc_loaded)
            load(ropes[:, :, :, :], rope.rearrange("(t p) r d -> p t r d", p=P), misc_loaded)
            load(gains[:, 0, :], bass.AP(q_norm.tensor, q_norm.offset, [[0, P], [1, HD]]), misc_loaded)
            load(gains[:, 1, :], bass.AP(k_norm.tensor, k_norm.offset, [[0, P], [1, HD]]), misc_loaded)

            act.wait_ge(cc_loaded, 16)
            act.wait_ge(silu_zeroed, 1)
            act.activation(silu_c[:, :, 0:2].rearrange("p k v -> p v k"), ccb[:, :, :], ACT.Silu).then_inc(silu_ready, 1)
            act.wait_ge(lam_loaded, 64)
            act.activation(small[:, 3, :], small[:, 2, :], ACT.Exp).then_inc(dt_ready, 1)
            act.wait_ge(damp_ready, 1)
            act.activation(small[:, 6, :], small[:, 4, :], ACT.Exp).then_inc(mag_ready, 1)
            act.wait_ge(angle_ready, 2)
            act.activation(small[:, 10:12, :], small[:, 8:10, :], ACT.Sin).then_inc(trig_ready, 1)
            for i in range(4):
                act.wait_ge(xc_loaded[i], 16)
                if i:
                    act.wait_ge(ssx_ready, i)
                act.activation(phi_mem[:, 0:1024], xc[:, i, :], ACT.Square, accum_out=ssq[:, i:i + 1]).then_inc(ssx_ready, 1)

            def copy_xT(k):
                bank = filled(act, ("xT", k))
                act.activation(hT[:, k, :], ps[:, bank, :], ACT.Copy).then_inc(bank_drained[bank], 1)

            def copy_ada(b):
                bank = filled(act, ("ada", b))
                if b >= 2:
                    act.wait_ge(bank_filled[4], RESULTS[("mT", b - 2)][1])
                act.activation(m_ada[:, b % 2, :], ps[:, bank, 0:BW], ACT.Copy).then_inc(bank_drained[bank], 1)

            def copy_phi(n):
                for h in range(2):
                    bank = filled(act, ("phi", n, h))
                    act.activation(phi[:, 4 * n + 2 * h:4 * n + 2 * h + 2, :, :].rearrange("p g r n -> p (g r n)"),
                                   ps[:, bank, :], ACT.Copy).then_inc(bank_drained[bank], 1)

            act.wait_ge(ssx_ready, 4)
            copy_ada(0)
            for k in range(4):
                copy_xT(k)
            copy_ada(1)
            for k in range(4, 8):
                copy_xT(k)
            for b in range(2, 8):
                copy_ada(b)
            for n in range(8):
                bank = filled(act, ("u", n))
                act.activation(u_sb[:, (n // 4) * 16:(n // 4 + 1) * 16, n % 4, :],
                               ps[:, bank, 0:BW].rearrange("p (g q) -> p g q", g=16), ACT.Copy)\
                    .then_inc(bank_drained[bank], 1)
                copy_phi(n)
            for n in range(8):
                bank = filled(act, ("UT", n))
                v = ps[0:64, bank, :].rearrange("p (g c t) -> p t g c", g=4, t=2)
                act.activation(U[0:64, 4 * n:4 * n + 4, :], v[:, 0], ACT.Copy)
                act.activation(U[64:128, 4 * n:4 * n + 4, :], v[:, 1], ACT.Copy).then_inc(bank_drained[bank], 1)
            act.wait_ge(w8_ready, 1)
            for n in range(8):
                bank = filled(act, ("S", n))
                r, g0 = n // 4, (n % 4) * 8
                act.activation(S[:, :, :, r, g0:g0 + 8].rearrange("p j b g -> p g b j"),
                               ps[:, bank, :].rearrange("p (g b j) -> p g b j", g=8, b=2), ACT.Copy)\
                    .then_inc(bank_drained[bank], 1)

            chain = [0]

            def act_chain(ins):
                chain[0] += 1
                ins.then_inc(act_step, 1)
                act.wait_ge(act_step, chain[0])

            for n in range(4):
                bank = filled(act, ("kv", n))
                dst = kc_raw[:, n, :] if n < 2 else raw[:, n - 2, 512:640]
                act_chain(act.activation(dst, ps[:, bank, 0:P], ACT.Copy))
                act.activation(V[:, n, :], ps[:, bank, P:2 * P], ACT.Copy).then_inc(bank_drained[bank], 1)
            for t in range(2):
                bank = filled(act, ("q", t))
                act.activation(raw[:, t, 0:512], ps[:, bank, :], ACT.Copy).then_inc(bank_drained[bank], 1)
            for t in range(2):
                drained(act, ("q", t))
                for h in range(10):
                    act_chain(act.activation(sq_junk[:, :], raw[:, t, h * HD:(h + 1) * HD], ACT.Square,
                                             accum_out=ssq[:, 4 + 10 * t + h:5 + 10 * t + h]))
                act.activation(sq_junk[:, :], kc_raw[:, t, 0:HD], ACT.Square,
                               accum_out=ssq[:, 24 + 2 * t:25 + 2 * t]).then_inc(ssqk_ready, 1)
                act.wait_ge(ssqk_ready, 2 * t + 1)
                act.activation(sq_junk[:, :], kc_raw[:, t, HD:2 * HD], ACT.Square,
                               accum_out=ssq[:, 25 + 2 * t:26 + 2 * t]).then_inc(ssqk_ready, 1)
                act.wait_ge(ssqk_ready, 2 * t + 2)

            for h in range(2):
                bank = filled(act, ("M", h))
                act.activation(m_rows[:, 4 * h:4 * h + 4, SP_:TAPS * SP_],
                               ps[:, bank, :].rearrange("p (g n) -> p g n", g=4), ACT.Copy).then_inc(bank_drained[bank], 1)
            for n in range(4):
                bank = filled(act, ("ga", n))
                act.activation(ga[:, n, :], ps[:, bank, 0:S_LAT], ACT.Silu).then_inc(bank_drained[bank], 1)
            bank = filled(act, ("kT", 0))
            act.activation(kT[:, :], ps[:, bank, :], ACT.Copy).then_inc(bank_drained[bank], 1)
            act.wait_ge(qT_zeroed, 2)
            for t in range(2):
                bank = filled(act, ("qT", t))
                for half in range(2):
                    rows_ = slice(64 * half, 64 * half + 64)
                    ins = act.activation(qT[rows_, 4 * half:4 * half + 4, t * P:(t + 1) * P],
                                         ps[rows_, bank, :].rearrange("p (h t) -> p h t", h=4), ACT.Copy)
                    if half == 0:
                        act_chain(ins)
                    else:
                        ins.then_inc(bank_drained[bank], 1)

            def fillers(s):
                if s < 4:
                    bank = filled(act, ("gs", s))
                    act.activation(gs[:, s, :], ps[:, bank, 0:S_LAT], ACT.Copy).then_inc(bank_drained[bank], 1)
                elif s < 8:
                    bank = filled(act, ("gate", s - 4))
                    act.activation(gate_m[:, (s - 4) * BW:(s - 3) * BW], ps[:, bank, 0:BW], ACT.Copy)\
                        .then_inc(bank_drained[bank], 1)

            def copy_pt(n):
                bank = filled(act, ("pt", n))
                h, t = n // 2, n % 2
                if h >= 4:
                    act.wait_ge(bank_filled[7], RESULTS[("o", h // 2 - 2)][1])
                act.activation(PT[:, (h // 2) % 2, h % 2, :, t * P:(t + 1) * P],
                               ps[:, bank, :].rearrange("p (k t) -> p k t", k=KEYT), ACT.Copy).then_inc(bank_drained[bank], 1)

            for s in range(NH + 1):
                if s < NH:
                    for t in range(2):
                        n = 2 * s + t
                        bank = filled(act, ("sc", n))
                        act.wait_ge(max_ready, n + 1)
                        if n == 0:
                            filled(act, ("qT", 1))
                        if n >= 4:
                            filled(act, ("pt", n - 4))
                        act.activation(prob[:, n % 4, :], ps[:, bank, :], ACT.Exp, bias=nmax[:, n:n + 1],
                                       accum_out=rsum[:, n:n + 1]).then_inc(bank_drained[bank], 1)
                if s >= 1:
                    copy_pt(2 * s - 2)
                    copy_pt(2 * s - 1)
                fillers(s)
            for n in range(4):
                drained(act, ("gs", n))
            act.activation(gs[:, :, :], gs[:, :, :], ACT.Silu).then_inc(gs_ready, 1)
            for h in range(2):
                bank = filled(act, ("y", h))
                act.activation(y_sb[:, :, 4 * h:4 * h + 4, :].rearrange("p t g q -> p g t q"), ps[:, bank, :].rearrange("p (g t q) -> p g t q", g=4, t=L),
                               ACT.Gelu_apprx_tanh).then_inc(bank_drained[bank], 1)
            for n in range(4):
                bank = filled(act, ("glu", n))
                act.activation(sig[:, n], ps[:, bank, 0:S_LAT].rearrange("p (t c) -> p t c", t=L), ACT.Sigmoid,
                               bias=bglu[:, n:n + 1]).then_inc(sig_ready, 1)
            for n in range(4):
                bank = filled(act, ("out", n))
                if n:
                    act.wait_ge(sso_ready, n)
                act.activation(sq_out[:, :], ps[:, bank, :], ACT.Square, accum_out=ssq[:, 28 + n:29 + n]).then_inc(sso_ready, 1)

        @block.vector
        def _(dve):
            steps = [0]

            def step(ins):
                steps[0] += 1
                ins.then_inc(dve_step, 1)
                return steps[0]

            def settle(s=None):
                dve.wait_ge(dve_step, steps[0] if s is None else s)

            tt = dve.tensor_tensor
            ts = dve.tensor_scalar
            stt = dve.scalar_tensor_tensor

            def cmul(o_re, o_im, a_re, a_im, b_re_, b_im_, t):
                step(tt(t[0], a_re, b_re_, ALU.mult))
                s1 = step(tt(t[1], a_im, b_im_, ALU.mult))
                step(tt(t[2], a_re, b_im_, ALU.mult))
                s2 = step(tt(t[3], a_im, b_re_, ALU.mult))
                settle(s1)
                step(tt(o_re, t[0], t[1], ALU.subtract))
                settle(s2)
                return step(tt(o_im, t[2], t[3], ALU.add))

            sm = lambda i: small[:, i, :]
            lr, li, dt = sm(0), sm(1), sm(3)
            dve.wait_ge(lam_loaded, 64)
            dve.wait_ge(dt_ready, 1)
            tt(sm(4), dt, lr, ALU.mult).then_inc(damp_ready, 1)
            step(tt(sm(5), dt, li, ALU.mult))
            settle()
            step(ts(sm(7), sm(5), INV_2PI, ROUND, ALU.mult, ALU.add))
            settle()
            step(ts(sm(7), sm(7), ROUND, None, ALU.subtract))
            settle()
            for c in (C1, C2, C3):
                step(stt(sm(5), sm(7), -c, sm(5), ALU.mult, ALU.add))
                settle()
            ts(sm(8), sm(5), PI32, -PI32, ALU.min, ALU.max).then_inc(angle_ready, 1)
            dve.wait_ge(angle_ready, 1)
            step(stt(sm(7), sm(8), -1.0, sm(8), ALU.mult, ALU.max))
            settle()
            ts(sm(9), sm(7), -1.0, TWO_PI / 4, ALU.mult, ALU.add).then_inc(angle_ready, 1)
            step(tt(sm(12), lr, lr, ALU.mult))
            step(tt(sm(13), li, li, ALU.mult))
            settle()
            step(tt(sm(12), sm(12), sm(13), ALU.add))
            settle()
            step(dve.reciprocal(sm(14), sm(12)))
            dve.wait_ge(trig_ready, 1)
            dve.wait_ge(mag_ready, 1)
            step(tt(pw[:, 1, 0, :], sm(6), sm(11), ALU.mult))
            step(tt(pw[:, 1, 1, :], sm(6), sm(10), ALU.mult))
            settle()
            step(ts(sm(15), pw[:, 1, 0, :], -1.0, None, ALU.add))
            settle()
            nr, ni = sm(15), pw[:, 1, 1, :]
            step(tt(sm(16), nr, lr, ALU.mult))
            step(tt(sm(17), ni, li, ALU.mult))
            step(tt(sm(18), ni, lr, ALU.mult))
            step(tt(sm(19), nr, li, ALU.mult))
            settle()
            step(tt(sm(16), sm(16), sm(17), ALU.add))
            step(tt(sm(18), sm(18), sm(19), ALU.subtract))
            settle()
            step(tt(sm(20), sm(16), sm(14), ALU.mult))
            step(tt(sm(21), sm(18), sm(14), ALU.mult))
            settle()
            tmp = [vt[:, i, :].rearrange("p (g q) -> p g q", g=G) for i in range(4)]
            dve.wait_ge(bc_loaded, 64)

            def gq(ap):
                return ap.rearrange("p (g q) -> p g q", g=G)

            cmul(gq(bh[:, 0, 0:GW]), gq(bh[:, 1, 0:GW]), bcast(sm(20), 2, SP_), bcast(sm(21), 2, SP_),
                 gq(bc_mem[:, 0, :]), gq(bc_mem[:, 1, :]), tmp)
            settle()
            dve.wait_ge(pool_consts, 6)

            def double(tab, n):
                m = min(n, tab.shape[1] - 1 - n)
                t4 = [vt[:, i, 0:m * G].rearrange("p (e g) -> p e g", g=G) for i in range(4)]
                cmul(tab[:, n + 1:n + 1 + m, 0, :], tab[:, n + 1:n + 1 + m, 1, :], tab[:, 1:1 + m, 0, :], tab[:, 1:1 + m, 1, :],
                     bcast(tab[:, n, 0, :], 1, m), bcast(tab[:, n, 1, :], 1, m), t4)
                settle()

            for n in (1, 2, 4):
                double(pw, n)
            dve.tensor_copy(e_psi[0:64], pw[0:64, 1:9]).then_inc(epsi_ready, 1)
            dve.tensor_copy(e_psi[64:128], pw[64:128, 8:0:-1]).then_inc(epsi_ready, 1)
            step(dve.tensor_copy(e_phi[0:64], pw[0:64, 7::-1]))
            step(dve.tensor_copy(e_phi[64:128], pw[64:128, 0:8]))
            settle()

            dve.wait_ge(rstdx_ready, 1)
            for i in range(4):
                ts(xc[:, i, :], xc[:, i, :], rstd[:, i:i + 1], None, ALU.mult).then_inc(xn_ready, 1)

            def phi_batch(n):
                g0 = 4 * n
                er = bcast(e_phi[:, :, 0, g0:g0 + 4].rearrange("p t g -> p g t"), 3, SP_)
                ei = bcast(e_phi[:, :, 1, g0:g0 + 4].rearrange("p t g -> p g t"), 3, SP_)
                br = bcast(gq(bh[:, 0, 0:GW])[:, g0:g0 + 4, :], 2, L)
                bi = bcast(gq(bh[:, 1, 0:GW])[:, g0:g0 + 4, :], 2, L)
                o = phiT[:, n % 2]
                t = [vt[:, i, :].rearrange("p (g t q) -> p g t q", g=4, t=L) for i in range(4)]
                settle()
                if n >= 2:
                    filled(dve, ("phi", n - 2, 1))
                step(tt(t[0], er, br, ALU.mult))
                s1 = step(tt(t[1], ei, bi, ALU.mult))
                step(tt(t[2], er, bi, ALU.mult))
                s2 = step(tt(t[3], ei, br, ALU.mult))
                settle(s1)
                tt(o[:, :, 0], t[0], t[1], ALU.subtract).then_inc(phiT_ready, 1)
                settle(s2)
                tt(o[:, :, 1], t[2], t[3], ALU.add).then_inc(phiT_ready, 1)
                dve.wait_ge(phiT_ready, 2 * n + 2)

            def ada_reduce(n):
                b = STREAM[n][1]
                bank = filled(dve, ("mT", n))
                dve.tensor_reduce(red[:, b, :, :], ps[:, bank, 0:2 * P].rearrange("p (f j v) -> p f v j", f=2, j=4)[:, :, 0:2, :],
                                  AX_X, ALU.add).then_inc(bank_drained[bank], 1)

            def modulate(pair):
                bank, use = RESULTS[("mT", 2 * pair + 1)]
                dve.wait_ge(bank_drained[bank], use)
                f = slice(2 * pair, 2 * pair + 2)
                step(tt(mshift[:, f, :], red[:, pair, :, :], bcast(bias_ada[:, f], 2, 2), ALU.add))
                step(tt(mgain[:, f, :], red[:, 4 + pair, :, :],
                        bcast(bias_ada[:, 8 + 2 * pair:10 + 2 * pair], 2, 2), ALU.add))
                settle()
                step(stt(mgain[:, f, :], mgain[:, f, :], 1.0, bcast(pre[:, f], 2, 2), ALU.add, ALU.mult))
                settle()
                for k in (2 * pair, 2 * pair + 1):
                    drained(dve, ("xT", k))
                    for v, c0 in ((1, 0), (0, S_CTX)):
                        o = hT[:, k, c0:c0 + 256]
                        ts(o, o, mgain[:, k, v:v + 1], mshift[:, k, v:v + 1], ALU.mult, ALU.add).then_inc(h_ready, 1)

            dve.wait_ge(consts_loaded, 48)
            for pair in range(4):
                ada_reduce(2 * pair)
                ada_reduce(2 * pair + 1)
                modulate(pair)
                if pair < 2:
                    phi_batch(pair)
            for n in range(2, 8):
                phi_batch(n)

            step(dve.tensor_copy(w8[:, 1, :, :], pw[:, 8, :, :]))
            settle()
            for n in (1, 2, 4, 8, 16):
                double(w8, n)
            step(dve.tensor_copy(a4[:, 0, :], pw[:, 8, 0, :]))
            step(dve.tensor_copy(a4[:, 2, :], pw[:, 8, 1, :]))
            step(ts(a4[:, 1, :], pw[:, 8, 1, :], -1.0, None, ALU.mult))
            settle()
            dve.tensor_copy(a4[:, 3, :], pw[:, 8, 0, :]).then_inc(w8_ready, 1)
            dve.wait_ge(w8_ready, 1)

            for n in range(8):
                drained(dve, ("S", n))
            a4v = bcast(a4[:, :, :].rearrange("p (o k) g -> p o (k g)", o=2), 1, 2)
            prodv = prod[:, :, :].rearrange("p (b o k) g -> p b o (k g)", b=2, o=2)
            pk = prod[:, :, :].rearrange("p (b k) g -> p k b g", k=2)

            def chunk(prev, here, done):
                tt(prodv, a4v, bcast(prev.rearrange("p (b n) -> p b n", b=2), 2, 2), ALU.mult).then_inc(scan_step, 1)
                dve.wait_ge(scan_step, done + 1)
                tt(qsum[:, :, :], pk[:, 0], pk[:, 1], ALU.add).then_inc(scan_step, 1)
                dve.wait_ge(scan_step, done + 2)
                tt(here, here, qsum[:, :, :].rearrange("p b g -> p (b g)"), ALU.add).then_inc(scan_step, 1)

            chunk(scan_mem[:, 0:128], scan_mem[:, 128:256], 0)
            with dve.Fori(1, NC - 1) as j:
                dve.wait_ge(scan_step, j * 3)
                chunk(scan_mem[:, bass.ds(j * 128, 128)], scan_mem[:, bass.ds(j * 128 + 128, 128)], j * 3)
            dve.wait_ge(scan_step, 3 * (NC - 1))
            step(dve.tensor_copy(h_ctx[:, :, :], S[:, NC - 1, 0, :, :]))
            settle()
            hr, hi = bcast(h_ctx[:, 0, :], 1, NC), bcast(h_ctx[:, 1, :], 1, NC)
            t1, t2 = S[:, :, 0, 0, :], S[:, :, 0, 1, :]
            for r in range(2):
                a, b = ((hr, hi), (hi, hr))[r]
                step(tt(t1, w8[:, :, 0, :], a, ALU.mult))
                step(tt(t2, w8[:, :, 1, :], b, ALU.mult))
                settle()
                step(tt(t1, t1, t2, ALU.subtract if r == 0 else ALU.add))
                settle()
                for d, c_first, c_rest in ((0, 0, slice(1, NC)), (1, NC - 1, slice(NC - 2, None, -1))):
                    h = slice(64 * d, 64 * d + 64)
                    dve.tensor_copy(hprev[h, c_first, r, :], t1[h, 0, :]).then_inc(hprev_ready, 1)
                    tt(hprev[h, c_rest, r, :], t1[h, 1:NC, :], S[h, 0:NC - 1, 1, r, :], ALU.add).then_inc(hprev_ready, 1)
                dve.wait_ge(hprev_ready, 4 * (r + 1))

            bank = filled(dve, ("M0", 0))
            dve.wait_ge(skip_ready, 1)
            tt(m_rows[:, :, 0:SP_], ps[:, bank, 0:8 * SP_].rearrange("p (g n) -> p g n", g=8), skip[:, :, :], ALU.add)\
                .then_inc(bank_drained[bank], 1)

            dve.wait_ge(misc_loaded, 16 * MISC)
            step(ts(gains[:, 0, :], gains[:, 0, :], float(HD) ** -0.5, None, ALU.mult))
            dve.wait_ge(rstdqk_ready, 1)
            settle()
            for t in range(2):
                k3 = kc_raw[:, t, :].rearrange("p (h d) -> p h d", h=NKV)
                step(tt(k3, k3, bcast(rstd[:, 24 + 2 * t:26 + 2 * t], 2, HD), ALU.mult))
                settle()
                tt(k3, k3, bcast(gains[:, 1, :], 1, NKV), ALU.mult).then_inc(rot_ready, 1)
            for t in range(2):
                h3 = raw[:, t, :].rearrange("p (h d) -> p h d", h=10)
                a3 = rot_a.rearrange("p (h d) -> p h d", h=10)
                step(tt(h3, h3, bcast(rstd[:, 4 + 10 * t:14 + 10 * t], 2, HD), ALU.mult))
                settle()
                step(tt(h3[:, 0:8], h3[:, 0:8], bcast(gains[:, 0, :], 1, 8), ALU.mult))
                step(tt(h3[:, 8:10], h3[:, 8:10], bcast(gains[:, 1, :], 1, 2), ALU.mult))
                settle()
                step(tt(a3, h3, bcast(ropes[:, t, 0, :], 1, 10), ALU.mult))
                h5 = raw[:, t, :].rearrange("p (h s d) -> p s h d", s=2, d=16)
                b5 = rot_b[:, :].rearrange("p (h s d) -> p s h d", s=2, d=16)
                for s_ in range(2):
                    for half in range(2):
                        sin = ropes[:, t, 1, half * 32 + s_ * 16:half * 32 + s_ * 16 + 16]
                        step(tt(b5[:, s_, half::2], h5[:, 1 - s_, half::2], bcast(sin, 1, 10), ALU.mult))
                settle()
                tt(raw[:, t, 0:512].rearrange("p (i half d) -> p half i d", half=2, d=HD),
                   rot_a[:, 0:512].rearrange("p (half i d) -> p half i d", half=2, d=HD),
                   rot_b[:, 0:512].rearrange("p (half i d) -> p half i d", half=2, d=HD), ALU.add).then_inc(rot_ready, 1)
                tt(raw[:, t, 512:640], rot_a[:, 512:640], rot_b[:, 512:640], ALU.add).then_inc(rot_ready, 1)
                dve.wait_ge(rot_ready, 4 + 2 * t)

            def norm(n):
                bank, use = RESULTS[("sc", n)]
                dve.wait_ge(bank_drained[bank], use)
                step(dve.reciprocal(rinv[:, n:n + 1], rsum[:, n:n + 1]))
                settle()
                ts(prob[:, n % 4, :], prob[:, n % 4, :], rinv[:, n:n + 1], None, ALU.mult).then_inc(prob_ready, 1)

            def merge_attn(i):
                bank = filled(dve, ("o", i))
                if i == 0:
                    for n in range(4):
                        drained(dve, ("ga", n))
                tt(merged[:, i, :], ps[:, bank, 0:S_LAT], ga[:, i, :], ALU.mult).then_inc(bank_drained[bank], 1)

            for s in range(NH + 2):
                if s < NH:
                    for t in range(2):
                        n = 2 * s + t
                        bank = filled(dve, ("sc", n))
                        dve.tensor_reduce(nmax[:, n:n + 1], ps[:, bank, :], AX_X, ALU.max, negate=True).then_inc(max_ready, 1)
                    norm(2 * s)
                    norm(2 * s + 1)
                if s >= 3 and s % 2 == 1:
                    merge_attn((s - 3) // 2)

            dve.wait_ge(post_loaded, 16)
            for h in range(2):
                bank = filled(dve, ("gb", h))
                tt(gpost[:, h * 512:(h + 1) * 512], ps[:, bank, :], post_b[:, h * 512:(h + 1) * 512], ALU.mult)\
                    .then_inc(bank_drained[bank], 1)
            for h in range(2):
                bank = filled(dve, ("yT", h))
                dve.tensor_copy(yT[:, :, 4 * h:4 * h + 4, :].rearrange("p j t c -> p t j c"),
                                ps[:, bank, :].rearrange("p (t j c) -> p t j c", t=4, j=4)).then_inc(bank_drained[bank], 1)
            dve.wait_ge(gs_ready, 1)
            for h in range(2):
                drained(dve, ("yT", h))
            for n in range(4):
                dve.wait_ge(sig_ready, n + 1)
                step(tt(sig[:, n], sig[:, n], yT[:, n], ALU.mult))
                settle()
                tt(merged[:, 4 + n, :].rearrange("p (c t) -> p t c", t=L), sig[:, n],
                   gs[:, n, :].rearrange("p (c t) -> p t c", t=L), ALU.mult).then_inc(merged_ssm, 1)
            loaded(dve, ("x", 0))
            xr = block_of(("x", 0)).rearrange("p (t n) -> p t n", t=2)
            for h in range(2):
                drained(dve, ("gb", h))
            for t in range(2):
                dve.wait_ge(sso_ready, 2 * t + 2)
                tt(ssq[:, 36 + t:37 + t], ssq[:, 28 + 2 * t:29 + 2 * t], ssq[:, 29 + 2 * t:30 + 2 * t], ALU.add).then_inc(sso_sum, 1)
                dve.wait_ge(rstdo_ready, t + 1)
                for h in range(2):
                    bank, _ = RESULTS[("out", 2 * t + h)]
                    c = slice(512 * h, 512 * h + 512)
                    step(stt(o_sb[:, t, c], ps[:, bank, :], rstd[:, 36 + t:37 + t], gpost[:, c], ALU.mult, ALU.mult))
                    settle()
                    tt(o_sb[:, t, c], o_sb[:, t, c], xr[:, t, c], ALU.add).then_inc(o_ready, 1)

        @block.tensor
        def _(pe):
            mm = pe.matmul

            def free(key):
                bank, use = RESULTS[key]
                if use > 1:
                    pe.wait_ge(bank_drained[bank], use - 1)
                return bank

            def fill(ins, bank):
                ins.then_inc(bank_filled[bank], 1)

            def ada(n, key, b):
                bank = free(key)
                loaded(pe, ("ada", b))
                w = block_of(("ada", b)).rearrange("p (k n) -> p k n", k=KT)
                for k in range(KT):
                    j = k % 4
                    last = mm(ps[32 * j:32 * j + 32, bank, 0:BW], silu_c[:, k, :], w[:, k, :], start=k < 4, stop=k >= 4)
                fill(last, bank)

            def turn_ada(n):
                bank = free(("mT", n))
                drained(pe, ("ada", n))
                for f in range(2):
                    last = pe.transpose(ps[:, bank, f * P:(f + 1) * P], m_ada[:, n % 2, f * P:(f + 1) * P], ident[:, :])
                fill(last, bank)

            def turn_x(k):
                bank = free(("xT", k))
                for i in range(4):
                    if k == 0:
                        pe.wait_ge(xn_ready, i + 1)
                    last = pe.transpose(ps[:, bank, i * P:(i + 1) * P], xc[:, i, k * P:(k + 1) * P], ident[:, :])
                fill(last, bank)

            pe.wait_ge(consts_loaded, 48)
            pe.wait_ge(silu_ready, 1)

            for n in range(8):
                ada(n, ("ada", n), STREAM[n][1])
                if n < 2:
                    for k in range(4 * n, 4 * n + 4):
                        turn_x(k)
                if n >= 1:
                    turn_ada(n - 1)
            turn_ada(7)

            def project_u(n):
                b, t = n // 4, n % 4
                bank = free(("u", n))
                loaded(pe, ("u", b))
                w = block_of(("u", b)).rearrange("p (k n) -> p k n", k=KT)
                for k in range(KT):
                    if n == 0:
                        pe.wait_ge(h_ready, 4 * (k // 2) + 2 * (k % 2) + 2)
                    last = mm(ps[:, bank, 0:BW], hT[:, k, t::4], w[:, k, :], start=k == 0, stop=k == KT - 1)
                fill(last, bank)

            def turn_phi(n):
                pe.wait_ge(phiT_ready, 2 * n + 2)
                for h in range(2):
                    bank = free(("phi", n, h))
                    for i in range(4):
                        g, r = 2 * h + i // 2, i % 2
                        last = pe.transpose(ps[:, bank, i * P:(i + 1) * P],
                                            phiT[:, n % 2, g, r].rearrange("p t q -> p (t q)"), ident[:, :])
                    fill(last, bank)

            for n in range(8):
                project_u(n)
                turn_phi(n)
            for n in range(8):
                drained(pe, ("u", n))
            for n in range(8):
                bank = free(("UT", n))
                for i in range(4):
                    g = 4 * n + i
                    last = pe.transpose(ps[0:64, bank, i * P:(i + 1) * P], u_sb[:, g].rearrange("p t q -> p (t q)"), ident[:, :])
                fill(last, bank)
            for n in range(8):
                drained(pe, ("phi", n, 0))
                drained(pe, ("phi", n, 1))
            for n in range(8):
                bank = free(("S", n))
                r, g0 = n // 4, (n % 4) * 8
                for i in range(8):
                    g = g0 + i
                    drained(pe, ("UT", g // 4))
                    ug = U[:, g, :].rearrange("p (b j) -> p b j", b=2)
                    for d in range(2):
                        last = mm(ps[64 * d:64 * d + 64, bank, i * 64:(i + 1) * 64].rearrange("p (b j) -> p b j", b=2),
                                  phi[:, g, r, 64 * d:64 * d + 64], ug if d == 0 else ug[:, :, ::-1], start=True, stop=True)
                fill(last, bank)

            def project(key, wkey, cols, c0, off=0, done=True):
                bank, use = RESULTS[key]
                if off == 0:
                    free(key)
                loaded(pe, wkey)
                w = block_of(wkey).rearrange("p (k n) -> p k n", k=KT)
                for k in range(KT):
                    last = mm(ps[:, bank, off:off + BW], hT[:, k, c0:c0 + P], w[:, k, :], start=k == 0, stop=k == KT - 1)
                if done:
                    fill(last, bank)

            def project_T(key, wkey, c0):
                bank = free(key)
                loaded(pe, wkey)
                w = block_of(wkey).rearrange("p (k n) -> p k n", k=KT)
                for k in range(KT):
                    last = mm(ps[:, bank, 0:S_LAT], w[:, k, c0:c0 + P], hT[:, k, S_CTX:TOK], start=k == 0, stop=k == KT - 1)
                fill(last, bank)

            for n in range(4):
                project(("kv", n), ("kv", 0), None, n * P)
            for b in range(2):
                for t in range(2):
                    project(("q", t), ("q", b), None, S_CTX + t * P, off=b * BW, done=b == 1)

            pe.wait_ge(bblk_ready, 4)
            for h in range(2):
                bank = free(("M", h))
                for i in range(4):
                    for r in range(2):
                        for j in range(4):
                            g = 8 * j + 4 * h + i
                            last = mm(ps[32 * j:32 * j + 32, bank, i * P:(i + 1) * P], b_blk[:, r, g, :],
                                      psi[:, r, g, 1:TAPS, :], start=r == 0, stop=r == 1)
                fill(last, bank)
            bank = free(("M0", 0))
            for i in range(8):
                for r in range(2):
                    for j in range(4):
                        g = 8 * j + i
                        last = mm(ps[32 * j:32 * j + 32, bank, i * SP_:(i + 1) * SP_], bh[:, r, g * SP_:g * SP_ + 32],
                                  psi[:, r, g, 0, :], start=r == 0, stop=r == 1)
            fill(last, bank)

            for n in range(4):
                project_T(("ga", n), ("ga", n // 2), (n % 2) * P)

            bank = free(("kT", 0))
            pe.wait_ge(rot_ready, 2)
            for n in range(4):
                if n == 2:
                    pe.wait_ge(rot_ready, 6)
                src = kc_raw[:, n, :] if n < 2 else raw[:, n - 2, 512:640]
                last = pe.transpose(ps[:, bank, n * P:(n + 1) * P], src, ident[:, :])
            fill(last, bank)
            for t in range(2):
                bank = free(("qT", t))
                for i in range(4):
                    last = pe.transpose(ps[:, bank, i * P:(i + 1) * P], raw[:, t, i * P:(i + 1) * P], ident[:, :])
                fill(last, bank)

            def scores(n):
                h, t = n // 2, n % 2
                bank = free(("sc", n))
                if n == 0:
                    drained(pe, ("kT", 0))
                    drained(pe, ("qT", 0))
                    drained(pe, ("qT", 1))
                fill(mm(ps[:, bank, :], qT[:, h, t * P:(t + 1) * P], kT[:, :], start=True, stop=True), bank)

            def turn_probs(n):
                bank = free(("pt", n))
                pe.wait_ge(prob_ready, n + 1)
                for k in range(KEYT):
                    last = pe.transpose(ps[:, bank, k * P:(k + 1) * P], prob[:, n % 4, k * P:(k + 1) * P], ident[:, :])
                fill(last, bank)

            def attend(i):
                bank = free(("o", i))
                for n in range(4 * i, 4 * i + 4):
                    drained(pe, ("pt", n))
                kv = i // 2
                for k in range(KEYT):
                    for e in range(2):
                        last = mm(ps[64 * e:64 * e + 64, bank, 0:S_LAT], V[:, k, kv * HD:(kv + 1) * HD], PT[:, i % 2, e, k, :],
                                  start=k == 0, stop=k == KEYT - 1)
                fill(last, bank)

            for s in range(NH + 2):
                if s < NH:
                    scores(2 * s)
                    scores(2 * s + 1)
                if s < 4:
                    project_T(("gs", s), ("gs", s // 2), (s % 2) * P)
                elif s < 8:
                    ada(s, ("gate", s - 4), s + 4)
                if 1 <= s <= NH:
                    turn_probs(2 * s - 2)
                    turn_probs(2 * s - 1)
                if s >= 3 and s % 2 == 1:
                    attend((s - 3) // 2)

            for n in range(4):
                drained(pe, ("gate", n))
            pe.wait_ge(misc_loaded, 16 * MISC)
            pe.wait_ge(brow_loaded, 16)
            for h in range(2):
                bank = free(("gb", h))
                c = slice(512 * h, 512 * h + 512)
                mm(ps[:, bank, :], quad[:, :], gate_m[:, c], start=True, stop=False)
                fill(mm(ps[:, bank, :], quad[0:1, :], brow[0:1, c], start=False, stop=True), bank)

            pe.wait_ge(hprev_ready, 8)
            loaded(pe, ("T", 0))
            loaded(pe, ("T", 1))
            for h in range(2):
                bank = free(("y", h))
                for i in range(4):
                    for part in range(3):
                        for j in range(4):
                            g = 8 * j + 4 * h + i
                            if part < 2:
                                a, b = hprev[:, :, part, g], psi[:, part, g, 1:TAPS, :]
                            else:
                                T = block_of(("T", g // 16)).rearrange("p (g n) -> p g n", g=16)
                                a, b = U[:, g, NC:2 * NC], T[:, g % 16, :]
                            last = mm(ps[32 * j:32 * j + 32, bank, i * P:(i + 1) * P], a, b, start=part == 0, stop=part == 2)
                fill(last, bank)
            drained(pe, ("y", 0))
            drained(pe, ("y", 1))
            for h in range(2):
                bank = free(("yT", h))
                for i in range(4):
                    last = pe.transpose(ps[:, bank, i * P:(i + 1) * P], y_sb[:, 4 * h + i].rearrange("p g q -> p (g q)"), ident[:, :])
                fill(last, bank)
            drained(pe, ("yT", 0))
            drained(pe, ("yT", 1))
            loaded(pe, ("glu", 0))
            w = block_of(("glu", 0)).rearrange("p (k n) -> p k n", k=4)
            for n in range(4):
                bank = free(("glu", n))
                for k in range(4):
                    last = mm(ps[:, bank, 0:S_LAT], w[:, k, n * P:(n + 1) * P], yT[:, k].rearrange("p t c -> p (t c)"),
                              start=k == 0, stop=k == 3)
                fill(last, bank)
            for i in range(4):
                drained(pe, ("o", i))
            pe.wait_ge(merged_ssm, 4)
            for b in range(4):
                loaded(pe, ("out", b))
                w = block_of(("out", b)).rearrange("p (k n) -> p k n", k=KT)
                for t in range(2):
                    key = ("out", 2 * t + b // 2)
                    bank = RESULTS[key][0]
                    if b % 2 == 0:
                        free(key)
                    for k in range(KT):
                        last = mm(ps[:, bank, (b % 2) * BW:(b % 2 + 1) * BW], merged[:, k, t * P:(t + 1) * P], w[:, k, :],
                                  start=k == 0, stop=k == KT - 1)
                    if b % 2 == 1:
                        fill(last, bank)


def kernel(x, c, ctx, c_ctx, w_ada, b_ada, pre_norm, post_norm, w_in, q_norm, k_norm,
           ssm_lam_re, ssm_lam_im, ssm_log_dt, ssm_b_re, ssm_b_im, ssm_c_re, ssm_c_im,
           ssm_d, w_glu, b_glu, w_out):
    import numpy as np
    import concourse.bacc as bacc
    from concourse.bass_utils import run_bass_kernel_spmd

    f = np.float32
    x, c, ctx, c_ctx, w_ada, b_ada, pre_norm, post_norm, w_in, q_norm, k_norm = (
        np.asarray(a) for a in (x, c, ctx, c_ctx, w_ada, b_ada, pre_norm, post_norm, w_in, q_norm, k_norm))
    w_glu, b_glu, w_out = (np.asarray(a) for a in (w_glu, b_glu, w_out))

    def states(a):
        a = np.asarray(a)[0]
        return np.moveaxis(a, 2, 1).reshape(P, -1)

    grid_w, freqs = 64, HD // 4
    inv = (f(10000.0) ** (-np.arange(freqs, dtype=f) / f(freqs))).astype(f)
    pos = np.arange(S_LAT)
    ang = np.stack([(pos // grid_w).astype(f)[:, None] * inv, (pos % grid_w).astype(f)[:, None] * inv], 1)
    cos, sin = np.cos(ang).astype(f), np.sin(ang).astype(f)
    rope = np.stack([np.stack([cos, cos], 2).reshape(S_LAT, HD), np.stack([-sin, sin], 2).reshape(S_LAT, HD)], 1)

    d = np.asarray(ssm_d)[0]
    d_t = np.zeros((4, 32, 8), f)
    d_t[:, 0:SP_, :] = np.swapaxes(d.reshape(4, 8, SP_), 1, 2)
    quad = np.zeros((P, P), f)
    quad[::32] = 1.0
    id16 = np.zeros((4, 32, SP_), f)
    id16[:, 0:SP_] = np.eye(SP_, dtype=f)

    arrays = {
        "x": x[0], "cc": np.stack([c[0].reshape(KT, P).T, c_ctx.reshape(KT, P).T], 1), "ctx_in": ctx[0],
        "w_ada": w_ada[0], "b_ada_t": b_ada[0, :2 * D].reshape(2 * KT, P).T, "b_ada_g": b_ada[:, 2 * D:],
        "pre_t": pre_norm[0].reshape(KT, P).T, "post": post_norm[0], "w_in": w_in[0],
        "q_norm": q_norm[0], "k_norm": k_norm[0], "rope": rope,
        "lam_re": states(ssm_lam_re), "lam_im": states(ssm_lam_im), "log_dt": np.asarray(ssm_log_dt)[0],
        "b_re": states(ssm_b_re), "b_im": states(ssm_b_im),
        "c_re": states(np.swapaxes(np.asarray(ssm_c_re), 3, 4)), "c_im": states(np.swapaxes(np.asarray(ssm_c_im), 3, 4)),
        "d_t": d_t.reshape(P, 8), "w_glu": w_glu[0], "b_glu_t": b_glu[0].reshape(4, P).T, "w_out": w_out[0],
        "ident_in": np.eye(P, dtype=f), "quad_in": quad, "id16_in": id16.reshape(P, SP_),
    }
    nc = bacc.Bacc("TRN2", target_bir_lowering=False, num_devices=1)
    args = {}
    for name, a in arrays.items():
        arrays[name] = np.ascontiguousarray(a)
        args[name] = nc.dram_tensor(name, arrays[name].shape, F32, kind="ExternalInput").ap()
    args["out"] = nc.dram_tensor("out", (S_LAT, D), F32, kind="ExternalOutput").ap()
    hymba_layer(nc, **args)
    result = run_bass_kernel_spmd(nc, [arrays], core_ids=[0])
    return result.results[0]["out"].reshape(1, S_LAT, D)
```

```python
from contextlib import ExitStack

import concourse.bass as bass
from concourse import mybir

ALU = mybir.AluOpType
ACT = mybir.ActivationFunctionType
F32 = mybir.dt.float32
AX_X = mybir.AxisListType.X

P = 128
D = 1024
KT = D // P
S_LAT = 256
S_CTX = 256
TOK = S_CTX + S_LAT
HD = 64
NH = 8
NKV = 2
KEYT = TOK // P
EPS = 1e-6
G = 32
SP_ = 16
L = 8
NC = S_LAT // L
TAPS = L + 1
SEG = 4
NJ = NC // SEG
ROW = 2 * SEG * 2 * G
GW = G * SP_
SSM_N = 64

Q0, KV0, GA0, U0, GS0 = 0, 512, 768, 1280, 1792

BW = 256
BLK = KT * BW
SLOTS = 5
STREAM = ([("ada", b) for b in (0, 4, 1, 5, 2, 6, 3, 7)]
          + [("u", 0), ("u", 1), ("kv", 0), ("q", 0), ("q", 1), ("ga", 0), ("ga", 1), ("gs", 0), ("gs", 1)]
          + [("ada", 8), ("ada", 9), ("ada", 10), ("ada", 11)]
          + [("T", 0), ("T", 1), ("glu", 0), ("x", 0)]
          + [("out", b) for b in range(4)])
PLACE = {key: n for n, key in enumerate(STREAM)}


def last_reader(n):
    kind, b = STREAM[n]
    if kind == "ada":
        return ("ada", n) if n < 8 else ("gate", b - 8)
    return {"u": ("u", 4 * b + 3), "kv": ("kv", 3), "q": ("q", b), "ga": ("ga", 2 * b + 1),
            "gs": ("gs", 2 * b + 1), "T": ("y", 1), "glu": ("glu", 3)}[kind]


USES = {}
RESULTS = {}


def _results():
    USES.clear()
    RESULTS.clear()

    def put(key, bank):
        USES[bank] = USES.get(bank, 0) + 1
        RESULTS[key] = (bank, USES[bank])

    for b in range(8):
        put(("ada", b), b % 2)
        put(("mT", b), 4)
    for k in range(KT):
        put(("xT", k), 2 + k % 2)
    for n in range(8):
        put(("u", n), n % 2)
        put(("phi", n, 0), 5)
        put(("phi", n, 1), 6)
    for n in range(8):
        put(("UT", n), 2 + n % 2)
    for n in range(8):
        put(("S", n), (4, 7)[n % 2])
    for n in range(4):
        put(("kv", n), n % 2)
    for n in range(2):
        put(("q", n), 5 + n)
    put(("M", 0), 4)
    put(("M", 1), 7)
    put(("M0", 0), 2)
    for n in range(4):
        put(("ga", n), n % 2)
    for n in range(4):
        put(("gs", n), n % 2)
    for n in range(4):
        put(("gate", n), n % 2)
    put(("kT", 0), 3)
    put(("qT", 0), 2)
    put(("qT", 1), 7)
    for n in range(2 * NH):
        put(("sc", n), 4 + n % 3)
        put(("pt", n), 2 + n % 2)
    for n in range(NH // 2):
        put(("o", n), 7)
    for n in range(2):
        put(("gb", n), n)
    for n in range(2):
        put(("y", n), 4 + n)
    for n in range(2):
        put(("yT", n), 2 + n)
    for n in range(4):
        put(("glu", n), (0, 1, 6, 7)[n])
    for n in range(4):
        put(("out", n), (4, 5, 2, 3)[n])


_results()

TWO_PI = 6.283185307179586
PI32 = 3.1415925
INV_2PI = 1.0 / TWO_PI
ROUND = 12582912.0
C1 = 6.28125
C2 = 0.0019350051879882812
C3 = TWO_PI - C1 - C2
MISC = 2
FIRST = {"cc": 2 * KT, "bias": 2 * KT, "pre": KT, "lam": 3 * G}
TABLES = {"quad": P, "id16": SP_, "d": 8, "bglu": 4, "rope": 4 * HD}


def bcast(ap, at, n):
    dims = [list(d) for d in ap.ap]
    dims.insert(at, [0, n])
    return bass.AP(ap.tensor, ap.offset, dims)


def columns(ap, widths):
    views, at = {}, 0
    for name, width in widths.items():
        views[name] = ap[:, at:at + width]
        at += width
    return views


def hymba_layer(nc, x, first_in, ctx_in, w_ada, b_ada_g, post, w_in, qk_norm, bc_in, w_glu, w_out,
                ident_in, tables_in, out):
    kernel_scratch = nc.dram_tensor("toeplitz_rows", [G, SP_, (2 * L - 1) * SP_], F32, kind="Internal")
    rows = kernel_scratch.ap()

    with ExitStack() as stack:
        def sb(name, *shape):
            return stack.enter_context(nc.sbuf_tensor(name, [P, *shape], F32))

        def sem(name):
            return stack.enter_context(nc.semaphore(name))

        ps = stack.enter_context(nc.psum_tensor("ps", [P, 8, 512], F32))

        ring = sb("ring", SLOTS, BLK)
        hT_mem = sb("hT_mem", KT * TOK)
        psi = sb("psi", 2, G, TAPS, SP_)
        phi_mem = sb("phi_mem", G * 2 * P)
        scan_mem = sb("scan_mem", NC * 2 * 2 * G)
        U = sb("U", G, 2 * NC)
        early = sb("early", 4096)
        qT_mem = sb("qT_mem", NH * S_LAT)
        kT = sb("kT", TOK)
        V = sb("V", KEYT, NKV * HD)
        bc_mem = sb("bc_mem", 4, GW)
        bh = sb("bh", 2, GW + SP_)
        pw = sb("pw", TAPS, 2, G)
        e_psi = sb("e_psi", L, 2, G)
        pool_mem = sb("pool_mem", 8 * (L * SP_ + SP_))
        small = sb("small", 24, G)
        ident = sb("ident", P)
        gains = sb("gains", 2, HD)
        kc_raw = sb("kc_raw", 2, NKV * HD)
        silu_c = sb("silu_c", KT, 32)
        ssq = sb("ssq", 40)
        rstd = sb("rstd", 40)
        mhalf = sb("mhalf", 32)
        red = sb("red", 8, 2, 2)
        mshift = sb("mshift", KT, 2)
        mgain = sb("mgain", KT, 2)
        nmax = sb("nmax", 2 * NH)
        rsum = sb("rsum", 2 * NH)
        rinv = sb("rinv", 2 * NH)

        first = sb("first", sum(FIRST.values()))
        ccb, bias_ada, pre, lam = columns(first, FIRST).values()
        ccb = ccb.rearrange("p (v k) -> p v k", v=2)
        lam = lam.rearrange("p (i g) -> p i g", i=3)
        tables = sb("tables", sum(TABLES.values()))
        quad, id16, dcol, bglu, ropes = columns(tables, TABLES).values()
        ropes = ropes.rearrange("p (t r d) -> p t r d", t=2, r=2)

        hT = hT_mem[:, :].rearrange("p (k t) -> p k t", k=KT)
        phi = phi_mem[:, :].rearrange("p (g r n) -> p g r n", g=G, r=2)
        S = scan_mem[:, :].rearrange("p (j b s r g) -> p j b s r g", j=NJ, b=2, s=SEG, r=2)
        phiT = scan_mem[:, 0:2048].rearrange("p (b g r t q) -> p b g r t q", b=2, g=4, r=2, t=L)
        vt = scan_mem[:, 2048:4096].rearrange("p (i n) -> p i n", i=4)
        xc = early[:, :].rearrange("p (i d) -> p i d", i=4)
        u_sb = early[:, 0:2048].rearrange("p (g t q) -> p g t q", g=G, t=4)
        neg_c = bc_mem[:, 0:2, :]
        b_blk = early[:, 2048:4096].rearrange("p (r g n) -> p r g n", r=2, g=G)
        raw = early[:, 0:1280].rearrange("p (t n) -> p t n", t=2)
        rot_a = early[:, 1280:1920]
        prob = early[:, 0:2048].rearrange("p (i n) -> p i n", i=4)
        ga = early[:, 2048:3072].rearrange("p (i t) -> p i t", i=4)
        gs = early[:, 3072:4096].rearrange("p (i t) -> p i t", i=4)
        m_ada = V[:, :, :].rearrange("p a b -> p (a b)")[:, 0:512].rearrange("p (b n) -> p b n", b=2)
        w8 = pw
        qT = qT_mem[:, :].rearrange("p (h t) -> p h t", h=NH)
        merged = phi_mem[:, 0:2048].rearrange("p (k t) -> p k t", k=KT)
        hprev = phi_mem[:, 2048:4096].rearrange("p (c r g) -> p c r g", c=NC, r=2)
        PT = phi_mem[:, 4096:8192].rearrange("p (b h k t) -> p b h k t", b=2, h=2, k=KEYT)
        pool_t = pool_mem[:, 0:1024].rearrange("p (i n) -> p i n", i=2)
        m_rows = pool_mem[:, :].rearrange("p (g n) -> p g n", g=8)
        gate_m = bc_mem[:, 0:2, :].rearrange("p a b -> p (a b)")
        post_b = bc_mem[:, 2:4, :].rearrange("p a b -> p (a b)")
        y_sb = hT_mem[:, 0:1024].rearrange("p (t g q) -> p t g q", g=8, t=L)
        yT = hT_mem[:, 1024:2048].rearrange("p (j t c) -> p j t c", j=4, t=L)
        gpost = hT_mem[:, 2048:3072]
        sig = hT_mem[:, 3072:4096].rearrange("p (i t c) -> p i t c", i=4, t=L)
        e_phi = kT[:, :].rearrange("p (t r g) -> p t r g", t=L, r=2)
        prod = bc_mem[:, 0:2, :].rearrange("p c (a g) -> p (c a) g", g=G)
        qsum = kT[:, :].rearrange("p (a g) -> p a g", g=G)
        brow = scan_mem[:, 2048:3072]
        rot_b = scan_mem[:, 3072:3712]
        o_sb = scan_mem[:, 0:2048].rearrange("p (i d) -> p i d", i=2)
        a4 = sb("a4", 4, G)
        a64 = sb("a64", 4, G)
        carry = small[:, 0:4 * SEG - 4, :].rearrange("p (m r) g -> p m r g", r=2)
        skip = sb("skip", 8, SP_)
        sq_junk = sb("sq_junk", HD)
        sq_out = early[:, 0:512]

        slot_loaded = [sem(f"slot_loaded{s}") for s in range(SLOTS)]
        bank_filled = [sem(f"bank_filled{b}") for b in range(8)]
        bank_drained = [sem(f"bank_drained{b}") for b in range(8)]
        first_loaded = sem("first_loaded")
        ident_loaded = sem("ident_loaded")
        xc_loaded = [sem(f"xc_loaded{i}") for i in range(4)]
        bc_loaded = sem("bc_loaded")
        misc_loaded = sem("misc_loaded")
        post_loaded = sem("post_loaded")
        brow_loaded = sem("brow_loaded")
        silu_zeroed = sem("silu_zeroed")
        silu_ready = sem("silu_ready")
        dt_ready = sem("dt_ready")
        damp_ready = sem("damp_ready")
        mag_ready = sem("mag_ready")
        angle_ready = sem("angle_ready")
        trig_ready = sem("trig_ready")
        ssx_ready = sem("ssx_ready")
        rstdx_ready = sem("rstdx_ready")
        xn_ready = sem("xn_ready")
        h_ready = sem("h_ready")
        phiT_ready = sem("phiT_ready")
        epsi_ready = sem("epsi_ready")
        pool_consts = sem("pool_consts")
        psi_ready = sem("psi_ready")
        bblk_ready = sem("bblk_ready")
        skip_ready = sem("skip_ready")
        rows_written = sem("rows_written")
        ssqk_ready = sem("ssqk_ready")
        rstdqk_ready = sem("rstdqk_ready")
        w8_ready = sem("w8_ready")
        scan_step = sem("scan_step")
        carry_step = sem("carry_step")
        hprev_ready = sem("hprev_ready")
        qT_zeroed = sem("qT_zeroed")
        rot_ready = sem("rot_ready")
        max_ready = sem("max_ready")
        prob_ready = sem("prob_ready")
        merged_ssm = sem("merged_ssm")
        sig_ready = sem("sig_ready")
        sso_ready = sem("sso_ready")
        sso_sum = sem("sso_sum")
        rstdo_ready = sem("rstdo_ready")
        o_ready = sem("o_ready")
        out_written = sem("out_written")
        dve_step = sem("dve_step")
        act_step = sem("act_step")
        pool_step = sem("pool_step")

        def filled(eng, key):
            bank, use = RESULTS[key]
            eng.wait_ge(bank_filled[bank], use)
            return bank

        def drained(eng, key):
            bank, use = RESULTS[key]
            eng.wait_ge(bank_drained[bank], use)

        def block_of(key):
            return ring[:, PLACE[key] % SLOTS, :]

        def loaded(eng, key):
            n = PLACE[key]
            eng.wait_ge(slot_loaded[n % SLOTS], LOADS[key])

        LOADS = {}
        per_slot = [0] * SLOTS
        for n, key in enumerate(STREAM):
            per_slot[n % SLOTS] += 16 * (L if key[0] == "T" else 1)
            LOADS[key] = per_slot[n % SLOTS]

        block = stack.enter_context(nc.Block())

        @block.sync
        def _(sp):
            def cols(w, c0):
                return w.rearrange("(k p) n -> p k n", p=P)[:, :, c0:c0 + BW]

            sources = {"ada": (w_ada, 0), "u": (w_in, U0), "kv": (w_in, KV0), "q": (w_in, Q0),
                       "ga": (w_in, GA0), "gs": (w_in, GS0), "out": (w_out, 0)}
            sp.dma_start(first[:, :], first_in).then_inc(first_loaded, 16)
            sp.dma_start(ident[:, :], ident_in).then_inc(ident_loaded, 16)
            for i in range(4):
                src = (ctx_in, x)[i // 2]
                sp.dma_start(xc[:, i, :], src[(i % 2) * P:(i % 2 + 1) * P, :]).then_inc(xc_loaded[i], 16)
            for n, key in enumerate(STREAM):
                kind, b = key
                if n == 2:
                    sp.dma_start(bc_mem[:, :, :], bc_in).then_inc(bc_loaded, 16)
                if n >= SLOTS:
                    filled(sp, last_reader(n - SLOTS))
                dst = ring[:, n % SLOTS, :]
                done = slot_loaded[n % SLOTS]
                if kind in sources:
                    w, c0 = sources[kind]
                    sp.dma_start(dst.rearrange("p (k n) -> p k n", k=KT), cols(w, c0 + b * BW)).then_inc(done, 16)
                elif kind == "glu":
                    sp.dma_start(dst.rearrange("p (k n) -> p k n", k=4),
                                 w_glu.rearrange("(k p) n -> p k n", p=P)).then_inc(done, 16)
                elif kind == "x":
                    sp.dma_start(dst.rearrange("p (k n) -> p k n", k=2),
                                 x.rearrange("(k p) n -> p k n", p=P)).then_inc(done, 16)
                else:
                    if b == 0:
                        sp.wait_ge(rows_written, 16 * 12)
                    for t in range(L):
                        src = rows.rearrange("g q n -> q g n")[:, b * 16:b * 16 + 16, (L - 1 - t) * SP_:(2 * L - 1 - t) * SP_]
                        sp.dma_start(dst.rearrange("p (g n) -> p g n", g=16)[t * SP_:(t + 1) * SP_],
                                     src).then_inc(done, 16)
            for t in range(2):
                sp.wait_ge(o_ready, 2 * (t + 1))
                sp.dma_start(out[t * P:(t + 1) * P, :], o_sb[:, t, :]).then_inc(out_written, 16)
            sp.wait_ge(out_written, 32)

        @block.gpsimd
        def _(pool):
            steps = [0]

            def step(ins):
                steps[0] += 1
                ins.then_inc(pool_step, 1)
                return steps[0]

            pool.memset(silu_c[:, :, :], 0.0).then_inc(silu_zeroed, 1)
            pool.memset(mhalf[:, :], -0.5).then_inc(pool_consts, 1)
            pool.memset(bh[:, :, GW:GW + SP_], 0.0).then_inc(pool_consts, 1)
            pool.memset(pw[:, 0, 0, :], 1.0).then_inc(pool_consts, 1)
            pool.memset(pw[:, 0, 1, :], 0.0).then_inc(pool_consts, 1)

            pool.memset(qT[:, :, :], 0.0).then_inc(qT_zeroed, 1)

            def rsqrt(n0, n1, ready, count):
                s = step(pool.tensor_scalar(rstd[:, n0:n1], ssq[:, n0:n1], 1.0 / count, EPS, ALU.mult, ALU.add))
                pool.wait_ge(pool_step, s)
                pool.tensor_tensor(rstd[:, n0:n1], rstd[:, n0:n1], mhalf[:, 0:n1 - n0], ALU.pow).then_inc(ready, 1)

            pool.wait_ge(pool_consts, 4)
            for half in range(2):
                pool.wait_ge(ssx_ready, 2 * half + 2)
                rsqrt(2 * half, 2 * half + 2, rstdx_ready, D)

            pool.wait_ge(bc_loaded, 16)
            pool.wait_ge(epsi_ready, 2)
            s = step(pool.tensor_scalar(neg_c[:, :, :], bc_mem[:, 2:4, :], -1.0, 0.0, ALU.mult, ALU.add))
            pool.wait_ge(pool_step, s)

            def cmat(ap, g0):
                return bcast(ap[:, g0 * SP_:(g0 + 4) * SP_].rearrange("p (g q) -> p g q", g=4), 2, L)

            def power(r, g0):
                return bcast(e_psi[:, :, r, g0:g0 + 4].rearrange("p t g -> p g t"), 3, SP_)

            def spread_b():
                filled(pool, ("xT", KT - 1))
                s = step(pool.memset(b_blk[:, :, :, :], 0.0))
                pool.wait_ge(pool_step, s)
                for r in range(2):
                    for d in range(2):
                        pool.tensor_copy(b_blk[d * 64:(d + 1) * 64, r, :, d * SP_:(d + 1) * SP_],
                                         bh[d * 64:(d + 1) * 64, r, 0:GW].rearrange("p (g q) -> p g q", g=G))\
                            .then_inc(bblk_ready, 1)
                        pool.wait_ge(bblk_ready, 2 * r + d + 1)

            added = [0, 0]
            for g0 in range(0, G, 4):
                if g0 == 12:
                    spread_b()
                out_ = [psi[:, r, g0:g0 + 4, 1:TAPS, :] for r in range(2)]
                tmp = [pool_t[:, r, :].rearrange("p (g t q) -> p g t q", g=4, t=L) for r in range(2)]
                made = []
                for r, (c_a, c_b) in enumerate(((bc_mem[:, 2, :], neg_c[:, 1, :]), (neg_c[:, 1, :], neg_c[:, 0, :]))):
                    step(pool.tensor_tensor(out_[r], power(0, g0), cmat(c_a, g0), ALU.mult))
                    if added[r]:
                        pool.wait_ge(pool_step, added[r])
                    made.append(step(pool.tensor_tensor(tmp[r], power(1, g0), cmat(c_b, g0), ALU.mult)))
                for r in range(2):
                    pool.wait_ge(pool_step, made[r])
                    added[r] = step(pool.tensor_tensor(out_[r], out_[r], tmp[r], ALU.add))
            step(pool.tensor_copy(psi[:, 0, :, 0, :], bc_mem[:, 2, :].rearrange("p (g q) -> p g q", g=G)))
            pool.wait_ge(pool_step, steps[0])
            pool.tensor_copy(psi[:, 1, :, 0, :], neg_c[:, 1, :].rearrange("p (g q) -> p g q", g=G)).then_inc(psi_ready, 1)
            pool.wait_ge(psi_ready, 1)
            pool.dma_start(post_b, bass.AP(post.tensor, post.offset, [[0, P], [1, D]])).then_inc(post_loaded, 16)
            pool.wait_ge(misc_loaded, 16 * MISC)
            pool.tensor_tensor(skip[:, :, :], bcast(dcol[:, :], 2, SP_), bcast(id16[:, :], 1, 8), ALU.mult)\
                .then_inc(skip_ready, 1)

            pool.wait_ge(ssqk_ready, 4)
            rsqrt(4, 28, rstdqk_ready, HD)
            for key in (("M", 0), ("M", 1), ("M0", 0)):
                drained(pool, key)
            for j in range(4):
                for p0, c0, c1, r0 in ((0, 0, SP_, L - 1), (0, SP_, L * SP_, L), (SP_, 2 * SP_, TAPS * SP_, 0)):
                    dst = rows.rearrange("g q n -> q g n")[:, j * 8:j * 8 + 8, r0 * SP_:r0 * SP_ + c1 - c0]
                    pool.dma_start(dst, m_rows[32 * j + p0:32 * j + p0 + SP_, :, c0:c1]).then_inc(rows_written, 16)
            pool.wait_ge(hprev_ready, 8)
            pool.dma_start(brow[0:1, :], b_ada_g).then_inc(brow_loaded, 16)
            for t in range(2):
                pool.wait_ge(sso_sum, t + 1)
                rsqrt(36 + t, 37 + t, rstdo_ready, D)

        @block.scalar
        def _(act):
            def load(dst, src, s):
                act.dma_start(dst, src).then_inc(s, 16)

            load(tables[:, :], tables_in, misc_loaded)
            load(gains[:, :, :], bass.AP(qk_norm.tensor, qk_norm.offset, [[0, P], [HD, 2], [1, HD]]), misc_loaded)

            act.wait_ge(first_loaded, 16)
            act.wait_ge(silu_zeroed, 1)
            act.activation(silu_c[:, :, 0:2].rearrange("p k v -> p v k"), ccb[:, :, :], ACT.Silu).then_inc(silu_ready, 1)
            act.activation(small[:, 3, :], lam[:, 2, :], ACT.Exp).then_inc(dt_ready, 1)
            act.wait_ge(damp_ready, 1)
            act.activation(small[:, 6, :], small[:, 4, :], ACT.Exp).then_inc(mag_ready, 1)
            act.wait_ge(angle_ready, 2)
            act.activation(small[:, 10:12, :], small[:, 8:10, :], ACT.Sin).then_inc(trig_ready, 1)
            for i in range(4):
                act.wait_ge(xc_loaded[i], 16)
                if i:
                    act.wait_ge(ssx_ready, i)
                act.activation(phi_mem[:, 0:1024], xc[:, i, :], ACT.Square, accum_out=ssq[:, i:i + 1]).then_inc(ssx_ready, 1)

            def copy_xT(k):
                bank = filled(act, ("xT", k))
                act.activation(hT[:, k, :], ps[:, bank, :], ACT.Copy).then_inc(bank_drained[bank], 1)

            def copy_ada(b):
                bank = filled(act, ("ada", b))
                if b >= 2:
                    act.wait_ge(bank_filled[4], RESULTS[("mT", b - 2)][1])
                act.activation(m_ada[:, b % 2, :], ps[:, bank, 0:BW], ACT.Copy).then_inc(bank_drained[bank], 1)

            def copy_phi(n):
                for h in range(2):
                    bank = filled(act, ("phi", n, h))
                    act.activation(phi[:, 4 * n + 2 * h:4 * n + 2 * h + 2, :, :].rearrange("p g r n -> p (g r n)"),
                                   ps[:, bank, :], ACT.Copy).then_inc(bank_drained[bank], 1)

            act.wait_ge(ssx_ready, 4)
            copy_ada(0)
            for k in range(4):
                copy_xT(k)
            copy_ada(1)
            for k in range(4, 8):
                copy_xT(k)
            for b in range(2, 8):
                copy_ada(b)
                if b in (3, 5):
                    copy_phi((b - 3) // 2)
            for n in range(8):
                bank = filled(act, ("u", n))
                act.activation(u_sb[:, (n // 4) * 16:(n // 4 + 1) * 16, n % 4, :],
                               ps[:, bank, 0:BW].rearrange("p (g q) -> p g q", g=16), ACT.Copy)\
                    .then_inc(bank_drained[bank], 1)
                if n < 6:
                    copy_phi(n + 2)
            for n in range(8):
                bank = filled(act, ("UT", n))
                v = ps[0:64, bank, :].rearrange("p (g c t) -> p t g c", g=4, t=2)
                act.activation(U[0:64, 4 * n:4 * n + 4, :], v[:, 0], ACT.Copy)
                act.activation(U[64:128, 4 * n:4 * n + 4, :], v[:, 1], ACT.Copy).then_inc(bank_drained[bank], 1)
            act.wait_ge(w8_ready, 1)
            for n in range(8):
                bank = filled(act, ("S", n))
                r, g0 = n // 4, (n % 4) * 8
                act.activation(S[:, :, :, :, r, g0:g0 + 8].rearrange("p j b s g -> p g (b s) j"),
                               ps[:, bank, :].rearrange("p (g s j) -> p g s j", g=8, j=NJ), ACT.Copy)\
                    .then_inc(bank_drained[bank], 1)

            chain = [0]

            def act_chain(ins):
                chain[0] += 1
                ins.then_inc(act_step, 1)
                act.wait_ge(act_step, chain[0])

            for n in range(4):
                bank = filled(act, ("kv", n))
                dst = kc_raw[:, n, :] if n < 2 else raw[:, n - 2, 512:640]
                act_chain(act.activation(dst, ps[:, bank, 0:P], ACT.Copy))
                act.activation(V[:, n, :], ps[:, bank, P:2 * P], ACT.Copy).then_inc(bank_drained[bank], 1)
            for t in range(2):
                bank = filled(act, ("q", t))
                act.activation(raw[:, t, 0:512], ps[:, bank, :], ACT.Copy).then_inc(bank_drained[bank], 1)
            for t in range(2):
                drained(act, ("q", t))
                for h in range(10):
                    act_chain(act.activation(sq_junk[:, :], raw[:, t, h * HD:(h + 1) * HD], ACT.Square,
                                             accum_out=ssq[:, 4 + 10 * t + h:5 + 10 * t + h]))
                act.activation(sq_junk[:, :], kc_raw[:, t, 0:HD], ACT.Square,
                               accum_out=ssq[:, 24 + 2 * t:25 + 2 * t]).then_inc(ssqk_ready, 1)
                act.wait_ge(ssqk_ready, 2 * t + 1)
                act.activation(sq_junk[:, :], kc_raw[:, t, HD:2 * HD], ACT.Square,
                               accum_out=ssq[:, 25 + 2 * t:26 + 2 * t]).then_inc(ssqk_ready, 1)
                act.wait_ge(ssqk_ready, 2 * t + 2)

            for h in range(2):
                bank = filled(act, ("M", h))
                act.activation(m_rows[:, 4 * h:4 * h + 4, SP_:TAPS * SP_],
                               ps[:, bank, :].rearrange("p (g n) -> p g n", g=4), ACT.Copy).then_inc(bank_drained[bank], 1)
            for n in range(4):
                bank = filled(act, ("ga", n))
                act.activation(ga[:, n, :], ps[:, bank, 0:S_LAT], ACT.Silu).then_inc(bank_drained[bank], 1)
            for n in range(4):
                bank = filled(act, ("gs", n))
                act.activation(gs[:, n, :], ps[:, bank, 0:S_LAT], ACT.Silu).then_inc(bank_drained[bank], 1)
            act.wait_ge(carry_step, 3 * (2 * SEG - 2))
            for n in range(4):
                bank = filled(act, ("gate", n))
                act.activation(gate_m[:, n * BW:(n + 1) * BW], ps[:, bank, 0:BW], ACT.Copy).then_inc(bank_drained[bank], 1)
            bank = filled(act, ("kT", 0))
            act.activation(kT[:, :], ps[:, bank, :], ACT.Copy).then_inc(bank_drained[bank], 1)
            act.wait_ge(qT_zeroed, 1)
            for t in range(2):
                bank = filled(act, ("qT", t))
                for half in range(2):
                    rows_ = slice(64 * half, 64 * half + 64)
                    ins = act.activation(qT[rows_, 4 * half:4 * half + 4, t * P:(t + 1) * P],
                                         ps[rows_, bank, :].rearrange("p (h t) -> p h t", h=4), ACT.Copy)
                    if half == 0:
                        act_chain(ins)
                    else:
                        ins.then_inc(bank_drained[bank], 1)

            def copy_pt(n):
                bank = filled(act, ("pt", n))
                h, t = n // 2, n % 2
                if h >= 4:
                    act.wait_ge(bank_filled[7], RESULTS[("o", h // 2 - 2)][1])
                act.activation(PT[:, (h // 2) % 2, h % 2, :, t * P:(t + 1) * P],
                               ps[:, bank, :].rearrange("p (k t) -> p k t", k=KEYT), ACT.Copy).then_inc(bank_drained[bank], 1)

            for s in range(NH + 1):
                if s < NH:
                    for t in range(2):
                        n = 2 * s + t
                        bank = filled(act, ("sc", n))
                        act.wait_ge(max_ready, n + 1)
                        if n == 0:
                            filled(act, ("qT", 1))
                        if n >= 4:
                            filled(act, ("pt", n - 4))
                        act.activation(prob[:, n % 4, :], ps[:, bank, :], ACT.Exp, bias=nmax[:, n:n + 1],
                                       accum_out=rsum[:, n:n + 1]).then_inc(bank_drained[bank], 1)
                if s >= 1:
                    copy_pt(2 * s - 2)
                    copy_pt(2 * s - 1)
            for h in range(2):
                bank = filled(act, ("y", h))
                act.activation(y_sb[:, :, 4 * h:4 * h + 4, :].rearrange("p t g q -> p g t q"), ps[:, bank, :].rearrange("p (g t q) -> p g t q", g=4, t=L),
                               ACT.Gelu_apprx_tanh).then_inc(bank_drained[bank], 1)
            for n in range(4):
                bank = filled(act, ("glu", n))
                act.activation(sig[:, n], ps[:, bank, 0:S_LAT].rearrange("p (t c) -> p t c", t=L), ACT.Sigmoid,
                               bias=bglu[:, n:n + 1]).then_inc(sig_ready, 1)
            for n in range(4):
                bank = filled(act, ("out", n))
                if n:
                    act.wait_ge(sso_ready, n)
                act.activation(sq_out[:, :], ps[:, bank, :], ACT.Square, accum_out=ssq[:, 28 + n:29 + n]).then_inc(sso_ready, 1)

        @block.vector
        def _(dve):
            steps = [0]

            def step(ins):
                steps[0] += 1
                ins.then_inc(dve_step, 1)
                return steps[0]

            def settle(s=None):
                dve.wait_ge(dve_step, steps[0] if s is None else s)

            tt = dve.tensor_tensor
            ts = dve.tensor_scalar
            stt = dve.scalar_tensor_tensor

            def cmul(o_re, o_im, a_re, a_im, b_re_, b_im_, t):
                step(tt(t[0], a_re, b_re_, ALU.mult))
                s1 = step(tt(t[1], a_im, b_im_, ALU.mult))
                step(tt(t[2], a_re, b_im_, ALU.mult))
                s2 = step(tt(t[3], a_im, b_re_, ALU.mult))
                settle(s1)
                step(tt(o_re, t[0], t[1], ALU.subtract))
                settle(s2)
                return step(tt(o_im, t[2], t[3], ALU.add))

            sm = lambda i: small[:, i, :]
            lr, li, dt = lam[:, 0, :], lam[:, 1, :], sm(3)
            dve.wait_ge(first_loaded, 16)
            dve.wait_ge(dt_ready, 1)
            tt(sm(4), dt, lr, ALU.mult).then_inc(damp_ready, 1)
            step(tt(sm(5), dt, li, ALU.mult))
            settle()
            step(ts(sm(7), sm(5), INV_2PI, ROUND, ALU.mult, ALU.add))
            settle()
            step(ts(sm(7), sm(7), ROUND, None, ALU.subtract))
            settle()
            for c in (C1, C2, C3):
                step(stt(sm(5), sm(7), -c, sm(5), ALU.mult, ALU.add))
                settle()
            ts(sm(8), sm(5), PI32, -PI32, ALU.min, ALU.max).then_inc(angle_ready, 1)
            dve.wait_ge(angle_ready, 1)
            step(stt(sm(7), sm(8), -1.0, sm(8), ALU.mult, ALU.max))
            settle()
            ts(sm(9), sm(7), -1.0, TWO_PI / 4, ALU.mult, ALU.add).then_inc(angle_ready, 1)
            step(tt(sm(12), lr, lr, ALU.mult))
            step(tt(sm(13), li, li, ALU.mult))
            settle()
            step(tt(sm(12), sm(12), sm(13), ALU.add))
            settle()
            step(dve.reciprocal(sm(14), sm(12)))
            dve.wait_ge(trig_ready, 1)
            dve.wait_ge(mag_ready, 1)
            step(tt(pw[:, 1, 0, :], sm(6), sm(11), ALU.mult))
            step(tt(pw[:, 1, 1, :], sm(6), sm(10), ALU.mult))
            settle()
            step(ts(sm(15), pw[:, 1, 0, :], -1.0, None, ALU.add))
            settle()
            nr, ni = sm(15), pw[:, 1, 1, :]
            step(tt(sm(16), nr, lr, ALU.mult))
            step(tt(sm(17), ni, li, ALU.mult))
            step(tt(sm(18), ni, lr, ALU.mult))
            step(tt(sm(19), nr, li, ALU.mult))
            settle()
            step(tt(sm(16), sm(16), sm(17), ALU.add))
            step(tt(sm(18), sm(18), sm(19), ALU.subtract))
            settle()
            step(tt(sm(20), sm(16), sm(14), ALU.mult))
            step(tt(sm(21), sm(18), sm(14), ALU.mult))
            settle()
            for i in range(4):
                dve.wait_ge(rstdx_ready, i // 2 + 1)
                ts(xc[:, i, :], xc[:, i, :], rstd[:, i:i + 1], None, ALU.mult).then_inc(xn_ready, 1)

            tmp = [vt[:, i, :].rearrange("p (g q) -> p g q", g=G) for i in range(4)]
            dve.wait_ge(bc_loaded, 16)

            def gq(ap):
                return ap.rearrange("p (g q) -> p g q", g=G)

            cmul(gq(bh[:, 0, 0:GW]), gq(bh[:, 1, 0:GW]), bcast(sm(20), 2, SP_), bcast(sm(21), 2, SP_),
                 gq(bc_mem[:, 0, :]), gq(bc_mem[:, 1, :]), tmp)
            settle()
            dve.wait_ge(pool_consts, 4)

            def double(tab, n):
                m = min(n, tab.shape[1] - 1 - n)
                t4 = [vt[:, i, 0:m * G].rearrange("p (e g) -> p e g", g=G) for i in range(4)]
                cmul(tab[:, n + 1:n + 1 + m, 0, :], tab[:, n + 1:n + 1 + m, 1, :], tab[:, 1:1 + m, 0, :], tab[:, 1:1 + m, 1, :],
                     bcast(tab[:, n, 0, :], 1, m), bcast(tab[:, n, 1, :], 1, m), t4)
                settle()

            for n in (1, 2, 4):
                double(pw, n)
            dve.tensor_copy(e_psi[0:64], pw[0:64, 1:9]).then_inc(epsi_ready, 1)
            dve.tensor_copy(e_psi[64:128], pw[64:128, 8:0:-1]).then_inc(epsi_ready, 1)
            step(dve.tensor_copy(e_phi[0:64], pw[0:64, 7::-1]))
            step(dve.tensor_copy(e_phi[64:128], pw[64:128, 0:8]))
            settle()

            def phi_batch(n):
                g0 = 4 * n
                er = bcast(e_phi[:, :, 0, g0:g0 + 4].rearrange("p t g -> p g t"), 3, SP_)
                ei = bcast(e_phi[:, :, 1, g0:g0 + 4].rearrange("p t g -> p g t"), 3, SP_)
                br = bcast(gq(bh[:, 0, 0:GW])[:, g0:g0 + 4, :], 2, L)
                bi = bcast(gq(bh[:, 1, 0:GW])[:, g0:g0 + 4, :], 2, L)
                o = phiT[:, n % 2]
                t = [vt[:, i, :].rearrange("p (g t q) -> p g t q", g=4, t=L) for i in range(4)]
                settle()
                if n >= 2:
                    filled(dve, ("phi", n - 2, 1))
                step(tt(t[0], er, br, ALU.mult))
                s1 = step(tt(t[1], ei, bi, ALU.mult))
                step(tt(t[2], er, bi, ALU.mult))
                s2 = step(tt(t[3], ei, br, ALU.mult))
                settle(s1)
                tt(o[:, :, 0], t[0], t[1], ALU.subtract).then_inc(phiT_ready, 1)
                settle(s2)
                tt(o[:, :, 1], t[2], t[3], ALU.add).then_inc(phiT_ready, 1)
                dve.wait_ge(phiT_ready, 2 * n + 2)

            def ada_reduce(n):
                b = STREAM[n][1]
                bank = filled(dve, ("mT", n))
                dve.tensor_reduce(red[:, b, :, :], ps[:, bank, 0:2 * P].rearrange("p (f j v) -> p f v j", f=2, j=4)[:, :, 0:2, :],
                                  AX_X, ALU.add).then_inc(bank_drained[bank], 1)

            def modulate(pair):
                bank, use = RESULTS[("mT", 2 * pair + 1)]
                dve.wait_ge(bank_drained[bank], use)
                f = slice(2 * pair, 2 * pair + 2)
                step(tt(mshift[:, f, :], red[:, pair, :, :], bcast(bias_ada[:, f], 2, 2), ALU.add))
                step(tt(mgain[:, f, :], red[:, 4 + pair, :, :],
                        bcast(bias_ada[:, 8 + 2 * pair:10 + 2 * pair], 2, 2), ALU.add))
                settle()
                step(stt(mgain[:, f, :], mgain[:, f, :], 1.0, bcast(pre[:, f], 2, 2), ALU.add, ALU.mult))
                settle()
                for k in (2 * pair, 2 * pair + 1):
                    drained(dve, ("xT", k))
                    for v, c0 in ((1, 0), (0, S_CTX)):
                        o = hT[:, k, c0:c0 + 256]
                        ts(o, o, mgain[:, k, v:v + 1], mshift[:, k, v:v + 1], ALU.mult, ALU.add).then_inc(h_ready, 1)

            for pair in range(4):
                ada_reduce(2 * pair)
                ada_reduce(2 * pair + 1)
                modulate(pair)
                if pair < 2:
                    phi_batch(pair)
            for n in range(2, 8):
                phi_batch(n)

            step(dve.tensor_copy(w8[:, 1, :, :], pw[:, 8, :, :]))
            settle()
            def as_matrix(m, re, im):
                step(dve.tensor_copy(m[:, 0, :], re))
                step(dve.tensor_copy(m[:, 2, :], im))
                step(ts(m[:, 1, :], im, -1.0, None, ALU.mult))
                settle()

            as_matrix(a4, w8[:, 1, 0, :], w8[:, 1, 1, :])
            step(dve.tensor_copy(a4[:, 3, :], w8[:, 1, 0, :]))
            for n in (1, 2, 4):
                double(w8, n)
            as_matrix(a64, w8[:, NJ, 0, :], w8[:, NJ, 1, :])
            dve.tensor_copy(a64[:, 3, :], w8[:, NJ, 0, :]).then_inc(w8_ready, 1)
            dve.wait_ge(w8_ready, 1)

            for n in range(8):
                drained(dve, ("S", n))
            dve.wait_ge(psi_ready, 1)
            nb = 2 * SEG

            def chunk(mat, b, prev, here, out_, signal, done):
                p_, q_ = prod[:, 0:4 * b, :], qsum[:, 0:2 * b, :]
                matv = bcast(mat[:, :, :].rearrange("p (o k) g -> p o (k g)", o=2), 1, b)
                pk = p_.rearrange("p (b k) g -> p k b g", k=2)
                tt(p_.rearrange("p (b o k) g -> p b o (k g)", b=b, o=2), matv,
                   bcast(prev.rearrange("p (b n) -> p b n", b=b), 2, 2), ALU.mult).then_inc(signal, 1)
                dve.wait_ge(signal, done + 1)
                tt(q_, pk[:, 0], pk[:, 1], ALU.add).then_inc(signal, 1)
                dve.wait_ge(signal, done + 2)
                tt(out_, here, q_.rearrange("p b g -> p (b g)"), ALU.add).then_inc(signal, 1)

            chunk(a4, nb, scan_mem[:, 0:ROW], scan_mem[:, ROW:2 * ROW], scan_mem[:, ROW:2 * ROW], scan_step, 0)
            with dve.Fori(1, NJ - 1) as j:
                dve.wait_ge(scan_step, j * 3)
                here = scan_mem[:, bass.ds(j * ROW + ROW, ROW)]
                chunk(a4, nb, scan_mem[:, bass.ds(j * ROW, ROW)], here, here, scan_step, j * 3)
            dve.wait_ge(scan_step, 3 * (NJ - 1))
            flat = lambda ap: ap.rearrange("p r g -> p (r g)")
            before = flat(S[:, NJ - 1, 0, 0])
            for m in range(2 * SEG - 2):
                b, sg = (m + 1) // SEG, (m + 1) % SEG
                if m:
                    dve.wait_ge(carry_step, 3 * m)
                chunk(a64, 1, before, flat(S[:, NJ - 1, b, sg]), flat(carry[:, m]), carry_step, 3 * m)
                before = flat(carry[:, m])
            dve.wait_ge(carry_step, 3 * (2 * SEG - 2))
            hr, hi = (bcast(carry[:, SEG - 2:, r, :], 1, NJ) for r in range(2))
            wr, wi = (bcast(w8[:, 0:NJ, r, :], 2, SEG) for r in range(2))
            t1, t2 = S[:, :, 0, :, 0, :], S[:, :, 0, :, 1, :]
            hp = hprev.rearrange("p (s j) r g -> p j s r g", s=SEG)
            for r in range(2):
                a, b = ((hr, hi), (hi, hr))[r]
                step(tt(t1, wr, a, ALU.mult))
                step(tt(t2, wi, b, ALU.mult))
                settle()
                step(tt(t1, t1, t2, ALU.subtract if r == 0 else ALU.add))
                settle()
                for d, j_first, j_rest, order in ((0, 0, slice(1, NJ), slice(None)),
                                                  (1, NJ - 1, slice(NJ - 2, None, -1), slice(None, None, -1))):
                    h = slice(64 * d, 64 * d + 64)
                    dve.tensor_copy(hp[h, j_first, order, r, :], t1[h, 0]).then_inc(hprev_ready, 1)
                    tt(hp[h, j_rest, order, r, :], t1[h, 1:NJ], S[h, 0:NJ - 1, 1, :, r, :], ALU.add).then_inc(hprev_ready, 1)
                dve.wait_ge(hprev_ready, 4 * (r + 1))

            bank = filled(dve, ("M0", 0))
            dve.wait_ge(skip_ready, 1)
            tt(m_rows[:, :, 0:SP_], ps[:, bank, 0:8 * SP_].rearrange("p (g n) -> p g n", g=8), skip[:, :, :], ALU.add)\
                .then_inc(bank_drained[bank], 1)

            dve.wait_ge(misc_loaded, 16 * MISC)
            step(ts(gains[:, 0, :], gains[:, 0, :], float(HD) ** -0.5, None, ALU.mult))
            dve.wait_ge(rstdqk_ready, 1)
            settle()
            for t in range(2):
                k3 = kc_raw[:, t, :].rearrange("p (h d) -> p h d", h=NKV)
                step(tt(k3, k3, bcast(rstd[:, 24 + 2 * t:26 + 2 * t], 2, HD), ALU.mult))
                settle()
                tt(k3, k3, bcast(gains[:, 1, :], 1, NKV), ALU.mult).then_inc(rot_ready, 1)
            for t in range(2):
                h3 = raw[:, t, :].rearrange("p (h d) -> p h d", h=10)
                a3 = rot_a.rearrange("p (h d) -> p h d", h=10)
                step(tt(h3, h3, bcast(rstd[:, 4 + 10 * t:14 + 10 * t], 2, HD), ALU.mult))
                settle()
                step(tt(h3[:, 0:8], h3[:, 0:8], bcast(gains[:, 0, :], 1, 8), ALU.mult))
                step(tt(h3[:, 8:10], h3[:, 8:10], bcast(gains[:, 1, :], 1, 2), ALU.mult))
                settle()
                step(tt(a3, h3, bcast(ropes[:, t, 0, :], 1, 10), ALU.mult))
                h5 = raw[:, t, :].rearrange("p (h s d) -> p s h d", s=2, d=16)
                b5 = rot_b[:, :].rearrange("p (h s d) -> p s h d", s=2, d=16)
                for s_ in range(2):
                    for half in range(2):
                        sin = ropes[:, t, 1, half * 32 + s_ * 16:half * 32 + s_ * 16 + 16]
                        step(tt(b5[:, s_, half::2], h5[:, 1 - s_, half::2], bcast(sin, 1, 10), ALU.mult))
                settle()
                tt(raw[:, t, 0:512].rearrange("p (i half d) -> p half i d", half=2, d=HD),
                   rot_a[:, 0:512].rearrange("p (half i d) -> p half i d", half=2, d=HD),
                   rot_b[:, 0:512].rearrange("p (half i d) -> p half i d", half=2, d=HD), ALU.add).then_inc(rot_ready, 1)
                tt(raw[:, t, 512:640], rot_a[:, 512:640], rot_b[:, 512:640], ALU.add).then_inc(rot_ready, 1)
                dve.wait_ge(rot_ready, 4 + 2 * t)

            def norm(n):
                bank, use = RESULTS[("sc", n)]
                dve.wait_ge(bank_drained[bank], use)
                step(dve.reciprocal(rinv[:, n:n + 1], rsum[:, n:n + 1]))
                settle()
                ts(prob[:, n % 4, :], prob[:, n % 4, :], rinv[:, n:n + 1], None, ALU.mult).then_inc(prob_ready, 1)

            def merge_attn(i):
                bank = filled(dve, ("o", i))
                if i == 0:
                    for n in range(4):
                        drained(dve, ("ga", n))
                tt(merged[:, i, :], ps[:, bank, 0:S_LAT], ga[:, i, :], ALU.mult).then_inc(bank_drained[bank], 1)

            for s in range(NH + 2):
                if s < NH:
                    for t in range(2):
                        n = 2 * s + t
                        bank = filled(dve, ("sc", n))
                        dve.tensor_reduce(nmax[:, n:n + 1], ps[:, bank, :], AX_X, ALU.max, negate=True).then_inc(max_ready, 1)
                    norm(2 * s)
                    norm(2 * s + 1)
                if s >= 3 and s % 2 == 1:
                    merge_attn((s - 3) // 2)

            dve.wait_ge(post_loaded, 16)
            for h in range(2):
                bank = filled(dve, ("gb", h))
                tt(gpost[:, h * 512:(h + 1) * 512], ps[:, bank, :], post_b[:, h * 512:(h + 1) * 512], ALU.mult)\
                    .then_inc(bank_drained[bank], 1)
            for h in range(2):
                bank = filled(dve, ("yT", h))
                dve.tensor_copy(yT[:, :, 4 * h:4 * h + 4, :].rearrange("p j t c -> p t j c"),
                                ps[:, bank, :].rearrange("p (t j c) -> p t j c", t=4, j=4)).then_inc(bank_drained[bank], 1)
            for n in range(4):
                drained(dve, ("gs", n))
            for h in range(2):
                drained(dve, ("yT", h))
            for n in range(4):
                dve.wait_ge(sig_ready, n + 1)
                step(tt(sig[:, n], sig[:, n], yT[:, n], ALU.mult))
                settle()
                tt(merged[:, 4 + n, :].rearrange("p (c t) -> p t c", t=L), sig[:, n],
                   gs[:, n, :].rearrange("p (c t) -> p t c", t=L), ALU.mult).then_inc(merged_ssm, 1)
            loaded(dve, ("x", 0))
            xr = block_of(("x", 0)).rearrange("p (t n) -> p t n", t=2)
            for h in range(2):
                drained(dve, ("gb", h))
            for t in range(2):
                dve.wait_ge(sso_ready, 2 * t + 2)
                tt(ssq[:, 36 + t:37 + t], ssq[:, 28 + 2 * t:29 + 2 * t], ssq[:, 29 + 2 * t:30 + 2 * t], ALU.add).then_inc(sso_sum, 1)
                dve.wait_ge(rstdo_ready, t + 1)
                for h in range(2):
                    bank, _ = RESULTS[("out", 2 * t + h)]
                    c = slice(512 * h, 512 * h + 512)
                    step(stt(o_sb[:, t, c], ps[:, bank, :], rstd[:, 36 + t:37 + t], gpost[:, c], ALU.mult, ALU.mult))
                    settle()
                    tt(o_sb[:, t, c], o_sb[:, t, c], xr[:, t, c], ALU.add).then_inc(o_ready, 1)

        @block.tensor
        def _(pe):
            mm = pe.matmul

            def free(key):
                bank, use = RESULTS[key]
                if use > 1:
                    pe.wait_ge(bank_drained[bank], use - 1)
                return bank

            def fill(ins, bank):
                ins.then_inc(bank_filled[bank], 1)

            def ada(n, key, b):
                bank = free(key)
                loaded(pe, ("ada", b))
                w = block_of(("ada", b)).rearrange("p (k n) -> p k n", k=KT)
                for k in range(KT):
                    j = k % 4
                    last = mm(ps[32 * j:32 * j + 32, bank, 0:BW], silu_c[:, k, :], w[:, k, :], start=k < 4, stop=k >= 4)
                fill(last, bank)

            def turn_ada(n):
                bank = free(("mT", n))
                drained(pe, ("ada", n))
                for f in range(2):
                    last = pe.transpose(ps[:, bank, f * P:(f + 1) * P], m_ada[:, n % 2, f * P:(f + 1) * P], ident[:, :])
                fill(last, bank)

            def turn_x(k):
                bank = free(("xT", k))
                for i in range(4):
                    if k == 0:
                        pe.wait_ge(xn_ready, i + 1)
                    last = pe.transpose(ps[:, bank, i * P:(i + 1) * P], xc[:, i, k * P:(k + 1) * P], ident[:, :])
                fill(last, bank)

            pe.wait_ge(ident_loaded, 16)
            pe.wait_ge(silu_ready, 1)

            def turn_phi(n):
                pe.wait_ge(phiT_ready, 2 * n + 2)
                for h in range(2):
                    bank = free(("phi", n, h))
                    for i in range(4):
                        g, r = 2 * h + i // 2, i % 2
                        last = pe.transpose(ps[:, bank, i * P:(i + 1) * P],
                                            phiT[:, n % 2, g, r].rearrange("p t q -> p (t q)"), ident[:, :])
                    fill(last, bank)

            for n in range(8):
                ada(n, ("ada", n), STREAM[n][1])
                if n < 2:
                    for k in range(4 * n, 4 * n + 4):
                        turn_x(k)
                turn_ada(n)
                if n in (3, 5):
                    turn_phi((n - 3) // 2)

            def project_u(n):
                b, t = n // 4, n % 4
                bank = free(("u", n))
                loaded(pe, ("u", b))
                w = block_of(("u", b)).rearrange("p (k n) -> p k n", k=KT)
                for k in range(KT):
                    if n == 0:
                        pe.wait_ge(h_ready, 4 * (k // 2) + 2 * (k % 2) + 2)
                    last = mm(ps[:, bank, 0:BW], hT[:, k, t::4], w[:, k, :], start=k == 0, stop=k == KT - 1)
                fill(last, bank)

            for n in range(8):
                project_u(n)
                if n < 6:
                    turn_phi(n + 2)
            for n in range(8):
                drained(pe, ("u", n))
            for n in range(8):
                bank = free(("UT", n))
                for i in range(4):
                    g = 4 * n + i
                    last = pe.transpose(ps[0:64, bank, i * P:(i + 1) * P], u_sb[:, g].rearrange("p t q -> p (t q)"), ident[:, :])
                fill(last, bank)
            for n in range(8):
                drained(pe, ("phi", n, 0))
                drained(pe, ("phi", n, 1))
            for n in range(8):
                bank = free(("S", n))
                r, g0 = n // 4, (n % 4) * 8
                for i in range(8):
                    g = g0 + i
                    drained(pe, ("UT", g // 4))
                    ug = U[:, g, :].rearrange("p (b j) -> p b j", b=2)
                    for d in range(2):
                        last = mm(ps[64 * d:64 * d + 64, bank, i * 64:(i + 1) * 64].rearrange("p (b j) -> p b j", b=2),
                                  phi[:, g, r, 64 * d:64 * d + 64], ug if d == 0 else ug[:, :, ::-1], start=True, stop=True)
                fill(last, bank)

            def project(key, wkey, cols, c0, off=0, done=True):
                bank, use = RESULTS[key]
                if off == 0:
                    free(key)
                loaded(pe, wkey)
                w = block_of(wkey).rearrange("p (k n) -> p k n", k=KT)
                for k in range(KT):
                    last = mm(ps[:, bank, off:off + BW], hT[:, k, c0:c0 + P], w[:, k, :], start=k == 0, stop=k == KT - 1)
                if done:
                    fill(last, bank)

            def project_T(key, wkey, c0):
                bank = free(key)
                loaded(pe, wkey)
                w = block_of(wkey).rearrange("p (k n) -> p k n", k=KT)
                for k in range(KT):
                    last = mm(ps[:, bank, 0:S_LAT], w[:, k, c0:c0 + P], hT[:, k, S_CTX:TOK], start=k == 0, stop=k == KT - 1)
                fill(last, bank)

            for n in range(4):
                project(("kv", n), ("kv", 0), None, n * P)
            for b in range(2):
                for t in range(2):
                    project(("q", t), ("q", b), None, S_CTX + t * P, off=b * BW, done=b == 1)

            pe.wait_ge(bblk_ready, 4)
            pe.wait_ge(psi_ready, 1)
            for h in range(2):
                bank = free(("M", h))
                for i in range(4):
                    for r in range(2):
                        for j in range(4):
                            g = 8 * j + 4 * h + i
                            last = mm(ps[32 * j:32 * j + 32, bank, i * P:(i + 1) * P], b_blk[:, r, g, :],
                                      psi[:, r, g, 1:TAPS, :], start=r == 0, stop=r == 1)
                fill(last, bank)
            bank = free(("M0", 0))
            for i in range(8):
                for r in range(2):
                    for j in range(4):
                        g = 8 * j + i
                        last = mm(ps[32 * j:32 * j + 32, bank, i * SP_:(i + 1) * SP_], bh[:, r, g * SP_:g * SP_ + 32],
                                  psi[:, r, g, 0, :], start=r == 0, stop=r == 1)
            fill(last, bank)

            for n in range(4):
                project_T(("ga", n), ("ga", n // 2), (n % 2) * P)

            for n in range(4):
                project_T(("gs", n), ("gs", n // 2), (n % 2) * P)
            for n in range(4):
                ada(n, ("gate", n), 8 + n)

            bank = free(("kT", 0))
            pe.wait_ge(rot_ready, 2)
            for n in range(4):
                if n == 2:
                    pe.wait_ge(rot_ready, 6)
                src = kc_raw[:, n, :] if n < 2 else raw[:, n - 2, 512:640]
                last = pe.transpose(ps[:, bank, n * P:(n + 1) * P], src, ident[:, :])
            fill(last, bank)
            for t in range(2):
                bank = free(("qT", t))
                for i in range(4):
                    last = pe.transpose(ps[:, bank, i * P:(i + 1) * P], raw[:, t, i * P:(i + 1) * P], ident[:, :])
                fill(last, bank)

            def scores(n):
                h, t = n // 2, n % 2
                bank = free(("sc", n))
                if n == 0:
                    drained(pe, ("kT", 0))
                    drained(pe, ("qT", 0))
                    drained(pe, ("qT", 1))
                fill(mm(ps[:, bank, :], qT[:, h, t * P:(t + 1) * P], kT[:, :], start=True, stop=True), bank)

            def turn_probs(n):
                bank = free(("pt", n))
                pe.wait_ge(prob_ready, n + 1)
                for k in range(KEYT):
                    last = pe.transpose(ps[:, bank, k * P:(k + 1) * P], prob[:, n % 4, k * P:(k + 1) * P], ident[:, :])
                fill(last, bank)

            def attend(i):
                bank = free(("o", i))
                for n in range(4 * i, 4 * i + 4):
                    drained(pe, ("pt", n))
                kv = i // 2
                for k in range(KEYT):
                    for e in range(2):
                        last = mm(ps[64 * e:64 * e + 64, bank, 0:S_LAT], V[:, k, kv * HD:(kv + 1) * HD], PT[:, i % 2, e, k, :],
                                  start=k == 0, stop=k == KEYT - 1)
                fill(last, bank)

            for s in range(NH + 2):
                if s < NH:
                    scores(2 * s)
                    scores(2 * s + 1)
                if 1 <= s <= NH:
                    turn_probs(2 * s - 2)
                    turn_probs(2 * s - 1)
                if s >= 3 and s % 2 == 1:
                    attend((s - 3) // 2)

            for n in range(4):
                drained(pe, ("gate", n))
            pe.wait_ge(misc_loaded, 16 * MISC)
            pe.wait_ge(brow_loaded, 16)
            for h in range(2):
                bank = free(("gb", h))
                c = slice(512 * h, 512 * h + 512)
                mm(ps[:, bank, :], quad[:, :], gate_m[:, c], start=True, stop=False)
                fill(mm(ps[:, bank, :], quad[0:1, :], brow[0:1, c], start=False, stop=True), bank)

            pe.wait_ge(hprev_ready, 8)
            loaded(pe, ("T", 0))
            loaded(pe, ("T", 1))
            for h in range(2):
                bank = free(("y", h))
                for i in range(4):
                    for part in range(3):
                        for j in range(4):
                            g = 8 * j + 4 * h + i
                            if part < 2:
                                a, b = hprev[:, :, part, g], psi[:, part, g, 1:TAPS, :]
                            else:
                                T = block_of(("T", g // 16)).rearrange("p (g n) -> p g n", g=16)
                                a, b = U[:, g, NC:2 * NC], T[:, g % 16, :]
                            last = mm(ps[32 * j:32 * j + 32, bank, i * P:(i + 1) * P], a, b, start=part == 0, stop=part == 2)
                fill(last, bank)
            drained(pe, ("y", 0))
            drained(pe, ("y", 1))
            for h in range(2):
                bank = free(("yT", h))
                for i in range(4):
                    last = pe.transpose(ps[:, bank, i * P:(i + 1) * P], y_sb[:, 4 * h + i].rearrange("p g q -> p (g q)"), ident[:, :])
                fill(last, bank)
            drained(pe, ("yT", 0))
            drained(pe, ("yT", 1))
            loaded(pe, ("glu", 0))
            w = block_of(("glu", 0)).rearrange("p (k n) -> p k n", k=4)
            for n in range(4):
                bank = free(("glu", n))
                for k in range(4):
                    last = mm(ps[:, bank, 0:S_LAT], w[:, k, n * P:(n + 1) * P], yT[:, k].rearrange("p t c -> p (t c)"),
                              start=k == 0, stop=k == 3)
                fill(last, bank)
            for i in range(4):
                drained(pe, ("o", i))
            pe.wait_ge(merged_ssm, 4)
            for b in range(4):
                loaded(pe, ("out", b))
                w = block_of(("out", b)).rearrange("p (k n) -> p k n", k=KT)
                for t in range(2):
                    key = ("out", 2 * t + b // 2)
                    bank = RESULTS[key][0]
                    if b % 2 == 0:
                        free(key)
                    for k in range(KT):
                        last = mm(ps[:, bank, (b % 2) * BW:(b % 2 + 1) * BW], merged[:, k, t * P:(t + 1) * P], w[:, k, :],
                                  start=k == 0, stop=k == KT - 1)
                    if b % 2 == 1:
                        fill(last, bank)


def kernel(x, c, ctx, c_ctx, w_ada, b_ada, pre_norm, post_norm, w_in, q_norm, k_norm,
           ssm_lam_re, ssm_lam_im, ssm_log_dt, ssm_b_re, ssm_b_im, ssm_c_re, ssm_c_im,
           ssm_d, w_glu, b_glu, w_out):
    import numpy as np
    import concourse.bacc as bacc
    from concourse.bass_utils import run_bass_kernel_spmd

    f = np.float32
    x, c, ctx, c_ctx, w_ada, b_ada, pre_norm, post_norm, w_in, q_norm, k_norm = (
        np.asarray(a) for a in (x, c, ctx, c_ctx, w_ada, b_ada, pre_norm, post_norm, w_in, q_norm, k_norm))
    w_glu, b_glu, w_out = (np.asarray(a) for a in (w_glu, b_glu, w_out))

    def states(a):
        a = np.asarray(a)[0]
        return np.moveaxis(a, 2, 1).reshape(P, -1)

    grid_w, freqs = 64, HD // 4
    inv = (f(10000.0) ** (-np.arange(freqs, dtype=f) / f(freqs))).astype(f)
    pos = np.arange(S_LAT)
    ang = np.stack([(pos // grid_w).astype(f)[:, None] * inv, (pos % grid_w).astype(f)[:, None] * inv], 1)
    cos, sin = np.cos(ang).astype(f), np.sin(ang).astype(f)
    rope = np.stack([np.stack([cos, cos], 2).reshape(S_LAT, HD), np.stack([-sin, sin], 2).reshape(S_LAT, HD)], 1)

    d = np.asarray(ssm_d)[0]
    d_t = np.zeros((4, 32, 8), f)
    d_t[:, 0:SP_, :] = np.swapaxes(d.reshape(4, 8, SP_), 1, 2)
    quad = np.zeros((P, P), f)
    quad[::32] = 1.0
    id16 = np.zeros((4, 32, SP_), f)
    id16[:, 0:SP_] = np.eye(SP_, dtype=f)

    lam = [states(ssm_lam_re), states(ssm_lam_im), np.repeat(np.asarray(ssm_log_dt)[0], SSM_N, axis=0)]
    first = {"cc": np.stack([c[0].reshape(KT, P).T, c_ctx.reshape(KT, P).T], 1).reshape(P, -1),
             "bias": b_ada[0, :2 * D].reshape(2 * KT, P).T, "pre": pre_norm[0].reshape(KT, P).T,
             "lam": np.stack(lam, 1).reshape(P, -1)}
    tables = {"quad": quad, "id16": id16.reshape(P, SP_), "d": d_t.reshape(P, 8), "bglu": b_glu[0].reshape(4, P).T,
              "rope": np.moveaxis(rope.reshape(2, P, 2, HD), 0, 1).reshape(P, -1)}
    bc = [states(ssm_b_re), states(ssm_b_im),
          states(np.swapaxes(np.asarray(ssm_c_re), 3, 4)), states(np.swapaxes(np.asarray(ssm_c_im), 3, 4))]
    arrays = {
        "x": x[0], "ctx_in": ctx[0], "first_in": np.concatenate([first[n] for n in FIRST], 1),
        "w_ada": w_ada[0], "b_ada_g": b_ada[:, 2 * D:], "post": post_norm[0], "w_in": w_in[0],
        "qk_norm": np.stack([q_norm[0], k_norm[0]]), "bc_in": np.stack(bc, 1),
        "w_glu": w_glu[0], "w_out": w_out[0],
        "ident_in": np.eye(P, dtype=f), "tables_in": np.concatenate([tables[n] for n in TABLES], 1),
    }
    nc = bacc.Bacc("TRN2", target_bir_lowering=False, num_devices=1)
    args = {}
    for name, a in arrays.items():
        arrays[name] = np.ascontiguousarray(a)
        args[name] = nc.dram_tensor(name, arrays[name].shape, F32, kind="ExternalInput").ap()
    args["out"] = nc.dram_tensor("out", (S_LAT, D), F32, kind="ExternalOutput").ap()
    hymba_layer(nc, **args)
    result = run_bass_kernel_spmd(nc, [arrays], core_ids=[0])
    return result.results[0]["out"].reshape(1, S_LAT, D)
```

```python
from contextlib import ExitStack

import concourse.bass as bass
from concourse import mybir

ALU = mybir.AluOpType
ACT = mybir.ActivationFunctionType
F32 = mybir.dt.float32
F32R = mybir.dt.float32r
AX_X = mybir.AxisListType.X

P = 128
D = 1024
KT = D // P
S_LAT = 256
S_CTX = 256
TOK = S_CTX + S_LAT
HD = 64
NH = 8
NKV = 2
KEYT = TOK // P
EPS = 1e-6
G = 32
SP_ = 16
L = 8
NC = S_LAT // L
TAPS = L + 1
SEG = 4
NJ = NC // SEG
ROW = 2 * SEG * 2 * G
GW = G * SP_
SSM_N = 64

Q0, KV0, GA0, U0, GS0 = 0, 512, 768, 1280, 1792

BW = 256
BLK = KT * BW
SLOTS = 5
ADA = (0, 4, 1, 5, 2, 6, 3, 7)
STREAM = ([("ada", 0), ("ada", 4), ("u", 0), ("u", 1)] + [("ada", b) for b in ADA[2:]]
          + [("kv", 0), ("q", 0), ("q", 1), ("ga", 0), ("ga", 1), ("gs", 0), ("gs", 1)]
          + [("ada", 8), ("ada", 9), ("ada", 10), ("ada", 11)]
          + [("T", 0), ("T", 1), ("glu", 0)]
          + [("out", b) for b in range(4)])
SLOT = dict(zip(STREAM, (0, 1, 2, 3, 4, 0, 1, 4, 0, 1, 4, 0, 1, 2, 3, 4, 0, 1, 2, 3, 4, 0, 1, 2, 3, 4, 0, 1)))
BEFORE = {}
for _n, _key in enumerate(STREAM):
    for _old in STREAM[:_n]:
        if SLOT[_old] == SLOT[_key]:
            BEFORE[_key] = _old


def last_reader(key):
    kind, b = key
    if kind == "ada":
        return ("ada", ADA.index(b)) if b < 8 else ("gate", b - 8)
    return {"u": ("u", 3), "kv": ("kv", 3), "q": ("q", b), "ga": ("ga", 2 * b + 1),
            "gs": ("gs", 2 * b + 1), "T": ("y", 1), "glu": ("glu", 3)}[kind]


SPLIT = (("q", 0), ("q", 1), ("ga", 0), ("ga", 1), ("gs", 0), ("gs", 1))

USES = {}
RESULTS = {}


def _results():
    USES.clear()
    RESULTS.clear()

    def put(key, bank):
        USES[bank] = USES.get(bank, 0) + 1
        RESULTS[key] = (bank, USES[bank])

    for b in range(8):
        put(("ada", b), 0)
        put(("mT", b), 1)
    for k in range(KT):
        put(("xT", k), 5 + k % 2)
    for n in range(4):
        put(("u", n), (2, 3, 4, 7)[n])
    for n in range(8):
        put(("phi", n, 0), 5)
        put(("phi", n, 1), 6)
    for n in range(8):
        put(("UT", n), (0, 1, 4, 7)[n % 4])
    for n in range(3):
        put(("kv", n), 2 + n % 2)
    for n in range(8):
        put(("S", n), (4, 7)[n % 2])
    put(("M", 0), 4)
    put(("M", 1), 7)
    put(("M0", 0), 2)
    put(("kv", 3), 3)
    for n in range(2):
        put(("q", n), 5 + n)
    for n in range(4):
        put(("ga", n), (0, 1, 4, 7)[n])
    for n in range(4):
        put(("gs", n), (0, 1, 4, 7)[n])
    for n in range(4):
        put(("gate", n), n % 2)
    put(("kT", 0), 3)
    put(("qT", 0), 2)
    put(("qT", 1), 7)
    for n in range(2 * NH):
        put(("sc", n), 4 + n % 3)
        put(("pt", n), 2 + n % 2)
    for n in range(NH // 2):
        put(("o", n), 7)
    for kind, count in (("gb", 2), ("y", 2), ("yT", 2)):
        for n in range(count):
            put((kind, n), n % 2)
    for n in range(4):
        put(("glu", n), (0, 1, 6, 7)[n])
    for n in range(4):
        put(("out", n), (4, 5, 2, 3)[n])


_results()

BESIDE = [[("gate", 0), ("gate", 1)], [("gate", 2)],
          [("gate", 3)], [], [], [], [], [("gb", 0)], [("gb", 1)], [("y", 0)], [("y", 1)], []]

TWO_PI = 6.283185307179586
PI32 = 3.1415925
INV_2PI = 1.0 / TWO_PI
ROUND = 12582912.0
C1 = 6.28125
C2 = 0.0019350051879882812
C3 = TWO_PI - C1 - C2
MISC = 2
FIRST = {"cc": 2 * KT, "bias": 2 * KT, "pre": KT, "lam": 3 * G}
TABLES = {"quad": P, "id16": SP_, "d": 8, "bglu": 4, "rope": 4 * HD}


def bcast(ap, at, n):
    dims = [list(d) for d in ap.ap]
    dims.insert(at, [0, n])
    return bass.AP(ap.tensor, ap.offset, dims)


def columns(ap, widths):
    views, at = {}, 0
    for name, width in widths.items():
        views[name] = ap[:, at:at + width]
        at += width
    return views


def hymba_layer(nc, x, first_in, ctx_in, w_ada, b_ada_g, post, w_in, qk_norm, bc_in, w_glu, w_out,
                ident_in, tables_in, out):
    kernel_scratch = nc.dram_tensor("toeplitz_rows", [G, SP_, (2 * L - 1) * SP_], F32, kind="Internal")
    rows = kernel_scratch.ap()

    with ExitStack() as stack:
        def sb(name, *shape):
            return stack.enter_context(nc.sbuf_tensor(name, [P, *shape], F32))

        def sem(name):
            return stack.enter_context(nc.semaphore(name))

        def overlay(first, *rest):
            with nc.sbuf_tensor(first[0], [P, first[1]], first[2]) as under:
                pass
            return [under] + [stack.enter_context(nc.sbuf_tensor(name, [P, width], kind)) for name, width, kind in rest]

        ps = stack.enter_context(nc.psum_tensor("ps", [P, 8, 512], F32))

        ring, *ring_low = overlay(("ring", SLOTS * BLK, F32), *((f"ring_low{n}", BLK, F32R) for n in range(SLOTS)))
        ring = ring[:, :].rearrange("p (s n) -> p s n", s=SLOTS)
        hT_mem, *hT_high = overlay(("hT_mem", KT * TOK, F32), ("w_high1", BLK, F32R), ("w_high2", BLK, F32R))
        psi, *out_high, _ = overlay(
            ("psi", 2 * G * TAPS * SP_, F32), *((f"out_high{b}", BLK, F32R) for b in range(4)), ("psi_rest", 1024, F32))
        psi = psi[:, :].rearrange("p (r g t q) -> p r g t q", r=2, g=G, t=TAPS)
        phi_mem, w_high0, _, h_high, h_low = overlay(
            ("phi_mem", G * 2 * P, F32), ("w_high0", BLK, F32R), ("phi_rest", BLK, F32), ("h_high", BLK, F32R), ("h_low", BLK, F32R))
        scan_mem, _, attn_low = overlay(
            ("scan_mem", NC * 2 * 2 * G, F32), ("scan_rest", 3072, F32), ("attn_low", 4 * S_LAT, F32R))
        U = sb("U", G, 2 * NC)
        early, ssm_low, _ = overlay(("early", 4096, F32), ("ssm_low", 4 * S_LAT, F32R), ("early_rest", 3072, F32))
        qT_mem = sb("qT_mem", NH * S_LAT)
        kT = sb("kT", TOK)
        V = sb("V", KEYT, NKV * HD)
        bc_mem = sb("bc_mem", 4, GW)
        bh = sb("bh", 2, GW + SP_)
        pw = sb("pw", TAPS, 2, G)
        e_psi = sb("e_psi", L, 2, G)
        pool_mem = sb("pool_mem", 8 * (L * SP_ + SP_))
        small = sb("small", 24, G)
        ident = sb("ident", P)
        gains = sb("gains", 2, HD)
        kc_raw = sb("kc_raw", 2, NKV * HD)
        silu_c = sb("silu_c", KT, 32)
        ssq = sb("ssq", 40)
        rstd = sb("rstd", 40)
        mhalf = sb("mhalf", 32)
        red = sb("red", 8, 2, 2)
        mshift = sb("mshift", KT, 2)
        mgain = sb("mgain", KT, 2)
        nmax = sb("nmax", 2 * NH)
        rsum = sb("rsum", 2 * NH)
        rinv = sb("rinv", 2 * NH)

        first = sb("first", sum(FIRST.values()))
        ccb, bias_ada, pre, lam = columns(first, FIRST).values()
        ccb = ccb.rearrange("p (v k) -> p v k", v=2)
        lam = lam.rearrange("p (i g) -> p i g", i=3)
        tables = sb("tables", sum(TABLES.values()))
        quad, id16, dcol, bglu, ropes = columns(tables, TABLES).values()
        ropes = ropes.rearrange("p (t r d) -> p t r d", t=2, r=2)

        hT = hT_mem[:, :].rearrange("p (k t) -> p k t", k=KT)
        phi = phi_mem[:, :].rearrange("p (g r n) -> p g r n", g=G, r=2)
        S = scan_mem[:, :].rearrange("p (j b s r g) -> p j b s r g", j=NJ, b=2, s=SEG, r=2)
        phiT = scan_mem[:, 0:2048].rearrange("p (b g r t q) -> p b g r t q", b=2, g=4, r=2, t=L)
        vt = scan_mem[:, 2048:4096].rearrange("p (i n) -> p i n", i=4)
        xc = early[:, :].rearrange("p (i d) -> p i d", i=4)
        u_sb = early[:, 0:2048].rearrange("p (g t q) -> p g t q", g=G, t=4)
        neg_c = bc_mem[:, 0:2, :]
        b_blk = early[:, 2048:4096].rearrange("p (r g n) -> p r g n", r=2, g=G)
        raw = early[:, 0:1280].rearrange("p (t n) -> p t n", t=2)
        rot_a = early[:, 1280:1920]
        prob = early[:, 0:2048].rearrange("p (i n) -> p i n", i=4)
        ga = early[:, 2048:3072].rearrange("p (i t) -> p i t", i=4)
        gs = early[:, 3072:4096].rearrange("p (i t) -> p i t", i=4)
        m_ada = V[:, :, :].rearrange("p a b -> p (a b)")[:, 0:512].rearrange("p (b n) -> p b n", b=2)
        w8 = pw
        qT = qT_mem[:, :].rearrange("p (h t) -> p h t", h=NH)
        h_high, h_low = (h[:, :].rearrange("p (k t) -> p k t", k=KT) for h in (h_high, h_low))
        w_high = [w[:, :] for w in (w_high0, *hT_high)]
        xr = qT_mem[:, :].rearrange("p (t n) -> p t n", t=2)
        merged_high = w_high0[:, :].rearrange("p (k t) -> p k t", k=KT)
        merged_low = [m[:, :].rearrange("p (k t) -> p k t", k=4) for m in (attn_low, ssm_low)]
        hprev = phi_mem[:, 2048:4096].rearrange("p (c r g) -> p c r g", c=NC, r=2)
        PT = phi_mem[:, 4096:8192].rearrange("p (b h k t) -> p b h k t", b=2, h=2, k=KEYT)
        pool_t = pool_mem[:, 0:1024].rearrange("p (i n) -> p i n", i=2)
        m_rows = pool_mem[:, :].rearrange("p (g n) -> p g n", g=8)
        gate_m = bc_mem[:, 0:2, :].rearrange("p a b -> p (a b)")
        rot_b = bh[:, :, :].rearrange("p r n -> p (r n)")[:, 0:640]
        post_b = bc_mem[:, 2:4, :].rearrange("p a b -> p (a b)")
        y_sb = hT_mem[:, 0:1024].rearrange("p (t g q) -> p t g q", g=8, t=L)
        yT = hT_mem[:, 1024:2048].rearrange("p (j t c) -> p j t c", j=4, t=L)
        gpost = hT_mem[:, 2048:3072]
        sig = hT_mem[:, 3072:4096].rearrange("p (i t c) -> p i t c", i=4, t=L)
        e_phi = kT[:, :].rearrange("p (t r g) -> p t r g", t=L, r=2)
        prod = bc_mem[:, 0:2, :].rearrange("p c (a g) -> p (c a) g", g=G)
        qsum = kT[:, :].rearrange("p (a g) -> p a g", g=G)
        brow = hT_mem[:, 1024:2048]
        o_sb = scan_mem[:, 0:2048].rearrange("p (i d) -> p i d", i=2)
        a4 = sb("a4", 4, G)
        a64 = sb("a64", 4, G)
        carry = small[:, 0:4 * SEG - 4, :].rearrange("p (m r) g -> p m r g", r=2)
        skip = sb("skip", 8, SP_)
        sq_junk = sb("sq_junk", HD)
        newton = sb("newton", 24)
        sq_out = early[:, 1024:1536]

        slot_loaded = [sem(f"slot_loaded{s}") for s in range(SLOTS)]
        bank_filled = [sem(f"bank_filled{b}") for b in range(8)]
        bank_drained = [sem(f"bank_drained{b}") for b in range(8)]
        first_loaded = sem("first_loaded")
        ident_loaded = sem("ident_loaded")
        xc_loaded = [sem(f"xc_loaded{i}") for i in range(4)]
        bc_loaded = sem("bc_loaded")
        misc_loaded = sem("misc_loaded")
        post_loaded = sem("post_loaded")
        x_loaded = sem("x_loaded")
        h_high_ready = sem("h_high_ready")
        h_low_ready = sem("h_low_ready")
        w_high_ready = sem("w_high_ready")
        w_low_ready = sem("w_low_ready")
        out_high_ready = sem("out_high_ready")
        out_low_pool = sem("out_low_pool")
        out_low_dve = sem("out_low_dve")
        attn_high_ready = sem("attn_high_ready")
        attn_low_ready = sem("attn_low_ready")
        gpost_ready = sem("gpost_ready")
        brow_loaded = sem("brow_loaded")
        silu_zeroed = sem("silu_zeroed")
        silu_ready = sem("silu_ready")
        dt_ready = sem("dt_ready")
        damp_ready = sem("damp_ready")
        mag_ready = sem("mag_ready")
        angle_ready = sem("angle_ready")
        trig_ready = sem("trig_ready")
        ssx_ready = sem("ssx_ready")
        rstdx_ready = sem("rstdx_ready")
        xn_ready = sem("xn_ready")
        h_ready = sem("h_ready")
        phiT_ready = sem("phiT_ready")
        epsi_ready = sem("epsi_ready")
        bh_ready = sem("bh_ready")
        pool_consts = sem("pool_consts")
        psi_ready = sem("psi_ready")
        bblk_ready = sem("bblk_ready")
        skip_ready = sem("skip_ready")
        rows_written = sem("rows_written")
        ssqk_ready = sem("ssqk_ready")
        meansq_ready = sem("meansq_ready")
        rms_ready = sem("rms_ready")
        w8_ready = sem("w8_ready")
        scan_step = sem("scan_step")
        carry_step = sem("carry_step")
        hprev_ready = sem("hprev_ready")
        qT_zeroed = sem("qT_zeroed")
        rot_ready = sem("rot_ready")
        max_ready = sem("max_ready")
        prob_ready = sem("prob_ready")
        merged_ssm = sem("merged_ssm")
        sig_ready = sem("sig_ready")
        sso_ready = sem("sso_ready")
        sso_sum = sem("sso_sum")
        rstdo_ready = sem("rstdo_ready")
        o_ready = sem("o_ready")
        out_written = sem("out_written")
        dve_step = sem("dve_step")
        act_step = sem("act_step")
        pool_step = sem("pool_step")

        def filled(eng, key):
            bank, use = RESULTS[key]
            eng.wait_ge(bank_filled[bank], use)
            return bank

        def drained(eng, key):
            bank, use = RESULTS[key]
            eng.wait_ge(bank_drained[bank], use)

        def block_of(key):
            return ring[:, SLOT[key], :]

        def loaded(eng, key):
            eng.wait_ge(slot_loaded[SLOT[key]], LOADS[key])

        LOADS = {}
        per_slot = [0] * SLOTS
        for key in STREAM:
            per_slot[SLOT[key]] += 16 * (L if key[0] == "T" else 1)
            LOADS[key] = per_slot[SLOT[key]]

        def copy_qT(eng, t, chain):
            eng.wait_ge(qT_zeroed, 1)
            bank = filled(eng, ("qT", t))
            for half in range(2):
                r = slice(64 * half, 64 * half + 64)
                dst, src = qT[r, 4 * half:4 * half + 4, t * P:(t + 1) * P], ps[r, bank, :].rearrange("p (h t) -> p h t", h=4)
                ins = eng.activation(dst, src, ACT.Copy) if t == 0 else eng.tensor_copy(dst, src)
                if half == 0:
                    chain(ins)
                else:
                    ins.then_inc(bank_drained[bank], 1)

        block = stack.enter_context(nc.Block())

        @block.sync
        def _(sp):
            def cols(w, c0):
                return w.rearrange("(k p) n -> p k n", p=P)[:, :, c0:c0 + BW]

            sources = {"ada": (w_ada, 0), "u": (w_in, U0), "kv": (w_in, KV0), "q": (w_in, Q0),
                       "ga": (w_in, GA0), "gs": (w_in, GS0), "out": (w_out, 0)}
            sp.dma_start(first[:, :], first_in).then_inc(first_loaded, 16)
            sp.dma_start(ident[:, :], ident_in).then_inc(ident_loaded, 16)
            for i in range(4):
                src = (ctx_in, x)[i // 2]
                sp.dma_start(xc[:, i, :], src[(i % 2) * P:(i % 2 + 1) * P, :]).then_inc(xc_loaded[i], 16)
            for key in STREAM:
                kind, b = key
                if key == ("kv", 0):
                    sp.dma_start(tables[:, :], tables_in).then_inc(misc_loaded, 16)
                    sp.dma_start(gains[:, :, :], bass.AP(qk_norm.tensor, qk_norm.offset, [[0, P], [HD, 2], [1, HD]]))\
                        .then_inc(misc_loaded, 16)
                if key == ("u", 1):
                    sp.dma_start(bc_mem[:, :, :], bc_in).then_inc(bc_loaded, 16)
                if key in BEFORE:
                    filled(sp, last_reader(BEFORE[key]))
                if key == ("out", 2):
                    filled(sp, ("sc", 2 * NH - 1))
                    sp.dma_start(xr[:, :, :], x.rearrange("(t p) n -> p t n", p=P)).then_inc(x_loaded, 16)
                dst = block_of(key)
                done = slot_loaded[SLOT[key]]
                if kind in sources:
                    w, c0 = sources[kind]
                    sp.dma_start(dst.rearrange("p (k n) -> p k n", k=KT), cols(w, c0 + b * BW)).then_inc(done, 16)
                elif kind == "glu":
                    sp.dma_start(dst.rearrange("p (k n) -> p k n", k=4),
                                 w_glu.rearrange("(k p) n -> p k n", p=P)).then_inc(done, 16)
                else:
                    if b == 0:
                        for key in (("M", 0), ("M", 1), ("M0", 0)):
                            drained(sp, key)
                        for j in range(4):
                            for p0, c0, c1, r0 in ((0, 0, SP_, L - 1), (0, SP_, L * SP_, L), (SP_, 2 * SP_, TAPS * SP_, 0)):
                                lags = rows.rearrange("g q n -> q g n")[:, j * 8:j * 8 + 8, r0 * SP_:r0 * SP_ + c1 - c0]
                                sp.dma_start(lags, m_rows[32 * j + p0:32 * j + p0 + SP_, :, c0:c1]).then_inc(rows_written, 16)
                        sp.wait_ge(rows_written, 16 * 12)
                    for t in range(L):
                        src = rows.rearrange("g q n -> q g n")[:, b * 16:b * 16 + 16, (L - 1 - t) * SP_:(2 * L - 1 - t) * SP_]
                        sp.dma_start(dst.rearrange("p (g n) -> p g n", g=16)[t * SP_:(t + 1) * SP_],
                                     src).then_inc(done, 16)
            for t in range(2):
                for h in range(2):
                    sp.wait_ge(o_ready, 2 * t + h + 1)
                    c = slice(512 * h, 512 * h + 512)
                    sp.dma_start(out[t * P:(t + 1) * P, c], o_sb[:, t, c]).then_inc(out_written, 16)
            sp.wait_ge(out_written, 64)

        @block.gpsimd
        def _(pool):
            steps = [0]

            def step(ins):
                steps[0] += 1
                ins.then_inc(pool_step, 1)
                return steps[0]

            pool.memset(silu_c[:, :, :], 0.0).then_inc(silu_zeroed, 1)
            pool.memset(mhalf[:, :], -0.5).then_inc(pool_consts, 1)
            pool.memset(bh[:, :, GW:GW + SP_], 0.0).then_inc(pool_consts, 1)
            pool.memset(pw[:, 0, 0, :], 1.0).then_inc(pool_consts, 1)
            pool.memset(pw[:, 0, 1, :], 0.0).then_inc(pool_consts, 1)

            pool.memset(qT[:, :, :], 0.0).then_inc(qT_zeroed, 1)

            def rsqrt(n0, n1, ready, count):
                s = step(pool.tensor_scalar(rstd[:, n0:n1], ssq[:, n0:n1], 1.0 / count, EPS, ALU.mult, ALU.add))
                pool.wait_ge(pool_step, s)
                pool.tensor_tensor(rstd[:, n0:n1], rstd[:, n0:n1], mhalf[:, 0:n1 - n0], ALU.pow).then_inc(ready, 1)

            pool.wait_ge(pool_consts, 4)
            for half in range(2):
                pool.wait_ge(ssx_ready, 2 * half + 2)
                rsqrt(2 * half, 2 * half + 2, rstdx_ready, D)

            pool.wait_ge(bc_loaded, 16)
            pool.wait_ge(epsi_ready, 2)
            pool.wait_ge(bh_ready, 1)
            s = step(pool.tensor_scalar(neg_c[:, :, :], bc_mem[:, 2:4, :], -1.0, 0.0, ALU.mult, ALU.add))
            pool.wait_ge(pool_step, s)

            def cmat(ap, g0):
                return bcast(ap[:, g0 * SP_:(g0 + 4) * SP_].rearrange("p (g q) -> p g q", g=4), 2, L)

            def power(r, g0):
                return bcast(e_psi[:, :, r, g0:g0 + 4].rearrange("p t g -> p g t"), 3, SP_)

            def spread_b():
                filled(pool, ("xT", KT - 1))
                s = step(pool.memset(b_blk[:, :, :, :], 0.0))
                pool.wait_ge(pool_step, s)
                for r in range(2):
                    for d in range(2):
                        pool.tensor_copy(b_blk[d * 64:(d + 1) * 64, r, :, d * SP_:(d + 1) * SP_],
                                         bh[d * 64:(d + 1) * 64, r, 0:GW].rearrange("p (g q) -> p g q", g=G))\
                            .then_inc(bblk_ready, 1)
                        pool.wait_ge(bblk_ready, 2 * r + d + 1)

            added = [0, 0]
            for g0 in range(0, G, 4):
                if g0 == 12:
                    spread_b()
                out_ = [psi[:, r, g0:g0 + 4, 1:TAPS, :] for r in range(2)]
                tmp = [pool_t[:, r, :].rearrange("p (g t q) -> p g t q", g=4, t=L) for r in range(2)]
                made = []
                for r, (c_a, c_b) in enumerate(((bc_mem[:, 2, :], neg_c[:, 1, :]), (neg_c[:, 1, :], neg_c[:, 0, :]))):
                    step(pool.tensor_tensor(out_[r], power(0, g0), cmat(c_a, g0), ALU.mult))
                    if added[r]:
                        pool.wait_ge(pool_step, added[r])
                    made.append(step(pool.tensor_tensor(tmp[r], power(1, g0), cmat(c_b, g0), ALU.mult)))
                for r in range(2):
                    pool.wait_ge(pool_step, made[r])
                    added[r] = step(pool.tensor_tensor(out_[r], out_[r], tmp[r], ALU.add))
            step(pool.tensor_copy(psi[:, 0, :, 0, :], bc_mem[:, 2, :].rearrange("p (g q) -> p g q", g=G)))
            pool.wait_ge(pool_step, steps[0])
            pool.tensor_copy(psi[:, 1, :, 0, :], neg_c[:, 1, :].rearrange("p (g q) -> p g q", g=G)).then_inc(psi_ready, 1)
            pool.wait_ge(psi_ready, 1)
            pool.dma_start(post_b, bass.AP(post.tensor, post.offset, [[0, P], [1, D]])).then_inc(post_loaded, 16)
            pool.wait_ge(misc_loaded, 16 * MISC)
            pool.tensor_tensor(skip[:, :, :], bcast(dcol[:, :], 2, SP_), bcast(id16[:, :], 1, 8), ALU.mult)\
                .then_inc(skip_ready, 1)

            pool.wait_ge(h_high_ready, 1)
            pool.tensor_tensor(h_low, hT[:, :, S_CTX:TOK], h_high.bitcast(F32), ALU.subtract).then_inc(h_low_ready, 1)
            for n, key in enumerate(SPLIT):
                pool.wait_ge(w_high_ready, n + 1)
                pool.tensor_tensor(ring_low[SLOT[key]][:, :], block_of(key), w_high[n % 3].bitcast(F32), ALU.subtract)\
                    .then_inc(w_low_ready, 1)
            pool.wait_ge(carry_step, 3 * (2 * SEG - 2))
            hr, hi = (bcast(carry[:, SEG - 2:, x_, :], 1, NJ) for x_ in range(2))
            wr, wi = (bcast(w8[:, 0:NJ, x_, :], 2, SEG) for x_ in range(2))
            t1, t2 = S[:, :, 0, :, 0, :], S[:, :, 0, :, 1, :]
            hp = hprev.rearrange("p (s j) r g -> p j s r g", s=SEG)
            for r, (a, b) in enumerate(((hr, hi), (hi, hr))):
                if r == 1:
                    filled(pool, ("gs", 1))
                    pool.dma_start(brow, bass.AP(b_ada_g.tensor, b_ada_g.offset, [[0, P], [1, D]])).then_inc(brow_loaded, 16)
                step(pool.tensor_tensor(t1, wr, a, ALU.mult))
                made = step(pool.tensor_tensor(t2, wi, b, ALU.mult))
                pool.wait_ge(pool_step, made)
                made = step(pool.tensor_tensor(t1, t1, t2, ALU.subtract if r == 0 else ALU.add))
                pool.wait_ge(pool_step, made)
                for d, (j_first, j_rest, order) in enumerate(((0, slice(1, NJ), slice(None)),
                                                              (NJ - 1, slice(NJ - 2, None, -1), slice(None, None, -1)))):
                    h = slice(64 * d, 64 * d + 64)
                    pool.tensor_copy(hp[h, j_first, order, r, :], t1[h, 0]).then_inc(hprev_ready, 1)
                    pool.tensor_tensor(hp[h, j_rest, order, r, :], t1[h, 1:NJ], S[h, 0:NJ - 1, 1, :, r, :], ALU.add)\
                        .then_inc(hprev_ready, 1)
                    pool.wait_ge(hprev_ready, 4 * r + 2 * d + 2)
            for b in (0, 2):
                pool.wait_ge(out_high_ready, b + 1)
                key = ("out", b)
                pool.tensor_tensor(ring_low[SLOT[key]][:, :], block_of(key), out_high[b][:, :].bitcast(F32), ALU.subtract)\
                    .then_inc(out_low_pool, 1)
            for t in range(2):
                pool.wait_ge(sso_sum, t + 1)
                rsqrt(36 + t, 37 + t, rstdo_ready, D)

        @block.scalar
        def _(act):
            act.wait_ge(first_loaded, 16)
            act.wait_ge(silu_zeroed, 1)
            act.activation(silu_c[:, :, 0:2].rearrange("p k v -> p v k"), ccb[:, :, :], ACT.Silu).then_inc(silu_ready, 1)
            act.activation(small[:, 3, :], lam[:, 2, :], ACT.Exp).then_inc(dt_ready, 1)
            act.wait_ge(damp_ready, 1)
            act.activation(small[:, 6, :], small[:, 4, :], ACT.Exp).then_inc(mag_ready, 1)
            act.wait_ge(angle_ready, 2)
            act.activation(small[:, 10:12, :], small[:, 8:10, :], ACT.Sin).then_inc(trig_ready, 1)
            for i in range(4):
                act.wait_ge(xc_loaded[i], 16)
                if i:
                    act.wait_ge(ssx_ready, i)
                act.activation(phi_mem[:, 0:1024], xc[:, i, :], ACT.Square, accum_out=ssq[:, i:i + 1]).then_inc(ssx_ready, 1)

            def copy_xT(k):
                bank = filled(act, ("xT", k))
                act.activation(hT[:, k, :], ps[:, bank, :], ACT.Copy).then_inc(bank_drained[bank], 1)

            def copy_ada(b):
                bank = filled(act, ("ada", b))
                if b >= 2:
                    filled(act, ("mT", b - 2))
                act.activation(m_ada[:, b % 2, :], ps[:, bank, 0:BW], ACT.Copy).then_inc(bank_drained[bank], 1)

            def copy_phi(n):
                for h in range(2):
                    bank = filled(act, ("phi", n, h))
                    act.activation(phi[:, 4 * n + 2 * h:4 * n + 2 * h + 2, :, :].rearrange("p g r n -> p (g r n)"),
                                   ps[:, bank, :], ACT.Copy).then_inc(bank_drained[bank], 1)

            act.wait_ge(ssx_ready, 4)
            copy_ada(0)
            copy_xT(0)
            copy_ada(1)
            for k in range(1, 8):
                copy_xT(k)
            for b in range(2, 8):
                copy_ada(b)
                if b % 2 == 1:
                    copy_phi(b // 2 - 1)
            for t in range(4):
                bank = filled(act, ("u", t))
                act.activation(u_sb[:, :, t, :], ps[:, bank, :].rearrange("p (g q) -> p g q", g=G), ACT.Copy)\
                    .then_inc(bank_drained[bank], 1)
            copy_phi(3)
            for n in range(8):
                bank = filled(act, ("UT", n))
                v = ps[0:64, bank, :].rearrange("p (g c t) -> p t g c", g=4, t=2)
                act.activation(U[0:64, 4 * n:4 * n + 4, :], v[:, 0], ACT.Copy)
                act.activation(U[64:128, 4 * n:4 * n + 4, :], v[:, 1], ACT.Copy).then_inc(bank_drained[bank], 1)
            copy_phi(4)
            def copy_lags():
                for h in range(2):
                    bank = filled(act, ("M", h))
                    act.activation(m_rows[:, 4 * h:4 * h + 4, SP_:TAPS * SP_],
                                   ps[:, bank, :].rearrange("p (g n) -> p g n", g=4), ACT.Copy).then_inc(bank_drained[bank], 1)

            def copy_sums():
                act.wait_ge(w8_ready, 1)
                for n in range(8):
                    bank = filled(act, ("S", n))
                    r, g0 = n // 4, (n % 4) * 8
                    act.activation(S[:, :, :, :, r, g0:g0 + 8].rearrange("p j b s g -> p g (b s) j"),
                                   ps[:, bank, :].rearrange("p (g s j) -> p g s j", g=8, j=NJ), ACT.Copy)\
                        .then_inc(bank_drained[bank], 1)

            chain = [0]

            def act_chain(ins):
                chain[0] += 1
                ins.then_inc(act_step, 1)
                act.wait_ge(act_step, chain[0])

            def split(n):
                loaded(act, SPLIT[n])
                for key in ((("S", 6), ("S", 7)), (("kv", 3),), (("kv", 3),), (("q", 1),), (("q", 1),), (("ga", 1),))[n]:
                    filled(act, key)
                if n in (1, 2):
                    act.wait_ge(h_low_ready, 1)
                act.activation(w_high[n % 3], block_of(SPLIT[n]), ACT.Copy).then_inc(w_high_ready, 1)

            for n in range(4):
                if n == 3:
                    copy_sums()
                    act.wait_ge(h_ready, 16)
                    filled(act, ("S", 6))
                    filled(act, ("S", 7))
                    act.activation(h_high, hT[:, :, S_CTX:TOK], ACT.Copy).then_inc(h_high_ready, 1)
                    split(0)
                    copy_lags()
                bank = filled(act, ("kv", n))
                dst = kc_raw[:, n, :] if n < 2 else raw[:, n - 2, 512:640]
                act_chain(act.activation(dst, ps[:, bank, 0:P], ACT.Copy))
                act.activation(V[:, n, :], ps[:, bank, P:2 * P], ACT.Copy).then_inc(bank_drained[bank], 1)
                if n < 3:
                    copy_phi(5 + n)
            split(1)
            for n in range(4):
                for h in range(NKV):
                    src = kc_raw[:, n, h * HD:(h + 1) * HD] if n < 2 else raw[:, n - 2, 512 + h * HD:512 + (h + 1) * HD]
                    at = 24 + 2 * n + h if n < 2 else 12 + 10 * (n - 2) + h
                    ins = act.activation(sq_junk[:, :], src, ACT.Square, accum_out=ssq[:, at:at + 1])
                    if (n, h) == (3, 1):
                        ins.then_inc(ssqk_ready, 1)
                    else:
                        act_chain(ins)
            split(2)
            for t in range(2):
                bank = filled(act, ("q", t))
                act.activation(raw[:, t, 0:512], ps[:, bank, :], ACT.Copy).then_inc(bank_drained[bank], 1)
            split(3)
            split(4)
            for gate, kind in ((ga, "ga"), (gs, "gs")):
                for n in range(4):
                    bank = filled(act, (kind, n))
                    act.activation(gate[:, n, :], ps[:, bank, 0:S_LAT], ACT.Silu).then_inc(bank_drained[bank], 1)
                    if kind == "ga" and n == 1:
                        split(5)
                        act.wait_ge(meansq_ready, 1)
                        act.activation(rstd[:, 4:28], ssq[:, 4:28], ACT.Sqrt).then_inc(rms_ready, 1)
            act.wait_ge(pool_consts, 4)
            act.activation(sq_junk[:, 0:1], mhalf[:, 0:1], ACT.Exp)

            def copy_gates(s):
                for kind, n in BESIDE[s]:
                    if kind == "gate":
                        bank = filled(act, ("gate", n))
                        if n == 0:
                            act.wait_ge(carry_step, 3 * (2 * SEG - 2))
                        act.activation(gate_m[:, n * BW:(n + 1) * BW], ps[:, bank, 0:BW], ACT.Copy)\
                            .then_inc(bank_drained[bank], 1)

            copy_gates(0)
            bank = filled(act, ("kT", 0))
            act.activation(kT[:, :], ps[:, bank, :], ACT.Copy).then_inc(bank_drained[bank], 1)
            copy_qT(act, 0, act_chain)

            copy_gates(1)

            def copy_pt(n):
                bank = filled(act, ("pt", n))
                h, t = n // 2, n % 2
                if h >= 4:
                    act.wait_ge(bank_filled[7], RESULTS[("o", h // 2 - 2)][1])
                act.activation(PT[:, (h // 2) % 2, h % 2, :, t * P:(t + 1) * P],
                               ps[:, bank, :].rearrange("p (k t) -> p k t", k=KEYT), ACT.Copy).then_inc(bank_drained[bank], 1)

            for s in range(NH + 1):
                if s < NH:
                    for t in range(2):
                        n = 2 * s + t
                        bank = filled(act, ("sc", n))
                        act.wait_ge(max_ready, n + 1)
                        if n == 0:
                            filled(act, ("qT", 1))
                        if n >= 4:
                            filled(act, ("pt", n - 4))
                        act.activation(prob[:, n % 4, :], ps[:, bank, :], ACT.Exp, bias=nmax[:, n:n + 1],
                                       accum_out=rsum[:, n:n + 1]).then_inc(bank_drained[bank], 1)
                copy_gates(s + 2)
                if s >= 1:
                    copy_pt(2 * s - 2)
                    copy_pt(2 * s - 1)
            for h in range(2):
                bank = filled(act, ("y", h))
                act.activation(y_sb[:, :, 4 * h:4 * h + 4, :].rearrange("p t g q -> p g t q"), ps[:, bank, :].rearrange("p (g t q) -> p g t q", g=4, t=L),
                               ACT.Gelu_apprx_tanh).then_inc(bank_drained[bank], 1)
            act.wait_ge(out_high_ready, 1)
            loaded(act, ("out", 1))
            act.activation(out_high[1][:, :], block_of(("out", 1)), ACT.Copy).then_inc(out_high_ready, 1)
            for n in range(4):
                bank = filled(act, ("glu", n))
                act.activation(sig[:, n], ps[:, bank, 0:S_LAT].rearrange("p (t c) -> p t c", t=L), ACT.Sigmoid,
                               bias=bglu[:, n:n + 1]).then_inc(sig_ready, 1)
            for n in range(4):
                bank = filled(act, ("out", n))
                if n:
                    act.wait_ge(sso_ready, n)
                act.activation(sq_out[:, :], ps[:, bank, :], ACT.Square, accum_out=ssq[:, 28 + n:29 + n]).then_inc(sso_ready, 1)

        @block.vector
        def _(dve):
            steps = [0]

            def step(ins):
                steps[0] += 1
                ins.then_inc(dve_step, 1)
                return steps[0]

            def settle(s=None):
                dve.wait_ge(dve_step, steps[0] if s is None else s)

            tt = dve.tensor_tensor
            ts = dve.tensor_scalar
            stt = dve.scalar_tensor_tensor

            def cmul(o_re, o_im, a_re, a_im, b_re_, b_im_, t, last=None):
                step(tt(t[0], a_re, b_re_, ALU.mult))
                s1 = step(tt(t[1], a_im, b_im_, ALU.mult))
                step(tt(t[2], a_re, b_im_, ALU.mult))
                s2 = step(tt(t[3], a_im, b_re_, ALU.mult))
                settle(s1)
                step(tt(o_re, t[0], t[1], ALU.subtract))
                settle(s2)
                ins = tt(o_im, t[2], t[3], ALU.add)
                if last is None:
                    step(ins)
                else:
                    ins.then_inc(last, 1)

            sm = lambda i: small[:, i, :]
            lr, li, dt = lam[:, 0, :], lam[:, 1, :], sm(3)
            dve.wait_ge(first_loaded, 16)
            dve.wait_ge(dt_ready, 1)
            tt(sm(4), dt, lr, ALU.mult).then_inc(damp_ready, 1)
            step(tt(sm(5), dt, li, ALU.mult))
            settle()
            step(ts(sm(7), sm(5), INV_2PI, ROUND, ALU.mult, ALU.add))
            settle()
            step(ts(sm(7), sm(7), ROUND, None, ALU.subtract))
            settle()
            for c in (C1, C2, C3):
                step(stt(sm(5), sm(7), -c, sm(5), ALU.mult, ALU.add))
                settle()
            ts(sm(8), sm(5), PI32, -PI32, ALU.min, ALU.max).then_inc(angle_ready, 1)
            dve.wait_ge(angle_ready, 1)
            step(stt(sm(7), sm(8), -1.0, sm(8), ALU.mult, ALU.max))
            settle()
            ts(sm(9), sm(7), -1.0, TWO_PI / 4, ALU.mult, ALU.add).then_inc(angle_ready, 1)
            step(tt(sm(12), lr, lr, ALU.mult))
            step(tt(sm(13), li, li, ALU.mult))
            settle()
            step(tt(sm(12), sm(12), sm(13), ALU.add))
            settle()
            step(dve.reciprocal(sm(14), sm(12)))
            dve.wait_ge(trig_ready, 1)
            dve.wait_ge(mag_ready, 1)
            step(tt(pw[:, 1, 0, :], sm(6), sm(11), ALU.mult))
            step(tt(pw[:, 1, 1, :], sm(6), sm(10), ALU.mult))
            settle()
            step(ts(sm(15), pw[:, 1, 0, :], -1.0, None, ALU.add))
            settle()
            nr, ni = sm(15), pw[:, 1, 1, :]
            step(tt(sm(16), nr, lr, ALU.mult))
            step(tt(sm(17), ni, li, ALU.mult))
            step(tt(sm(18), ni, lr, ALU.mult))
            step(tt(sm(19), nr, li, ALU.mult))
            settle()
            step(tt(sm(16), sm(16), sm(17), ALU.add))
            step(tt(sm(18), sm(18), sm(19), ALU.subtract))
            settle()
            step(tt(sm(20), sm(16), sm(14), ALU.mult))
            step(tt(sm(21), sm(18), sm(14), ALU.mult))
            settle()
            for i in range(4):
                dve.wait_ge(rstdx_ready, i // 2 + 1)
                ts(xc[:, i, :], xc[:, i, :], rstd[:, i:i + 1], None, ALU.mult).then_inc(xn_ready, 1)

            dve.wait_ge(pool_consts, 4)

            def double(tab, n):
                m = min(n, tab.shape[1] - 1 - n)
                t4 = [vt[:, i, 0:m * G].rearrange("p (e g) -> p e g", g=G) for i in range(4)]
                cmul(tab[:, n + 1:n + 1 + m, 0, :], tab[:, n + 1:n + 1 + m, 1, :], tab[:, 1:1 + m, 0, :], tab[:, 1:1 + m, 1, :],
                     bcast(tab[:, n, 0, :], 1, m), bcast(tab[:, n, 1, :], 1, m), t4)
                settle()

            for n in (1, 2, 4):
                double(pw, n)
            dve.tensor_copy(e_psi[0:64], pw[0:64, 1:9]).then_inc(epsi_ready, 1)
            dve.tensor_copy(e_psi[64:128], pw[64:128, 8:0:-1]).then_inc(epsi_ready, 1)
            step(dve.tensor_copy(e_phi[0:64], pw[0:64, 7::-1]))
            step(dve.tensor_copy(e_phi[64:128], pw[64:128, 0:8]))
            settle()

            def gq(ap):
                return ap.rearrange("p (g q) -> p g q", g=G)

            def phi_batch(n):
                g0 = 4 * n
                er = bcast(e_phi[:, :, 0, g0:g0 + 4].rearrange("p t g -> p g t"), 3, SP_)
                ei = bcast(e_phi[:, :, 1, g0:g0 + 4].rearrange("p t g -> p g t"), 3, SP_)
                br = bcast(gq(bh[:, 0, 0:GW])[:, g0:g0 + 4, :], 2, L)
                bi = bcast(gq(bh[:, 1, 0:GW])[:, g0:g0 + 4, :], 2, L)
                o = phiT[:, n % 2]
                t = [vt[:, i, :].rearrange("p (g t q) -> p g t q", g=4, t=L) for i in range(4)]
                settle()
                if n >= 2:
                    filled(dve, ("phi", n - 2, 1))
                step(tt(t[0], er, br, ALU.mult))
                s1 = step(tt(t[1], ei, bi, ALU.mult))
                step(tt(t[2], er, bi, ALU.mult))
                s2 = step(tt(t[3], ei, br, ALU.mult))
                settle(s1)
                tt(o[:, :, 0], t[0], t[1], ALU.subtract).then_inc(phiT_ready, 1)
                settle(s2)
                tt(o[:, :, 1], t[2], t[3], ALU.add).then_inc(phiT_ready, 1)
                dve.wait_ge(phiT_ready, 2 * n + 2)

            def ada_reduce(n):
                b = ADA[n]
                bank = filled(dve, ("mT", n))
                dve.tensor_reduce(red[:, b, :, :], ps[:, bank, 0:2 * P].rearrange("p (f j v) -> p f v j", f=2, j=4)[:, :, 0:2, :],
                                  AX_X, ALU.add).then_inc(bank_drained[bank], 1)

            def modulate(pair):
                bank, use = RESULTS[("mT", 2 * pair + 1)]
                dve.wait_ge(bank_drained[bank], use)
                f = slice(2 * pair, 2 * pair + 2)
                step(tt(mshift[:, f, :], red[:, pair, :, :], bcast(bias_ada[:, f], 2, 2), ALU.add))
                step(tt(mgain[:, f, :], red[:, 4 + pair, :, :],
                        bcast(bias_ada[:, 8 + 2 * pair:10 + 2 * pair], 2, 2), ALU.add))
                settle()
                step(stt(mgain[:, f, :], mgain[:, f, :], 1.0, bcast(pre[:, f], 2, 2), ALU.add, ALU.mult))
                settle()
                for k in (2 * pair, 2 * pair + 1):
                    drained(dve, ("xT", k))
                    for v, c0 in ((1, 0), (0, S_CTX)):
                        o = hT[:, k, c0:c0 + 256]
                        ts(o, o, mgain[:, k, v:v + 1], mshift[:, k, v:v + 1], ALU.mult, ALU.add).then_inc(h_ready, 1)

            def discretise_b():
                tmp = [vt[:, i, :].rearrange("p (g q) -> p g q", g=G) for i in range(4)]
                dve.wait_ge(bc_loaded, 16)
                cmul(gq(bh[:, 0, 0:GW]), gq(bh[:, 1, 0:GW]), bcast(sm(20), 2, SP_), bcast(sm(21), 2, SP_),
                     gq(bc_mem[:, 0, :]), gq(bc_mem[:, 1, :]), tmp, last=bh_ready)
                dve.wait_ge(bh_ready, 1)

            for pair in range(4):
                ada_reduce(2 * pair)
                ada_reduce(2 * pair + 1)
                modulate(pair)
                if pair == 0:
                    discretise_b()
                if pair < 3:
                    phi_batch(pair)
            for n in range(3, 8):
                phi_batch(n)

            step(dve.tensor_copy(w8[:, 1, :, :], pw[:, 8, :, :]))
            settle()
            def as_matrix(m, re, im):
                step(dve.tensor_copy(m[:, 0, :], re))
                step(dve.tensor_copy(m[:, 2, :], im))
                step(ts(m[:, 1, :], im, -1.0, None, ALU.mult))
                settle()

            as_matrix(a4, w8[:, 1, 0, :], w8[:, 1, 1, :])
            step(dve.tensor_copy(a4[:, 3, :], w8[:, 1, 0, :]))
            for n in (1, 2, 4):
                double(w8, n)
            as_matrix(a64, w8[:, NJ, 0, :], w8[:, NJ, 1, :])
            dve.tensor_copy(a64[:, 3, :], w8[:, NJ, 0, :]).then_inc(w8_ready, 1)
            dve.wait_ge(w8_ready, 1)

            for n in range(8):
                drained(dve, ("S", n))
            dve.wait_ge(psi_ready, 1)
            nb = 2 * SEG

            def chunk(mat, b, prev, here, out_, signal, done):
                p_, q_ = prod[:, 0:4 * b, :], qsum[:, 0:2 * b, :]
                matv = bcast(mat[:, :, :].rearrange("p (o k) g -> p o (k g)", o=2), 1, b)
                pk = p_.rearrange("p (b k) g -> p k b g", k=2)
                tt(p_.rearrange("p (b o k) g -> p b o (k g)", b=b, o=2), matv,
                   bcast(prev.rearrange("p (b n) -> p b n", b=b), 2, 2), ALU.mult).then_inc(signal, 1)
                dve.wait_ge(signal, done + 1)
                tt(q_, pk[:, 0], pk[:, 1], ALU.add).then_inc(signal, 1)
                dve.wait_ge(signal, done + 2)
                tt(out_, here, q_.rearrange("p b g -> p (b g)"), ALU.add).then_inc(signal, 1)

            chunk(a4, nb, scan_mem[:, 0:ROW], scan_mem[:, ROW:2 * ROW], scan_mem[:, ROW:2 * ROW], scan_step, 0)
            with dve.Fori(1, NJ - 1) as j:
                dve.wait_ge(scan_step, j * 3)
                here = scan_mem[:, bass.ds(j * ROW + ROW, ROW)]
                chunk(a4, nb, scan_mem[:, bass.ds(j * ROW, ROW)], here, here, scan_step, j * 3)
            dve.wait_ge(scan_step, 3 * (NJ - 1))
            flat = lambda ap: ap.rearrange("p r g -> p (r g)")
            before = flat(S[:, NJ - 1, 0, 0])
            for m in range(2 * SEG - 2):
                b, sg = (m + 1) // SEG, (m + 1) % SEG
                if m:
                    dve.wait_ge(carry_step, 3 * m)
                chunk(a64, 1, before, flat(S[:, NJ - 1, b, sg]), flat(carry[:, m]), carry_step, 3 * m)
                before = flat(carry[:, m])
            dve.wait_ge(carry_step, 3 * (2 * SEG - 2))
            bank = filled(dve, ("M0", 0))
            dve.wait_ge(skip_ready, 1)
            tt(m_rows[:, :, 0:SP_], ps[:, bank, 0:8 * SP_].rearrange("p (g n) -> p g n", g=8), skip[:, :, :], ALU.add)\
                .then_inc(bank_drained[bank], 1)

            for t in range(2):
                drained(dve, ("q", t))
                sq = rot_a if t == 0 else rot_b
                step(tt(sq[:, 0:512], raw[:, t, 0:512], raw[:, t, 0:512], ALU.mult))
                settle()
                dve.tensor_reduce(ssq[:, 4 + 10 * t:12 + 10 * t], sq[:, 0:512].rearrange("p (h d) -> p h d", h=8), AX_X, ALU.add)\
                    .then_inc(ssqk_ready, 1)
            dve.wait_ge(ssqk_ready, 3)
            ts(ssq[:, 4:28], ssq[:, 4:28], 1.0 / HD, EPS, ALU.mult, ALU.add).then_inc(meansq_ready, 1)

            dve.wait_ge(misc_loaded, 16 * MISC)
            step(ts(gains[:, 0, :], gains[:, 0, :], float(HD) ** -0.5, None, ALU.mult))
            settle()
            dve.wait_ge(rms_ready, 1)
            y, v, t_ = rstd[:, 4:28], ssq[:, 4:28], newton[:, :]
            step(dve.reciprocal(y, y))
            settle()
            step(tt(t_, y, y, ALU.mult))
            settle()
            step(tt(t_, t_, v, ALU.mult))
            settle()
            step(ts(t_, t_, -0.5, 1.5, ALU.mult, ALU.add))
            settle()
            step(tt(y, y, t_, ALU.mult))
            settle()
            for t in range(2):
                k3 = kc_raw[:, t, :].rearrange("p (h d) -> p h d", h=NKV)
                step(tt(k3, k3, bcast(rstd[:, 24 + 2 * t:26 + 2 * t], 2, HD), ALU.mult))
                settle()
                tt(k3, k3, bcast(gains[:, 1, :], 1, NKV), ALU.mult).then_inc(rot_ready, 1)
            for t in range(2):
                h3 = raw[:, t, :].rearrange("p (h d) -> p h d", h=10)
                a3 = rot_a.rearrange("p (h d) -> p h d", h=10)
                step(tt(h3, h3, bcast(rstd[:, 4 + 10 * t:14 + 10 * t], 2, HD), ALU.mult))
                settle()
                step(tt(h3[:, 0:8], h3[:, 0:8], bcast(gains[:, 0, :], 1, 8), ALU.mult))
                step(tt(h3[:, 8:10], h3[:, 8:10], bcast(gains[:, 1, :], 1, 2), ALU.mult))
                settle()
                step(tt(a3, h3, bcast(ropes[:, t, 0, :], 1, 10), ALU.mult))
                h5 = raw[:, t, :].rearrange("p (h s d) -> p s h d", s=2, d=16)
                b5 = rot_b[:, :].rearrange("p (h s d) -> p s h d", s=2, d=16)
                for s_ in range(2):
                    for half in range(2):
                        sin = ropes[:, t, 1, half * 32 + s_ * 16:half * 32 + s_ * 16 + 16]
                        step(tt(b5[:, s_, half::2], h5[:, 1 - s_, half::2], bcast(sin, 1, 10), ALU.mult))
                settle()
                tt(raw[:, t, 0:512].rearrange("p (i half d) -> p half i d", half=2, d=HD),
                   rot_a[:, 0:512].rearrange("p (half i d) -> p half i d", half=2, d=HD),
                   rot_b[:, 0:512].rearrange("p (half i d) -> p half i d", half=2, d=HD), ALU.add).then_inc(rot_ready, 1)
                tt(raw[:, t, 512:640], rot_a[:, 512:640], rot_b[:, 512:640], ALU.add).then_inc(rot_ready, 1)
                dve.wait_ge(rot_ready, 4 + 2 * t)

            copy_qT(dve, 1, lambda ins: (step(ins), settle()))

            def norm(n):
                bank, use = RESULTS[("sc", n)]
                dve.wait_ge(bank_drained[bank], use)
                step(dve.reciprocal(rinv[:, n:n + 1], rsum[:, n:n + 1]))
                settle()
                ts(prob[:, n % 4, :], prob[:, n % 4, :], rinv[:, n:n + 1], None, ALU.mult).then_inc(prob_ready, 1)

            def merge_attn(i):
                bank = filled(dve, ("o", i))
                if i == 0:
                    for n in range(4):
                        drained(dve, ("ga", n))
                tt(merged_high[:, i, :], ps[:, bank, 0:S_LAT], ga[:, i, :], ALU.mult).then_inc(attn_high_ready, 1)
                tt(ga[:, i, :], ps[:, bank, 0:S_LAT], ga[:, i, :], ALU.mult).then_inc(bank_drained[bank], 1)
                if i == 1:
                    dve.wait_ge(hprev_ready, 8)
                drained(dve, ("o", i))
                dve.wait_ge(attn_high_ready, i + 1)
                for n in {0: (), 1: (0, 1)}.get(i, (i,)):
                    tt(merged_low[0][:, n, :], ga[:, n, :], merged_high[:, n, :].bitcast(F32), ALU.subtract)\
                        .then_inc(attn_low_ready, 1)

            def out_block_high(b):
                loaded(dve, ("out", b))
                filled(dve, ("y", 1))
                dve.tensor_copy(out_high[b][:, :], block_of(("out", b))).then_inc(out_high_ready, 1)

            def out_block_low(b):
                dve.wait_ge(out_high_ready, b + 1)
                key = ("out", b)
                tt(ring_low[SLOT[key]][:, :], block_of(key), out_high[b][:, :].bitcast(F32), ALU.subtract).then_inc(out_low_dve, 1)

            for s in range(NH + 2):
                if s < NH:
                    for t in range(2):
                        n = 2 * s + t
                        bank = filled(dve, ("sc", n))
                        dve.tensor_reduce(nmax[:, n:n + 1], ps[:, bank, :], AX_X, ALU.max, negate=True).then_inc(max_ready, 1)
                    norm(2 * s)
                    norm(2 * s + 1)
                for kind, h in BESIDE[s + 2]:
                    if kind == "gb":
                        dve.wait_ge(brow_loaded, 16)
                        dve.wait_ge(post_loaded, 16)
                        bank = filled(dve, ("gb", h))
                        c = slice(512 * h, 512 * h + 512)
                        tt(gpost[:, c], ps[:, bank, :], brow[:, c], ALU.add).then_inc(bank_drained[bank], 1)
                        drained(dve, ("gb", h))
                        tt(gpost[:, c], gpost[:, c], post_b[:, c], ALU.mult).then_inc(gpost_ready, 1)
                if s == NH:
                    out_block_high(0)
                if s >= 3 and s % 2 == 1:
                    merge_attn((s - 3) // 2)
            for h in range(2):
                bank = filled(dve, ("yT", h))
                dve.tensor_copy(yT[:, :, 4 * h:4 * h + 4, :].rearrange("p j t c -> p t j c"),
                                ps[:, bank, :].rearrange("p (t j c) -> p t j c", t=4, j=4)).then_inc(bank_drained[bank], 1)
            out_block_low(1)
            dve.wait_ge(out_high_ready, 2)
            out_block_high(2)
            out_block_high(3)
            out_block_low(3)
            for n in range(4):
                drained(dve, ("gs", n))
            for h in range(2):
                drained(dve, ("yT", h))
            for n in range(4):
                dve.wait_ge(sig_ready, n + 1)
                step(tt(sig[:, n], sig[:, n], yT[:, n], ALU.mult))
                settle()
                high, low, gate = (a.rearrange("p (c t) -> p t c", t=L)
                                   for a in (merged_high[:, 4 + n, :], merged_low[1][:, n, :], gs[:, n, :]))
                step(tt(high, sig[:, n], gate, ALU.mult))
                step(tt(sig[:, n], sig[:, n], gate, ALU.mult))
                settle()
                tt(low, sig[:, n], high.bitcast(F32), ALU.subtract).then_inc(merged_ssm, 1)
            dve.wait_ge(gpost_ready, 2)
            dve.wait_ge(x_loaded, 16)
            for t in range(2):
                scaled = []
                for h in range(2):
                    dve.wait_ge(sso_ready, 2 * t + h + 1)
                    if h == 1:
                        tt(ssq[:, 36 + t:37 + t], ssq[:, 28 + 2 * t:29 + 2 * t], ssq[:, 29 + 2 * t:30 + 2 * t], ALU.add)\
                            .then_inc(sso_sum, 1)
                    bank, _ = RESULTS[("out", 2 * t + h)]
                    c = slice(512 * h, 512 * h + 512)
                    scaled.append(step(tt(o_sb[:, t, c], ps[:, bank, :], gpost[:, c], ALU.mult)))
                dve.wait_ge(rstdo_ready, t + 1)
                for h in range(2):
                    c = slice(512 * h, 512 * h + 512)
                    settle(scaled[h])
                    stt(o_sb[:, t, c], o_sb[:, t, c], rstd[:, 36 + t:37 + t], xr[:, t, c], ALU.mult, ALU.add).then_inc(o_ready, 1)

        @block.tensor
        def _(pe):
            mm = pe.matmul

            def free(key):
                bank, use = RESULTS[key]
                if use > 1:
                    pe.wait_ge(bank_drained[bank], use - 1)
                return bank

            def fill(ins, bank):
                ins.then_inc(bank_filled[bank], 1)

            def ada(n, key, b):
                bank = free(key)
                loaded(pe, ("ada", b))
                w = block_of(("ada", b)).rearrange("p (k n) -> p k n", k=KT)
                for k in range(KT):
                    j = k % 4
                    last = mm(ps[32 * j:32 * j + 32, bank, 0:BW], silu_c[:, k, :], w[:, k, :], start=k < 4, stop=k >= 4)
                fill(last, bank)

            def turn_ada(n):
                bank = free(("mT", n))
                drained(pe, ("ada", n))
                for f in range(2):
                    last = pe.transpose(ps[:, bank, f * P:(f + 1) * P], m_ada[:, n % 2, f * P:(f + 1) * P], ident[:, :])
                fill(last, bank)

            def turn_x(k):
                bank = free(("xT", k))
                for i in range(4):
                    if k == 0:
                        pe.wait_ge(xn_ready, i + 1)
                    last = pe.transpose(ps[:, bank, i * P:(i + 1) * P], xc[:, i, k * P:(k + 1) * P], ident[:, :])
                fill(last, bank)

            pe.wait_ge(ident_loaded, 16)
            pe.wait_ge(silu_ready, 1)

            def turn_phi(n):
                pe.wait_ge(phiT_ready, 2 * n + 2)
                for h in range(2):
                    bank = free(("phi", n, h))
                    for i in range(4):
                        g, r = 2 * h + i // 2, i % 2
                        last = pe.transpose(ps[:, bank, i * P:(i + 1) * P],
                                            phiT[:, n % 2, g, r].rearrange("p t q -> p (t q)"), ident[:, :])
                    fill(last, bank)

            def project_u(pair, b):
                loaded(pe, ("u", b))
                w = block_of(("u", b)).rearrange("p (k n) -> p k n", k=KT)
                for k in (2 * pair, 2 * pair + 1):
                    if b == 0:
                        pe.wait_ge(h_ready, 2 * k + 2)
                    for t in range(4):
                        bank = free(("u", t)) if k == 0 and b == 0 else RESULTS[("u", t)][0]
                        last = mm(ps[:, bank, b * BW:(b + 1) * BW], hT[:, k, t::4], w[:, k, :],
                                  start=k == 0 and b == 0, stop=k == KT - 1 and b == 1)
                        if k == KT - 1 and b == 1:
                            fill(last, bank)

            def ada_block(n):
                ada(n, ("ada", n), ADA[n])

            ada_block(0)
            turn_x(0)
            ada_block(1)
            turn_ada(0)
            turn_x(1)
            turn_x(2)
            turn_ada(1)
            for k in range(3, 7):
                turn_x(k)
            project_u(0, 0)
            turn_x(7)
            project_u(0, 1)
            ada_block(2)
            turn_phi(0)
            turn_ada(2)
            ada_block(3)
            turn_ada(3)
            ada_block(4)
            project_u(1, 0)
            ada_block(5)
            turn_ada(4)
            turn_ada(5)
            project_u(1, 1)
            turn_phi(1)
            ada_block(6)
            project_u(2, 0)
            ada_block(7)
            turn_ada(6)
            turn_ada(7)
            project_u(2, 1)
            turn_phi(2)
            project_u(3, 0)
            project_u(3, 1)
            turn_phi(3)
            for n in range(4):
                drained(pe, ("u", n))
            for n in range(8):
                bank = free(("UT", n))
                for i in range(4):
                    g = 4 * n + i
                    last = pe.transpose(ps[0:64, bank, i * P:(i + 1) * P], u_sb[:, g].rearrange("p t q -> p (t q)"), ident[:, :])
                fill(last, bank)
            turn_phi(4)
            def project(key, wkey, c0, off=0, done=True):
                bank, use = RESULTS[key]
                if off == 0:
                    free(key)
                loaded(pe, wkey)
                w = block_of(wkey).rearrange("p (k n) -> p k n", k=KT)
                for k in range(KT):
                    last = mm(ps[:, bank, off:off + BW], hT[:, k, c0:c0 + P], w[:, k, :], start=k == 0, stop=k == KT - 1)
                if done:
                    fill(last, bank)

            for n in range(3):
                project(("kv", n), ("kv", 0), n * P)
                turn_phi(5 + n)
            for n in range(8):
                bank = free(("S", n))
                r, g0 = n // 4, (n % 4) * 8
                for i in range(8):
                    g = g0 + i
                    drained(pe, ("UT", g // 4))
                    drained(pe, ("phi", g // 4, g // 2 % 2))
                    ug = U[:, g, :].rearrange("p (b j) -> p b j", b=2)
                    for d in range(2):
                        last = mm(ps[64 * d:64 * d + 64, bank, i * 64:(i + 1) * 64].rearrange("p (b j) -> p b j", b=2),
                                  phi[:, g, r, 64 * d:64 * d + 64], ug if d == 0 else ug[:, :, ::-1], start=True, stop=True)
                fill(last, bank)

            pe.wait_ge(bblk_ready, 4)
            pe.wait_ge(psi_ready, 1)
            for h in range(2):
                bank = free(("M", h))
                for i in range(4):
                    for r in range(2):
                        for j in range(4):
                            g = 8 * j + 4 * h + i
                            last = mm(ps[32 * j:32 * j + 32, bank, i * P:(i + 1) * P], b_blk[:, r, g, :],
                                      psi[:, r, g, 1:TAPS, :], start=r == 0, stop=r == 1)
                fill(last, bank)
            bank = free(("M0", 0))
            for i in range(8):
                for r in range(2):
                    for j in range(4):
                        g = 8 * j + i
                        last = mm(ps[32 * j:32 * j + 32, bank, i * SP_:(i + 1) * SP_], bh[:, r, g * SP_:g * SP_ + 32],
                                  psi[:, r, g, 0, :], start=r == 0, stop=r == 1)
            fill(last, bank)

            project(("kv", 3), ("kv", 0), 3 * P)

            def parts(wkey):
                n = SPLIT.index(wkey)
                high = w_high[n % 3].rearrange("p (k n) -> p k n", k=KT)
                low = ring_low[SLOT[wkey]][:, :].rearrange("p (k n) -> p k n", k=KT)
                return n, ((h_high, high), (h_low, high), (h_high, low))

            def wait_part(n, part):
                pe.wait_ge((w_high_ready, h_low_ready, w_low_ready)[part], (n + 1, 1, n + 1)[part])

            for b in range(2):
                n, products = parts(("q", b))
                for t in range(2):
                    bank = free(("q", t)) if b == 0 else RESULTS[("q", t)][0]
                    for part, (h, w) in enumerate(products):
                        if t == 0:
                            wait_part(n, part)
                        for k in range(KT):
                            last = mm(ps[:, bank, b * BW:(b + 1) * BW], h[:, k, t * P:(t + 1) * P], w[:, k, :],
                                      start=part == 0 and k == 0, stop=part == 2 and k == KT - 1)
                    if b == 1:
                        fill(last, bank)
            for kind in ("ga", "gs"):
                for i in range(4):
                    n, products = parts((kind, i // 2))
                    bank = free((kind, i))
                    c0 = (i % 2) * P
                    for part, (h, w) in enumerate(products):
                        if i % 2 == 0:
                            wait_part(n, part)
                        for k in range(KT):
                            last = mm(ps[:, bank, 0:S_LAT], w[:, k, c0:c0 + P], h[:, k, :],
                                      start=part == 0 and k == 0, stop=part == 2 and k == KT - 1)
                    fill(last, bank)

            def gate_rows(h):
                bank = free(("gb", h))
                if h == 0:
                    for n in range(4):
                        drained(pe, ("gate", n))
                    pe.wait_ge(misc_loaded, 16 * MISC)
                c = slice(512 * h, 512 * h + 512)
                fill(mm(ps[:, bank, :], quad[:, :], gate_m[:, c], start=True, stop=True), bank)

            def ssm_out(h):
                bank = free(("y", h))
                if h == 0:
                    pe.wait_ge(hprev_ready, 8)
                    loaded(pe, ("T", 0))
                    loaded(pe, ("T", 1))
                for i in range(4):
                    for part in range(3):
                        for j in range(4):
                            g = 8 * j + 4 * h + i
                            if part < 2:
                                a, b = hprev[:, :, part, g], psi[:, part, g, 1:TAPS, :]
                            else:
                                T = block_of(("T", g // 16)).rearrange("p (g n) -> p g n", g=16)
                                a, b = U[:, g, NC:2 * NC], T[:, g % 16, :]
                            last = mm(ps[32 * j:32 * j + 32, bank, i * P:(i + 1) * P], a, b, start=part == 0, stop=part == 2)
                fill(last, bank)

            def beside(s):
                for kind, n in BESIDE[s]:
                    if kind == "gate":
                        ada(n, ("gate", n), 8 + n)
                    elif kind == "gb":
                        gate_rows(n)
                    else:
                        ssm_out(n)

            beside(0)
            bank = free(("kT", 0))
            pe.wait_ge(rot_ready, 2)
            for n in range(4):
                if n == 2:
                    pe.wait_ge(rot_ready, 6)
                src = kc_raw[:, n, :] if n < 2 else raw[:, n - 2, 512:640]
                last = pe.transpose(ps[:, bank, n * P:(n + 1) * P], src, ident[:, :])
            fill(last, bank)
            for t in range(2):
                bank = free(("qT", t))
                for i in range(4):
                    last = pe.transpose(ps[:, bank, i * P:(i + 1) * P], raw[:, t, i * P:(i + 1) * P], ident[:, :])
                fill(last, bank)

            beside(1)

            def scores(n):
                h, t = n // 2, n % 2
                bank = free(("sc", n))
                if n == 0:
                    drained(pe, ("kT", 0))
                    drained(pe, ("qT", 0))
                    drained(pe, ("qT", 1))
                fill(mm(ps[:, bank, :], qT[:, h, t * P:(t + 1) * P], kT[:, :], start=True, stop=True), bank)

            def turn_probs(n):
                bank = free(("pt", n))
                pe.wait_ge(prob_ready, n + 1)
                for k in range(KEYT):
                    last = pe.transpose(ps[:, bank, k * P:(k + 1) * P], prob[:, n % 4, k * P:(k + 1) * P], ident[:, :])
                fill(last, bank)

            def attend(i):
                bank = free(("o", i))
                for n in range(4 * i, 4 * i + 4):
                    drained(pe, ("pt", n))
                kv = i // 2
                for k in range(KEYT):
                    for e in range(2):
                        last = mm(ps[64 * e:64 * e + 64, bank, 0:S_LAT], V[:, k, kv * HD:(kv + 1) * HD], PT[:, i % 2, e, k, :],
                                  start=k == 0, stop=k == KEYT - 1)
                fill(last, bank)

            for s in range(NH + 2):
                if s < NH:
                    scores(2 * s)
                    scores(2 * s + 1)
                if s < NH:
                    beside(s + 2)
                if 1 <= s <= NH:
                    turn_probs(2 * s - 2)
                    turn_probs(2 * s - 1)
                if s == NH:
                    beside(s + 2)
                if s >= 3 and s % 2 == 1:
                    attend((s - 3) // 2)

            def project_out(b, t, half, parts_=range(3)):
                key = ("out", 2 * t + b // 2)
                bank = RESULTS[key][0]
                if b % 2 == 0 and half == 0 and 0 in parts_:
                    free(key)
                high, low = (a[:, :].rearrange("p (k n) -> p k n", k=KT) for a in (out_high[b], ring_low[SLOT[("out", b)]]))
                for part in parts_:
                    w = low if part == 2 else high
                    if half == 0 and t == 0:
                        if part == 0:
                            pe.wait_ge(out_high_ready, b + 1)
                        elif part == 1 and b == 0:
                            pe.wait_ge(attn_low_ready, 4)
                        elif part == 2:
                            pe.wait_ge((out_low_pool, out_low_dve)[b % 2], b // 2 + 1)
                    for k in range(4 * half, 4 * half + 4):
                        if b == 0 and t == 0 and half == 0 and part == 0:
                            pe.wait_ge(attn_high_ready, k + 1)
                        m = merged_low[half][:, k - 4 * half] if part == 1 else merged_high[:, k]
                        last = mm(ps[:, bank, (b % 2) * BW:(b % 2 + 1) * BW], m[:, t * P:(t + 1) * P], w[:, k, :],
                                  start=part == 0 and k == 0 and b % 2 == 0, stop=part == 2 and k == KT - 1 and b % 2 == 1)
                if b % 2 == 1 and half == 1:
                    fill(last, bank)

            drained(pe, ("y", 0))
            drained(pe, ("y", 1))
            for h in range(2):
                bank = free(("yT", h))
                for i in range(4):
                    last = pe.transpose(ps[:, bank, i * P:(i + 1) * P], y_sb[:, 4 * h + i].rearrange("p g q -> p (g q)"), ident[:, :])
                fill(last, bank)
            for b in range(2):
                for t in range(2):
                    project_out(b, t, 0, (0, 1))
            for t in range(2):
                project_out(0, t, 0, (2,))
            drained(pe, ("yT", 0))
            drained(pe, ("yT", 1))
            loaded(pe, ("glu", 0))
            w = block_of(("glu", 0)).rearrange("p (k n) -> p k n", k=4)
            for n in range(4):
                bank = free(("glu", n))
                for k in range(4):
                    last = mm(ps[:, bank, 0:S_LAT], w[:, k, n * P:(n + 1) * P], yT[:, k].rearrange("p t c -> p (t c)"),
                              start=k == 0, stop=k == 3)
                fill(last, bank)
            for t in range(2):
                project_out(1, t, 0, (2,))
            for b in (2, 3):
                for t in range(2):
                    project_out(b, t, 0)
            pe.wait_ge(merged_ssm, 4)
            for t in range(2):
                for b in range(4):
                    project_out(b, t, 1)


def kernel(x, c, ctx, c_ctx, w_ada, b_ada, pre_norm, post_norm, w_in, q_norm, k_norm,
           ssm_lam_re, ssm_lam_im, ssm_log_dt, ssm_b_re, ssm_b_im, ssm_c_re, ssm_c_im,
           ssm_d, w_glu, b_glu, w_out):
    import numpy as np
    import concourse.bacc as bacc
    from concourse.bass_utils import run_bass_kernel_spmd

    f = np.float32
    x, c, ctx, c_ctx, w_ada, b_ada, pre_norm, post_norm, w_in, q_norm, k_norm = (
        np.asarray(a) for a in (x, c, ctx, c_ctx, w_ada, b_ada, pre_norm, post_norm, w_in, q_norm, k_norm))
    w_glu, b_glu, w_out = (np.asarray(a) for a in (w_glu, b_glu, w_out))

    def states(a):
        a = np.asarray(a)[0]
        return np.moveaxis(a, 2, 1).reshape(P, -1)

    grid_w, freqs = 64, HD // 4
    inv = (f(10000.0) ** (-np.arange(freqs, dtype=f) / f(freqs))).astype(f)
    pos = np.arange(S_LAT)
    ang = np.stack([(pos // grid_w).astype(f)[:, None] * inv, (pos % grid_w).astype(f)[:, None] * inv], 1)
    cos, sin = np.cos(ang).astype(f), np.sin(ang).astype(f)
    rope = np.stack([np.stack([cos, cos], 2).reshape(S_LAT, HD), np.stack([-sin, sin], 2).reshape(S_LAT, HD)], 1)

    d = np.asarray(ssm_d)[0]
    d_t = np.zeros((4, 32, 8), f)
    d_t[:, 0:SP_, :] = np.swapaxes(d.reshape(4, 8, SP_), 1, 2)
    quad = np.zeros((P, P), f)
    quad[::32] = 1.0
    id16 = np.zeros((4, 32, SP_), f)
    id16[:, 0:SP_] = np.eye(SP_, dtype=f)

    lam = [states(ssm_lam_re), states(ssm_lam_im), np.repeat(np.asarray(ssm_log_dt)[0], SSM_N, axis=0)]
    first = {"cc": np.stack([c[0].reshape(KT, P).T, c_ctx.reshape(KT, P).T], 1).reshape(P, -1),
             "bias": b_ada[0, :2 * D].reshape(2 * KT, P).T, "pre": pre_norm[0].reshape(KT, P).T,
             "lam": np.stack(lam, 1).reshape(P, -1)}
    tables = {"quad": quad, "id16": id16.reshape(P, SP_), "d": d_t.reshape(P, 8), "bglu": b_glu[0].reshape(4, P).T,
              "rope": np.moveaxis(rope.reshape(2, P, 2, HD), 0, 1).reshape(P, -1)}
    bc = [states(ssm_b_re), states(ssm_b_im),
          states(np.swapaxes(np.asarray(ssm_c_re), 3, 4)), states(np.swapaxes(np.asarray(ssm_c_im), 3, 4))]
    arrays = {
        "x": x[0], "ctx_in": ctx[0], "first_in": np.concatenate([first[n] for n in FIRST], 1),
        "w_ada": w_ada[0], "b_ada_g": b_ada[:, 2 * D:], "post": post_norm[0], "w_in": w_in[0],
        "qk_norm": np.stack([q_norm[0], k_norm[0]]), "bc_in": np.stack(bc, 1),
        "w_glu": w_glu[0], "w_out": w_out[0],
        "ident_in": np.eye(P, dtype=f), "tables_in": np.concatenate([tables[n] for n in TABLES], 1),
    }
    nc = bacc.Bacc("TRN2", target_bir_lowering=False, num_devices=1)
    args = {}
    for name, a in arrays.items():
        arrays[name] = np.ascontiguousarray(a)
        args[name] = nc.dram_tensor(name, arrays[name].shape, F32, kind="ExternalInput").ap()
    args["out"] = nc.dram_tensor("out", (S_LAT, D), F32, kind="ExternalOutput").ap()
    hymba_layer(nc, **args)
    result = run_bass_kernel_spmd(nc, [arrays], core_ids=[0])
    return result.results[0]["out"].reshape(1, S_LAT, D)
```
